# Optimizing a Trainium2 kernel written in Bass

```python
import jax, jax.numpy as jnp
from jax import lax
import numpy as np

D_MODEL = 1024
BATCH = 1
SEQ = 256
DEPTH = 1
DEC_BATCH = 8
DEC_SEQ = 8
PAST_LEN = 2048
PAGE_SIZE = 128

N_META = 16
D_MIX = D_MODEL
C_A = D_MIX // 2
HEAD_A = 64
H_A = C_A // HEAD_A
C_B = D_MIX - C_A
CONV_W = 31
D_DECAY_LORA = 64
D_AAA_LORA = 64
D_GATE_LORA = 128
SHIFT_COLS = 3 * C_A + D_DECAY_LORA + D_AAA_LORA + D_GATE_LORA
IN_COLS = SHIFT_COLS + 2 * C_B
N_EXPERTS = 32
TOP_K = 4
D_FF = D_MODEL
SWIGLU_LIMIT = 7.0
SWIGLU_ALPHA = 1.702
MOE_BLOCK = 128
RMS_EPS = 1e-5
LN_EPS = 1e-5
GN_EPS = 64e-5

kernel_name = "rwkv7_conformer_conv_moe_hybrid_step"

def rms_norm(x, g):
    xf = x.astype(jnp.float32)
    return xf * lax.rsqrt(jnp.mean(xf * xf, axis=-1, keepdims=True) + RMS_EPS) * g.astype(jnp.float32)

def layer_norm(x, w, b):
    mu = jnp.mean(x, axis=-1, keepdims=True)
    var = jnp.mean(jnp.square(x - mu), axis=-1, keepdims=True)
    return (x - mu) * lax.rsqrt(var + LN_EPS) * w.astype(jnp.float32) + b.astype(jnp.float32)

def heads(a):
    return a.reshape(*a.shape[:-1], H_A, HEAD_A)

def wkv7_scan(s0, r, decay, k, v, kk, kka):
    def step(s, inp):
        r_t, w_t, k_t, v_t, kk_t, b_t = inp
        sa = jnp.einsum('bhvk,bhk->bhv', s, kk_t)
        s = s * w_t[:, :, None, :] - sa[..., None] * b_t[:, :, None, :] + v_t[..., None] * k_t[:, :, None, :]
        y = jnp.einsum('bhvk,bhk->bhv', s, r_t)
        return s, y
    xs = tuple(jnp.moveaxis(a, 1, 0) for a in (r, decay, k, v, kk, kka))
    s, ys = lax.scan(step, s0.astype(jnp.float32), xs)
    return jnp.moveaxis(ys, 0, 1), s

def rwkv7_mix(p_a, prev_row, wkv0, tshift_mu, decay_w0, decay_w2, iclr_a0, iclr_a2, gate_g2,
              k_k, k_a, r_k, lnx_w, lnx_b):
    p_prev = jnp.concatenate([prev_row[:, None, :].astype(p_a.dtype), p_a[:, :-1]], axis=1)
    xs = p_a + (p_prev - p_a) * tshift_mu
    r, k, v, w_lo, a_lo, g_lo = jnp.split(
        xs, [C_A, 2 * C_A, 3 * C_A, 3 * C_A + D_DECAY_LORA, 3 * C_A + D_DECAY_LORA + D_AAA_LORA], axis=-1)
    w = -jax.nn.softplus(-(decay_w0 + jnp.tanh(w_lo) @ decay_w2)) - 0.5
    decay = jnp.exp(-jnp.exp(w))
    a = jax.nn.sigmoid(iclr_a0 + a_lo @ iclr_a2)
    g = jax.nn.sigmoid(g_lo) @ gate_g2
    kk = heads(k * k_k)
    kk = kk / jnp.maximum(jnp.sqrt(jnp.sum(kk * kk, axis=-1, keepdims=True)), 1e-12)
    k = k * (1.0 + (a - 1.0) * k_a)
    rh, kh, vh, ah = heads(r), heads(k), heads(v), heads(a)
    y, s_new = wkv7_scan(wkv0, rh, heads(decay), kh, vh, kk, kk * ah)
    mu = jnp.mean(y, axis=-1, keepdims=True)
    var = jnp.mean(jnp.square(y - mu), axis=-1, keepdims=True)
    y = ((y - mu) * lax.rsqrt(var + GN_EPS)).reshape(*y.shape[:-2], C_A) * lnx_w + lnx_b
    bonus = jnp.sum(rh * kh * r_k, axis=-1, keepdims=True) * vh
    y = (y + bonus.reshape(*bonus.shape[:-2], C_A)) * g
    return y, s_new, p_a[:, -1]

def conv_mix(p_b, buf, glu_b, dw_weight, dw_bias, conv_ln_w, conv_ln_b):
    u = p_b + glu_b
    u = u[..., :C_B] * jax.nn.sigmoid(u[..., C_B:])
    ext = jnp.concatenate([buf.astype(u.dtype), u], axis=1)
    z = lax.conv_general_dilated(ext, dw_weight.astype(ext.dtype)[:, None, :], window_strides=(1,),
                                 padding='VALID', dimension_numbers=('NWC', 'WIO', 'NWC'),
                                 feature_group_count=C_B) + dw_bias
    z = layer_norm(z, conv_ln_w, conv_ln_b)
    z = z * jax.nn.sigmoid(z)
    return z, ext[:, -(CONV_W - 1):]

def moe_ffn(h, w_router, b_router, w_gate, b_gate, w_up, b_up, w_down, b_down):
    n = h.shape[0]
    logits = (h @ w_router + b_router).astype(jnp.float32)
    top_val, top_idx = lax.top_k(logits, TOP_K)
    gates = jax.nn.softmax(top_val, axis=-1)
    n_assign = n * TOP_K
    flat_e = top_idx.reshape(-1)
    order = jnp.argsort(flat_e)
    sorted_e = flat_e[order]
    counts = jnp.bincount(flat_e, length=N_EXPERTS)
    padded = (counts + MOE_BLOCK - 1) // MOE_BLOCK * MOE_BLOCK
    pad_end = jnp.cumsum(padded)
    pad_start = pad_end - padded
    start = jnp.cumsum(counts) - counts
    dest = pad_start[sorted_e] + jnp.arange(n_assign) - start[sorted_e]
    n_blocks = (n_assign + N_EXPERTS * (MOE_BLOCK - 1) + MOE_BLOCK - 1) // MOE_BLOCK
    tok = order // TOP_K
    row_token = jnp.full((n_blocks * MOE_BLOCK,), n, jnp.int32).at[dest].set(tok.astype(jnp.int32))
    block_expert = jnp.minimum(jnp.searchsorted(pad_end, jnp.arange(n_blocks) * MOE_BLOCK, side='right'),
                               N_EXPERTS - 1)
    h_pad = jnp.concatenate([h, jnp.zeros((1, h.shape[1]), h.dtype)], axis=0)
    xb = h_pad[row_token].reshape(n_blocks, MOE_BLOCK, h.shape[1])

    def expert_block(args):
        xe, e = args
        gt = jnp.minimum(xe @ w_gate[e] + b_gate[e], SWIGLU_LIMIT)
        up = jnp.clip(xe @ w_up[e] + b_up[e], -SWIGLU_LIMIT, SWIGLU_LIMIT)
        return ((up + 1.0) * gt * jax.nn.sigmoid(SWIGLU_ALPHA * gt)) @ w_down[e] + b_down[e]

    yb = lax.map(expert_block, (xb, block_expert)).reshape(n_blocks * MOE_BLOCK, -1)
    contrib = yb[dest] * gates.reshape(-1)[order][:, None]
    return jax.ops.segment_sum(contrib, tok, num_segments=n)

def layer(x, prev_row, wkv0, conv_buf, norm_mix, w_in, tshift_mu, decay_w0, decay_w2, iclr_a0, iclr_a2,
          gate_g2, k_k, k_a, r_k, lnx_w, lnx_b, glu_b, dw_weight, dw_bias, conv_ln_w, conv_ln_b, w_out,
          norm_ffn, w_router, b_router, w_gate, b_gate, w_up, b_up, w_down, b_down):
    h = rms_norm(x, norm_mix)
    p = h @ w_in
    y_a, wkv_new, row_new = rwkv7_mix(p[..., :SHIFT_COLS], prev_row, wkv0, tshift_mu, decay_w0, decay_w2,
                                      iclr_a0, iclr_a2, gate_g2, k_k, k_a, r_k, lnx_w, lnx_b)
    y_b, buf_new = conv_mix(p[..., SHIFT_COLS:], conv_buf, glu_b, dw_weight, dw_bias, conv_ln_w, conv_ln_b)
    x = x + jnp.concatenate([y_a, y_b], axis=-1) @ w_out
    h2 = rms_norm(x, norm_ffn)
    b, t, d = h2.shape
    x = x + moe_ffn(h2.reshape(b * t, d), w_router, b_router, w_gate, b_gate, w_up, b_up,
                    w_down, b_down).reshape(b, t, d)
    return x, wkv_new, row_new, buf_new

def setup_inputs(seed: int = 0) -> dict:
    key = jax.random.key(seed)
    ks = jax.random.split(key, 40)
    L = DEPTH

    def nrm(k, shape, s):
        return jax.random.normal(k, shape, jnp.float32) * s

    return {
        "x_prompt": nrm(ks[0], (BATCH, SEQ, D_MODEL), 1.0),
        "x_sample": nrm(ks[1], (DEC_BATCH, DEC_SEQ, D_MODEL), 1.0),
        "state_wkv": nrm(ks[2], (L, DEC_BATCH, H_A, HEAD_A, HEAD_A), 0.3),
        "state_shift": nrm(ks[3], (L, DEC_BATCH, SHIFT_COLS), 1.0),
        "state_conv": nrm(ks[4], (L, DEC_BATCH, CONV_W - 1, C_B), 0.5),
        "meta_tokens": nrm(ks[5], (N_META, D_MODEL), 1.0),
        "norm_mix": 1.0 + nrm(ks[6], (L, D_MODEL), 0.02),
        "w_in": nrm(ks[7], (L, D_MODEL, IN_COLS), D_MODEL ** -0.5),
        "tshift_mu": jax.random.uniform(ks[8], (L, SHIFT_COLS), jnp.float32),
        "decay_w0": jax.random.uniform(ks[9], (L, C_A), jnp.float32, minval=-5.0, maxval=0.0),
        "decay_w2": nrm(ks[10], (L, D_DECAY_LORA, C_A), 0.1),
        "iclr_a0": nrm(ks[11], (L, C_A), 0.1),
        "iclr_a2": nrm(ks[12], (L, D_AAA_LORA, C_A), D_AAA_LORA ** -0.5),
        "gate_g2": nrm(ks[13], (L, D_GATE_LORA, C_A), D_GATE_LORA ** -0.5),
        "k_k": 0.85 + nrm(ks[14], (L, C_A), 0.02),
        "k_a": 1.0 + nrm(ks[15], (L, C_A), 0.02),
        "r_k": nrm(ks[16], (L, H_A, HEAD_A), 0.1),
        "lnx_w": 1.0 + nrm(ks[17], (L, C_A), 0.02),
        "lnx_b": nrm(ks[18], (L, C_A), 0.01),
        "glu_b": nrm(ks[19], (L, 2 * C_B), 0.02),
        "dw_weight": nrm(ks[20], (L, CONV_W, C_B), CONV_W ** -0.5),
        "dw_bias": nrm(ks[21], (L, C_B), 0.02),
        "conv_ln_w": 1.0 + nrm(ks[22], (L, C_B), 0.02),
        "conv_ln_b": nrm(ks[23], (L, C_B), 0.01),
        "w_out": nrm(ks[24], (L, D_MIX, D_MODEL), D_MIX ** -0.5),
        "norm_ffn": 1.0 + nrm(ks[25], (L, D_MODEL), 0.02),
        "w_router": nrm(ks[26], (L, D_MODEL, N_EXPERTS), D_MODEL ** -0.5),
        "b_router": nrm(ks[27], (L, N_EXPERTS), 0.01),
        "w_gate": nrm(ks[28], (L, N_EXPERTS, D_MODEL, D_FF), D_MODEL ** -0.5),
        "b_gate": nrm(ks[29], (L, N_EXPERTS, D_FF), 0.02),
        "w_up": nrm(ks[30], (L, N_EXPERTS, D_MODEL, D_FF), D_MODEL ** -0.5),
        "b_up": nrm(ks[31], (L, N_EXPERTS, D_FF), 0.02),
        "w_down": nrm(ks[32], (L, N_EXPERTS, D_FF, D_MODEL), D_FF ** -0.5),
        "b_down": nrm(ks[33], (L, N_EXPERTS, D_MODEL), 0.02),
        "norm_final": 1.0 + nrm(ks[34], (D_MODEL,), 0.02),
    }

def reference(x_prompt, x_sample, state_wkv, state_shift, state_conv, meta_tokens, norm_mix, w_in,
              tshift_mu, decay_w0, decay_w2, iclr_a0, iclr_a2, gate_g2, k_k, k_a, r_k, lnx_w, lnx_b,
              glu_b, dw_weight, dw_bias, conv_ln_w, conv_ln_b, w_out, norm_ffn, w_router, b_router,
              w_gate, b_gate, w_up, b_up, w_down, b_down, norm_final):
    b_p = x_prompt.shape[0]
    meta = jnp.broadcast_to(meta_tokens.astype(x_prompt.dtype)[None], (b_p, N_META, D_MODEL))
    xp = jnp.concatenate([meta, x_prompt], axis=1)
    xs = x_sample
    zero_row = jnp.zeros((b_p, SHIFT_COLS), jnp.float32)
    zero_wkv = jnp.zeros((b_p, H_A, HEAD_A, HEAD_A), jnp.float32)
    zero_buf = jnp.zeros((b_p, CONV_W - 1, C_B), jnp.float32)
    wkv_p, shift_p, conv_p, wkv_s, shift_s, conv_s = [], [], [], [], [], []
    for l in range(DEPTH):
        lw = tuple(a[l] for a in (norm_mix, w_in, tshift_mu, decay_w0, decay_w2, iclr_a0, iclr_a2, gate_g2,
                                  k_k, k_a, r_k, lnx_w, lnx_b, glu_b, dw_weight, dw_bias, conv_ln_w,
                                  conv_ln_b, w_out, norm_ffn, w_router, b_router, w_gate, b_gate, w_up,
                                  b_up, w_down, b_down))
        xp, sw, sr, sc = layer(xp, zero_row, zero_wkv, zero_buf, *lw)
        wkv_p.append(sw); shift_p.append(sr); conv_p.append(sc)
        xs, sw, sr, sc = layer(xs, state_shift[l], state_wkv[l], state_conv[l], *lw)
        wkv_s.append(sw); shift_s.append(sr); conv_s.append(sc)
    y_prompt = rms_norm(xp, norm_final)[:, N_META:].astype(x_prompt.dtype)
    y_sample = rms_norm(xs, norm_final).astype(x_sample.dtype)
    return (y_prompt, y_sample, jnp.stack(wkv_p), jnp.stack(shift_p), jnp.stack(conv_p),
            jnp.stack(wkv_s), jnp.stack(shift_s), jnp.stack(conv_s))


_drawn_inputs = setup_inputs


def setup_inputs(seed=0):
    import zlib

    import numpy as np

    out = dict(_drawn_inputs(seed))
    spreads = {}
    factors = {'lnx_w': 3.252,
     'b_gate': 7.01,
     'b_up': 8.0,
     'b_down': 6.601,
     'norm_final': 8.09,
     'lnx_b': 3.953,
     'conv_ln_b': 3.904}
    for name, (base, spread) in spreads.items():
        noise = np.random.default_rng([zlib.crc32(name.encode()), seed]).standard_normal(out[name].shape)
        drawn = base * np.exp(spread * noise) if base else spread * noise
        out[name] = __import__('jax').numpy.asarray(drawn.astype(out[name].dtype))
    for name, factor in factors.items():
        out[name] = (out[name] * factor).astype(out[name].dtype)
    return out
```

```python
from contextlib import ExitStack

import concourse.bass as bass
from concourse import mybir

ALU = mybir.AluOpType
ACT = mybir.ActivationFunctionType
AX = mybir.AxisListType
F32 = mybir.dt.float32
BF16 = mybir.dt.bfloat16
I32 = mybir.dt.int32
U32 = mybir.dt.uint32

P = 128
DM = 1024
KC = DM // P
META, SEQ = 16, 256
NPR = META + SEQ
NSEQ, SL = 8, 8
NSA = NSEQ * SL
NT = NPR + NSA
TILES = [(0, 128), (128, 128), (256, NT - 256)]
CA, CB = 512, 512
NH, HD = 8, 64
NPAIR = NH // 2
NBA = 14
SHC = NBA * P
CW = 31
HIST = CW - 1
NE, TOPK = 32, 4
LIMIT, ALPHA = 7.0, 1.702
RMS_EPS, LN_EPS, GN_EPS = 1e-5, 1e-5, 64e-5
HALF_DECAY = 0.6065306597126334

UNIT = 2048
RING = 8
UNITS_IN = 11
UNITS_OUT = 4
UPRE = UNITS_IN + UNITS_OUT
UPAIR = 24
C = 64
NOVER = 20
NBLK = NE + NOVER + 2
PAIRS, OPAIRS = NE // 2, NOVER // 2
OUT_ORDER = [2, 3, 0, 1]
IN_ORDER = [7, 9, 8, 10, 6, 2, 3, 0, 1, 4, 5]
CHUNKS = [0, 64, 128, 192, 256, NPR]
LEVELS = [6, 6, 6, 6, 4, 3]
EXTP = HIST + NPR
EXTS = HIST + SL



def build(nc, a):
    ctx = ExitStack()
    with ctx:
        stage_sems = []

        def sem(name):
            return ctx.enter_context(nc.semaphore(name))

        def lsem(name):
            stage_sems.append(nc.alloc_semaphore(name))
            return stage_sems[-1]

        def next_stage():
            nc.clear_and_free_semaphores(list(stage_sems))
            stage_sems.clear()
            nc.all_engine_barrier()

        bank = ctx.enter_context(nc.psum_tensor("bank", [P, 8, 512], F32))
        ring = ctx.enter_context(nc.sbuf_tensor("ring", [P, RING, UNIT], F32))
        arena_words = 36800
        arena = ctx.enter_context(nc.sbuf_tensor("arena", [P, arena_words], F32))
        cursor = [0]

        def shaped(v, *shape):
            if len(shape) == 2:
                return v.rearrange("p (a b) -> p a b", b=shape[1])
            if len(shape) == 3:
                return v.rearrange("p (a b c) -> p a b c", b=shape[1], c=shape[2])
            return v

        def take(*shape, dt=F32):
            n = 1
            for d in shape:
                n *= d
            words = (n + 1) // 2 if dt == BF16 else n
            v = arena[:, cursor[0]:cursor[0] + words]
            cursor[0] += words
            assert cursor[0] <= arena_words, (cursor[0], arena_words)
            if dt != F32:
                v = v.bitcast(dt)
            return shaped(v, *shape)

        def b3(ap, n):
            return ap.unsqueeze(2).broadcast_to([ap.shape[0], ap.shape[1], n])

        def b2(ap, n):
            return ap.unsqueeze(1).broadcast_to([ap.shape[0], n, ap.shape[1]])

        ident = take(P)
        ones = take(P)
        headones = take(P)
        strict = take(2, C)
        incl = take(2, C)
        level0 = take(P)
        level = take(6, C)
        seqrow = take(NSEQ)
        row16 = take(2)
        rowf = take(1)
        tribf = take(P, dt=BF16)
        onesbf = take(P, dt=BF16)
        vecA = take(80)
        vecW = take(CW * 4)
        vecS = take(NSEQ * NBA)
        slot_iota = take(C)
        exp_iota = take(NE)
        biasT = take(3, KC, NE)
        gffn = take(KC)
        small = take(64)
        rankm = take(3, NE)
        gates = take(3, NE)
        blockbase = take(NBLK)
        blocktab = take(NBLK + 2, dt=I32)
        Zc = take(NPAIR, HD)
        ZBD = take(NPAIR, P)
        mixer_start = cursor[0]
        rT, kT, vT, ldT, kkT, bT, gT, bonT, yT, zT = [take(4, NT) for _ in range(10)]
        zsBD = take(NSEQ * NPAIR, P)
        mixer_end = cursor[0]

        V_NORM, V_MU, V_W0, V_A0, V_KK, V_KA, V_RK, V_GLU, V_DWB, V_CLW, V_CLB, V_LW, V_LB, V_OMKA = \
            0, 8, 22, 26, 30, 34, 38, 42, 50, 54, 58, 62, 66, 70
        NVEC = 70

        unit_landed = [sem(f"unit_landed{i}") for i in range(RING)]
        unit_used = sem("unit_used")
        out_stored = sem("out_stored")
        stores = [0]

        def slot(t, n):
            return ring[:, t % RING, :].rearrange("p (c n) -> p c n", n=n)

        def load_unit(sp, t):
            if t >= RING:
                sp.wait_ge(unit_used, t - RING + 1)
            if t < UNITS_IN:
                n = IN_ORDER[t]
                src = a["w_in"][0].rearrange("(c p) n -> p c n", p=P)[:, :, n * 256:(n + 1) * 256]
                sp.dma_start(slot(t, 256), src).then_inc(unit_landed[t % RING], 16)
            else:
                u = OUT_ORDER[t - UNITS_IN]
                src = a["w_out"][0].rearrange("(c p) n -> p c n", p=P)[:, 2 * u:2 * u + 2, :]
                sp.dma_start(slot(t, DM), src).then_inc(unit_landed[t % RING], 16)

        def wait_unit(eng, t):
            eng.wait_ge(unit_landed[t % RING], 16 * (t // RING + 1))

        def diag(ap, i):
            return ap[64 * i:64 * i + 64, :, 64 * i:64 * i + 64]

        def half(ap, i):
            return ap[64 * i:64 * i + 64]

        def chain(eng, s):
            n = [0]

            def link(ins):
                n[0] += 1
                ins.then_inc(s, 1)
                eng.wait_ge(s, n[0])
            return link

        cursor[0] = mixer_end
        xt = take(3, DM)
        hT = take(KC, NT)
        ext = take(4, EXTP + NSEQ * EXTS)
        edge = take(2, NPR + 1 + NSEQ * (SL + 1))
        diff = take(2, NT)
        uval = take(2, NT)
        usig = take(2, NT)
        uflat = take(4, NSA)
        tmpA = take(4, NT)
        lastc = take(NBA * (1 + NSEQ))
        loraw = take(2, CA)
        s0c = shaped(xt.rearrange("p a b -> p (a b)")[:, 2 * CB:2 * CB + NSEQ * NPAIR * HD], NSEQ * NPAIR, HD)
        vrow = shaped(tmpA.rearrange("p a b -> p (a b)")[:, 0:384], 3, P)
        cbuf = shaped(zT.rearrange("p a b -> p (a b)")[:, 0:1024], 2, CB)
        junk = shaped(gT.rearrange("p a b -> p (a b)")[:, 0:DM])
        yi = yT.rearrange("p a b -> p (a b)")
        icol, irow, ixor, itmp, rowm = [yi[:, P * i:P * i + P].bitcast(I32) for i in range(5)]
        geq = shaped(yi[:, 640:640 + 7 * C], 7, C)
        lor_in = bonT[:, 0:2, :]
        lor_tanh, lor_sig = bonT[0:64, 2, :], bonT[:, 3, :]
        lastT = shaped(usig.rearrange("p a b -> p (a b)")[:, 0:P])
        cpT = shaped(xt.rearrange("p a b -> p (a b)")[:, 0:CB])
        csT = shaped(xt.rearrange("p a b -> p (a b)")[:, CB:2 * CB])

        def ext_prompt(j, lo, n):
            return ext[:, j, lo:lo + n]

        def ext_sample(j, lo, n):
            return ext[:, j, EXTP:].rearrange("p (s t) -> p s t", t=EXTS)[:, :, lo:lo + n]

        def edge_prompt(b, lo, n):
            return edge[:, b, lo:lo + n]

        def edge_sample(b, lo, n):
            return edge[:, b, NPR + 1:].rearrange("p (s t) -> p s t", t=SL + 1)[:, :, lo:lo + n]

        def by_seq(ap):
            return ap[:, NPR:NT].rearrange("p (s t) -> p s t", t=SL)

        x_in = lsem("x_in")
        rows_in = lsem("rows_in")
        hist_in = lsem("hist_in")
        s0_in = lsem("s0_in")
        lora_in = lsem("lora_in")
        iota_done = lsem("iota_done")
        consts_done = lsem("consts_done")
        dve_step = lsem("dve_step")
        rows_turned = lsem("rows_turned")
        vec_ready = lsem("vec_ready")
        hist_turned = lsem("hist_turned")
        hist_ready = lsem("hist_ready")
        ms_ready = lsem("ms_ready")
        rms_ready = lsem("rms_ready")
        xn_ready = lsem("xn_ready")
        x_turned = lsem("x_turned")
        hT_ready = lsem("hT_ready")
        proj_first = lsem("proj_first")
        proj_read = lsem("proj_read")
        uv_ready = lsem("uv_ready")
        u_ready = lsem("u_ready")
        edge_ready = lsem("edge_ready")
        diff_ready = lsem("diff_ready")
        last_taken = lsem("last_taken")
        shifted = lsem("shifted")
        lora_act = lsem("lora_act")
        lora_w = lsem("lora_w")
        lora_a = lsem("lora_a")
        lora_g = lsem("lora_g")
        decay_sig = lsem("decay_sig")
        rate_sig = lsem("rate_sig")
        gate_read = lsem("gate_read")
        kk_sq = lsem("kk_sq")
        kk_sum = lsem("kk_sum")
        kk_root = lsem("kk_root")
        rk_ready = lsem("rk_ready")
        rk_sum = lsem("rk_sum")
        last_turned = lsem("last_turned")
        last_copied = lsem("last_copied")
        cout_turned = lsem("cout_turned")
        cout_copied = lsem("cout_copied")
        s0_turned = lsem("s0_turned")
        s0_read = lsem("s0_read")
        pool_step = lsem("pool_step")
        conv_step = lsem("conv_step")

        order = [2 * n + b for n in IN_ORDER for b in range(2)]
        a_index = {cb: i for i, cb in enumerate(cb for cb in order if cb < NBA)}
        u_index = {cb: i for i, cb in enumerate(cb for cb in order if cb >= NBA + 4)}

        def wait_proj(eng, n):
            if n % 2:
                eng.wait_ge(unit_used, n // 2 + 1)
            else:
                eng.wait_ge(proj_first, n // 2 + 1)

        with nc.Block() as block:
            @block.sync
            def _(sp):
                sp.dma_start(xt[0:META, 0, :], a["meta_tokens"]).then_inc(x_in, 16)
                sp.dma_start(xt[META:P, 0, :], a["x_prompt"][0, 0:P - META, :]).then_inc(x_in, 16)
                sp.dma_start(xt[:, 1, :], a["x_prompt"][0, P - META:2 * P - META, :]).then_inc(x_in, 16)
                sp.dma_start(xt[0:META, 2, :], a["x_prompt"][0, 2 * P - META:SEQ, :]).then_inc(x_in, 16)
                sp.dma_start(xt[META:META + NSA, 2, :],
                             a["x_sample"].rearrange("s t d -> (s t) d")).then_inc(x_in, 16)
                for t in range(RING):
                    load_unit(sp, t)
                sp.wait_ge(hT_ready, 6)
                sp.dma_start(s0c[:, :, :].rearrange("p (s j) k -> p s j k", j=NPAIR),
                             a["state_wkv"][0].rearrange("s (j h) v k -> (h v) s j k", h=2)) \
                    .then_inc(s0_in, 16)
                sp.dma_start(a["conv_sample"][0][:, 0:HIST - SL, :],
                             a["state_conv"][0][:, SL:HIST, :]).then_inc(out_stored, 16)
                for t in range(RING, UPRE):
                    load_unit(sp, t)
                sp.wait_ge(last_copied, 1)
                sp.dma_start(a["shift_prompt"][0, 0].rearrange("(b p) -> b p", p=P),
                             lastT[0:NBA, :]).then_inc(out_stored, 16)
                sp.dma_start(a["shift_sample"][0].rearrange("s (b p) -> (s b) p", p=P),
                             lastT[NBA:NBA * (1 + NSEQ), :]).then_inc(out_stored, 16)
                sp.wait_ge(cout_copied, 2)
                sp.dma_start(a["conv_prompt"][0, 0], cpT[0:HIST, :]).then_inc(out_stored, 16)
                for s in range(NSEQ):
                    sp.dma_start(a["conv_sample"][0, s, HIST - SL:HIST, :],
                                 csT[SL * s:SL * s + SL, :]).then_inc(out_stored, 16)
                sp.wait_ge(out_stored, 16 * (4 + NSEQ))

            stores[0] = 4 + NSEQ

            @block.gpsimd
            def _(pool):
                nc.gpsimd.iota(icol, [[1, P]], base=0, channel_multiplier=0).then_inc(iota_done, 1)
                nc.gpsimd.iota(irow, [[0, P]], base=0, channel_multiplier=1).then_inc(iota_done, 1)
                link = chain(pool, pool_step)
                nc.gpsimd.memset(edge[:, :, 0:1], 0.0)
                nc.gpsimd.memset(ext[:, :, 0:HIST], 0.0)
                link(nc.gpsimd.memset(zsBD[:, :, :], 0.0))
                n_u = 0
                pool.wait_ge(hist_ready, 8)
                for n, cb in enumerate(order):
                    if cb >= NBA + 4:
                        j = cb - NBA - 4
                        pool.wait_ge(uv_ready, n + 1)
                        nc.gpsimd.tensor_tensor(ext_prompt(j, HIST, NPR), uval[:, j % 2, 0:NPR],
                                                usig[:, j % 2, 0:NPR], ALU.mult)
                        nc.gpsimd.tensor_tensor(ext_sample(j, HIST, SL), by_seq(uval[:, j % 2, :]),
                                                by_seq(usig[:, j % 2, :]), ALU.mult)
                        nc.gpsimd.tensor_tensor(uflat[:, j, :], uval[:, j % 2, NPR:NT],
                                                usig[:, j % 2, NPR:NT], ALU.mult).then_inc(u_ready, 1)
                        n_u += 1
                    elif cb < NBA:
                        i = a_index[cb]
                        b = i % 2
                        pool.wait_ge(edge_ready, i + 1)
                        if i >= 2:
                            pool.wait_ge(shifted, i - 1)
                        nc.gpsimd.tensor_tensor(diff[:, b, 0:NPR], edge_prompt(b, 0, NPR),
                                                edge_prompt(b, 1, NPR), ALU.subtract)
                        nc.gpsimd.tensor_tensor(by_seq(diff[:, b, :]), edge_sample(b, 0, SL),
                                                edge_sample(b, 1, SL), ALU.subtract).then_inc(diff_ready, 1)
                        nc.gpsimd.tensor_copy(lastc[:, cb:cb + 1], edge_prompt(b, NPR, 1))
                        nc.gpsimd.tensor_copy(lastc[:, NBA:].rearrange("p (s b) -> p s b", b=NBA)[:, :, cb:cb + 1],
                                              edge_sample(b, SL, 1)).then_inc(last_taken, 1)

            @block.scalar
            def _(act):
                at = 0
                for name, n in [("norm_mix", 8), ("tshift_mu", 14), ("decay_w0", 4), ("iclr_a0", 4), ("k_k", 4),
                                ("k_a", 4), ("r_k", 4), ("glu_b", 8), ("dw_bias", 4), ("conv_ln_w", 4),
                                ("conv_ln_b", 4), ("lnx_w", 4), ("lnx_b", 4)]:
                    src = a[name][0]
                    if name == "r_k":
                        src = src.rearrange("h k -> (h k)")
                    act.dma_start(vrow[at:at + n, 0, :], src.rearrange("(c p) -> c p", p=P)).then_inc(rows_in, 16)
                    at += n
                act.dma_start(vrow[0:CW * 4, 1, :],
                              a["dw_weight"][0].rearrange("t (c p) -> (t c) p", p=P)).then_inc(rows_in, 16)
                act.dma_start(vrow[0:NSEQ * NBA, 2, :],
                              a["state_shift"][0].rearrange("s (c p) -> (s c) p", p=P)).then_inc(rows_in, 16)
                act.dma_start(cbuf[0:120, :, :],
                              a["state_conv"][0].rearrange("(g s) t c -> (s t) g c", g=2)).then_inc(hist_in, 16)
                act.dma_start(loraw[0:64, 0, :], a["decay_w2"][0]).then_inc(lora_in, 16)
                act.dma_start(loraw[64:128, 0, :], a["iclr_a2"][0]).then_inc(lora_in, 16)
                act.dma_start(loraw[:, 1, :], a["gate_g2"][0]).then_inc(lora_in, 16)
                act.wait_ge(rows_turned, 1)
                nc.scalar.copy(vecA[:, 0:NVEC], bank[:, 7, 0:NVEC])
                nc.scalar.copy(vecW[:, :], bank[:, 7, P:P + CW * 4])
                nc.scalar.copy(vecS[:, :], bank[:, 7, 2 * P:2 * P + NSEQ * NBA]).then_inc(vec_ready, 1)
                for g in range(2):
                    act.wait_ge(hist_turned, g + 1)
                    for j in range(4):
                        nc.scalar.copy(ext_sample(j, 0, HIST)[:, 4 * g:4 * g + 4, :],
                                       bank[:, 5 + g, j * 120:j * 120 + 120]
                                       .rearrange("p (s t) -> p s t", t=HIST)).then_inc(hist_ready, 1)
                for i, (t0, n) in enumerate(TILES):
                    act.wait_ge(ms_ready, i + 1)
                    nc.scalar.activation(small[0:n, 4 + i:5 + i], small[0:n, i:i + 1], ACT.Sqrt)\
                        .then_inc(rms_ready, 1)
                for n, cb in enumerate(order):
                    wait_proj(act, n)
                    src = bank[:, n % 4, 0:NT]
                    if cb >= NBA:
                        j = cb - NBA
                        if j < 4:
                            if j >= 2:
                                act.wait_ge(u_ready, j - 1)
                            nc.scalar.activation(uval[:, j % 2, :], src, ACT.Identity,
                                                 bias=vecA[:, V_GLU + j:V_GLU + j + 1]).then_inc(uv_ready, 1)
                        else:
                            if j >= 6:
                                act.wait_ge(u_ready, j - 5)
                            nc.scalar.activation(usig[:, j % 2, :], src, ACT.Sigmoid,
                                                 bias=vecA[:, V_GLU + j:V_GLU + j + 1]).then_inc(uv_ready, 1)
                        act.wait_ge(uv_ready, n + 1)
                    else:
                        i = a_index[cb]
                        b = i % 2
                        if i >= 2:
                            act.wait_ge(shifted, i - 1)
                            act.wait_ge(last_taken, i - 1)
                        nc.scalar.copy(edge_prompt(b, 1, NPR), src[:, 0:NPR])
                        nc.scalar.copy(edge_sample(b, 0, 1),
                                       vecS.rearrange("p (s b) -> p s b", b=NBA)[:, :, cb:cb + 1])
                        nc.scalar.copy(edge_sample(b, 1, SL), by_seq(src)).then_inc(edge_ready, 1)
                        act.wait_ge(edge_ready, i + 1)
                    nc.scalar.sem_inc(proj_read, 1)
                act.wait_ge(shifted, a_index[13] + 1)
                nc.scalar.activation(lor_tanh, lor_in[0:64, 0, :], ACT.Tanh).then_inc(lora_act, 1)
                nc.scalar.activation(lor_sig, lor_in[:, 1, :], ACT.Sigmoid).then_inc(lora_act, 1)
                for j in range(4):
                    act.wait_ge(lora_w, j + 1)
                    nc.scalar.activation(ldT[:, j, :], bank[:, j, 0:NT], ACT.Sigmoid,
                                         bias=vecA[:, V_W0 + j:V_W0 + j + 1]).then_inc(decay_sig, 1)
                for j in range(4):
                    act.wait_ge(lora_a, j + 1)
                    nc.scalar.activation(bT[:, j, :], bank[:, 4 + j, 0:NT], ACT.Sigmoid,
                                         bias=vecA[:, V_A0 + j:V_A0 + j + 1]).then_inc(rate_sig, 1)
                for j in range(4):
                    act.wait_ge(lora_g, j + 1)
                    nc.scalar.copy(gT[:, j, :], bank[:, j, 0:NT]).then_inc(gate_read, 1)
                for j in range(4):
                    act.wait_ge(kk_sum, j + 1)
                    nc.scalar.activation(tmpA[:, j, :], bank[:, 4 + j, 0:NT], ACT.Sqrt).then_inc(kk_root, 1)
                act.wait_ge(last_turned, 1)
                nc.scalar.copy(lastT[0:NBA * (1 + NSEQ), :], bank[0:NBA * (1 + NSEQ), 0, 0:P])\
                    .then_inc(last_copied, 1)
                act.wait_ge(cout_turned, 1)
                nc.scalar.copy(cpT[0:HIST, :], bank[0:HIST, 1, :]).then_inc(cout_copied, 1)
                act.wait_ge(cout_turned, 2)
                nc.scalar.copy(csT[0:NSA, :], bank[0:NSA, 2, :]).then_inc(cout_copied, 1)
                for g in range(8):
                    act.wait_ge(s0_turned, g + 1)
                    src = shaped(bank[0:64, g % 2, :], 4, P)
                    for i in range(2):
                        nc.scalar.copy(zsBD[64 * i:64 * i + 64, 4 * g:4 * g + 4, 64 * i:64 * i + 64],
                                       src[:, :, 64 * i:64 * i + 64]).then_inc(s0_read, 1)

            @block.tensor
            def _(pe):
                pe.wait_ge(consts_done, 1)
                pe.wait_ge(rows_in, 16 * 15)
                nc.tensor.transpose(bank[:, 7, 0:NVEC], vrow[0:NVEC, 0, :], ident[0:NVEC, 0:NVEC])
                nc.tensor.transpose(bank[:, 7, P:P + CW * 4], vrow[0:CW * 4, 1, :], ident[0:CW * 4, 0:CW * 4])
                nc.tensor.transpose(bank[:, 7, 2 * P:2 * P + NSEQ * NBA], vrow[0:NSEQ * NBA, 2, :],
                                    ident[0:NSEQ * NBA, 0:NSEQ * NBA]).then_inc(rows_turned, 1)
                pe.wait_ge(hist_in, 16)
                for g in range(2):
                    for j in range(4):
                        mm = nc.tensor.transpose(bank[:, 5 + g, j * 120:j * 120 + 120],
                                                 cbuf[0:120, g, j * P:j * P + P], ident[0:120, 0:120])
                    mm.then_inc(hist_turned, 1)
                for i, (t0, n) in enumerate(TILES):
                    pe.wait_ge(xn_ready, i + 1)
                    for hb in range(2):
                        if i >= 1:
                            pe.wait_ge(hT_ready, 2 * i - 1 + hb)
                        for c in range(4):
                            mm = nc.tensor.transpose(bank[:, 3 + hb, c * P:c * P + n],
                                                     xt[0:n, i, (4 * hb + c) * P:(4 * hb + c + 1) * P],
                                                     ident[0:n, 0:n])
                        mm.then_inc(x_turned, 1)
                pe.wait_ge(hT_ready, 6)
                for n, cb in enumerate(order):
                    t, b = n // 2, n % 2
                    if b == 0:
                        wait_unit(pe, t)
                    if n >= 4:
                        pe.wait_ge(proj_read, n - 3)
                    w = slot(t, 256)
                    for c in range(KC):
                        mm = nc.tensor.matmul(bank[:, n % 4, 0:NT], w[:, c, b * P:b * P + P], hT[:, c, :],
                                              start=(c == 0), stop=(c == KC - 1))
                    mm.then_inc(unit_used if b else proj_first, 1)
                pe.wait_ge(lora_in, 48)
                pe.wait_ge(lora_act, 2)
                pe.wait_ge(proj_read, 22)
                for j in range(4):
                    nc.tensor.matmul(bank[:, j, 0:NT], loraw[0:64, 0, j * P:j * P + P], lor_tanh,
                                     start=True, stop=True).then_inc(lora_w, 1)
                for j in range(4):
                    nc.tensor.matmul(bank[:, 4 + j, 0:NT], loraw[64:128, 0, j * P:j * P + P], lor_in[64:128, 0, :],
                                     start=True, stop=True).then_inc(lora_a, 1)
                for j in range(4):
                    pe.wait_ge(decay_sig, j + 1)
                    nc.tensor.matmul(bank[:, j, 0:NT], loraw[:, 1, j * P:j * P + P], lor_sig,
                                     start=True, stop=True).then_inc(lora_g, 1)
                for j in range(4):
                    pe.wait_ge(rate_sig, j + 1)
                    pe.wait_ge(kk_sq, 1)
                    nc.tensor.matmul(bank[:, 4 + j, 0:NT], headones, tmpA[:, j, :],
                                     start=True, stop=True).then_inc(kk_sum, 1)
                pe.wait_ge(gate_read, 4)
                pe.wait_ge(last_taken, NBA)
                nc.tensor.transpose(bank[0:NBA * (1 + NSEQ), 0, 0:P], lastc[:, :], ident).then_inc(last_turned, 1)
                for j in range(4):
                    mm = nc.tensor.transpose(bank[0:HIST, 1, j * P:j * P + P], ext_prompt(j, NPR, HIST), ident)
                mm.then_inc(cout_turned, 1)
                for j in range(4):
                    mm = nc.tensor.transpose(bank[0:NSA, 2, j * P:j * P + P], uflat[:, j, :], ident)
                mm.then_inc(cout_turned, 1)
                pe.wait_ge(kk_root, 4)
                pe.wait_ge(rk_ready, 1)
                for j in range(4):
                    nc.tensor.matmul(bank[:, 4 + j, 0:NT], headones, tmpA[:, j, :],
                                     start=True, stop=True).then_inc(rk_sum, 1)
                pe.wait_ge(s0_in, 16)
                pe.wait_ge(last_copied, 1)
                pe.wait_ge(cout_copied, 1)
                for g in range(8):
                    if g >= 2:
                        pe.wait_ge(s0_read, 2 * (g - 1))
                    for q in range(4):
                        mm = nc.tensor.transpose(bank[0:64, g % 2, q * P:q * P + P], s0c[:, 4 * g + q, :], ident)
                    mm.then_inc(s0_turned, 1)

            @block.vector
            def _(dve):
                link = chain(dve, dve_step)
                V = nc.vector
                dve.wait_ge(iota_done, 2)
                link(V.tensor_tensor(ixor, icol, irow, ALU.bitwise_xor))
                V.tensor_scalar(ident, ixor, 0.0, None, ALU.is_equal)
                V.tensor_scalar(headones, ixor, 64.0, None, ALU.is_lt)
                V.tensor_scalar(level0, ixor, 1.0, None, ALU.is_equal)
                link(V.memset(ones, 1.0))
                V.memset(onesbf, 1.0).then_inc(consts_done, 1)
                V.tensor_tensor(tribf, irow, icol, ALU.is_lt)
                V.tensor_copy(rowf, irow[:, 0:1])
                V.tensor_copy(slot_iota, icol[:, 0:C])
                V.tensor_copy(exp_iota, icol[:, 0:NE])
                link(V.tensor_scalar(rowm, irow, 63, None, ALU.bitwise_and))
                link(V.tensor_scalar(itmp, ixor, 63, None, ALU.bitwise_and))
                for l in range(7):
                    last = V.tensor_scalar(geq[:, l, :], itmp[:, 0:C], float(2 ** l), None, ALU.is_ge)
                V.tensor_tensor(strict[:, 0, :], rowm[:, 0:C], icol[:, 0:C], ALU.is_lt)
                V.tensor_tensor(incl[:, 0, :], rowm[:, 0:C], icol[:, 0:C], ALU.is_le)
                V.tensor_scalar(row16[:, 0:1], rowm[:, 0:1], 16.0, None, ALU.is_lt)
                link(V.memset(row16[:, 1:2], 1.0))
                link(V.tensor_tensor(level[:, :, :], geq[:, 0:6, :], geq[:, 1:7, :], ALU.subtract))
                link(V.tensor_scalar(geq[:, 3, :], geq[:, 3, :], -1.0, 1.0, ALU.mult, ALU.add))
                V.tensor_tensor(strict[:, 1, :], strict[:, 0, :], geq[:, 3, :], ALU.mult)
                V.tensor_tensor(incl[:, 1, :], incl[:, 0, :], geq[:, 3, :], ALU.mult)
                link(V.tensor_scalar(itmp, rowm, 3, None, ALU.logical_shift_right))
                link(V.tensor_tensor(seqrow, itmp[:, 0:NSEQ], icol[:, 0:NSEQ], ALU.is_equal))
                dve.wait_ge(x_in, 16 * 5)
                for i, (t0, n) in enumerate(TILES):
                    link(V.tensor_tensor_reduce(out=junk[0:n, :], in0=xt[0:n, i, :], in1=xt[0:n, i, :], scale=1.0,
                                                scalar=0.0, op0=ALU.mult, op1=ALU.add,
                                                accum_out=small[0:n, 8 + i:9 + i]))
                    V.tensor_scalar(small[0:n, i:i + 1], small[0:n, 8 + i:9 + i], 1.0 / DM, RMS_EPS,
                                    ALU.mult, ALU.add).then_inc(ms_ready, 1)
                for i, (t0, n) in enumerate(TILES):
                    dve.wait_ge(rms_ready, i + 1)
                    link(V.reciprocal(small[0:n, 12 + i:13 + i], small[0:n, 4 + i:5 + i]))
                    V.tensor_scalar(xt[0:n, i, :], xt[0:n, i, :], small[0:n, 12 + i:13 + i], None,
                                    ALU.mult).then_inc(xn_ready, 1)
                dve.wait_ge(vec_ready, 1)
                for i, (t0, n) in enumerate(TILES):
                    for hb in range(2):
                        dve.wait_ge(x_turned, 2 * i + hb + 1)
                        V.tensor_tensor(hT[:, 4 * hb:4 * hb + 4, t0:t0 + n],
                                        shaped(bank[:, 3 + hb, :], 4, P)[:, :, 0:n],
                                        b3(vecA[:, V_NORM + 4 * hb:V_NORM + 4 * hb + 4], n),
                                        ALU.mult).then_inc(hT_ready, 1)
                link(V.tensor_scalar(vecA[:, V_OMKA:V_OMKA + 4], vecA[:, V_KA:V_KA + 4], -1.0, 1.0,
                                     ALU.mult, ALU.add))

                def conv_steps():
                    for tap in range(CW):
                        for j in range(4):
                            w = vecW[:, 4 * tap + j:4 * tap + j + 1]
                            if tap == 0:
                                dve.wait_ge(u_ready, j + 1)
                                bias = vecA[:, V_DWB + j:V_DWB + j + 1]
                                V.tensor_scalar(zT[:, j, 0:NPR], ext_prompt(j, tap, NPR), w, bias,
                                                ALU.mult, ALU.add)
                                V.tensor_scalar(by_seq(zT[:, j, :]), ext_sample(j, tap, SL), w, bias,
                                                ALU.mult, ALU.add).then_inc(conv_step, 1)
                            else:
                                dve.wait_ge(conv_step, 4 * (tap - 1) + j + 1)
                                V.scalar_tensor_tensor(zT[:, j, 0:NPR], ext_prompt(j, tap, NPR), w,
                                                       zT[:, j, 0:NPR], ALU.mult, ALU.add)
                                V.scalar_tensor_tensor(by_seq(zT[:, j, :]), ext_sample(j, tap, SL), w,
                                                       by_seq(zT[:, j, :]), ALU.mult, ALU.add)\
                                    .then_inc(conv_step, 1)
                            yield

                conv = conv_steps()
                share = -(-CW * 4 // NBA)
                a_order = sorted(a_index, key=a_index.get)
                for i, cb in enumerate(a_order):
                    b = i % 2
                    dst = [rT, kT, vT][cb // 4][:, cb % 4, :] if cb < 12 else lor_in[:, cb - 12, :]
                    mu = vecA[:, V_MU + cb:V_MU + cb + 1]
                    dve.wait_ge(diff_ready, i + 1)
                    V.scalar_tensor_tensor(dst[:, 0:NPR], diff[:, b, 0:NPR], mu, edge_prompt(b, 1, NPR),
                                           ALU.mult, ALU.add)
                    V.scalar_tensor_tensor(by_seq(dst), by_seq(diff[:, b, :]), mu, edge_sample(b, 1, SL),
                                           ALU.mult, ALU.add).then_inc(shifted, 1)
                    for _ in range(share):
                        next(conv, None)
                for _ in conv:
                    pass
                dve.wait_ge(shifted, NBA)
                for j in range(4):
                    last = V.tensor_scalar(kkT[:, j, :], kT[:, j, :], vecA[:, V_KK + j:V_KK + j + 1], None, ALU.mult)
                link(last)
                V.tensor_tensor(tmpA[:, :, :], kkT[:, :, :], kkT[:, :, :], ALU.mult).then_inc(kk_sq, 1)
                dve.wait_ge(decay_sig, 4)
                V.tensor_scalar(ldT[:, :, :], ldT[:, :, :], -HALF_DECAY, None, ALU.mult)
                dve.wait_ge(kk_root, 4)
                link(V.tensor_scalar(tmpA[:, :, :], tmpA[:, :, :], 1e-12, None, ALU.max))
                link(V.reciprocal(tmpA[:, :, :], tmpA[:, :, :]))
                link(V.tensor_tensor(kkT[:, :, :], kkT[:, :, :], tmpA[:, :, :], ALU.mult))
                dve.wait_ge(rate_sig, 4)
                for j in range(4):
                    last = V.tensor_scalar(tmpA[:, j, :], bT[:, j, :], vecA[:, V_KA + j:V_KA + j + 1],
                                           vecA[:, V_OMKA + j:V_OMKA + j + 1], ALU.mult, ALU.add)
                link(last)
                V.tensor_tensor(bT[:, :, :], kkT[:, :, :], bT[:, :, :], ALU.mult)
                link(V.tensor_tensor(kT[:, :, :], kT[:, :, :], tmpA[:, :, :], ALU.mult))
                for j in range(4):
                    last = V.scalar_tensor_tensor(tmpA[:, j, :], rT[:, j, :], vecA[:, V_RK + j:V_RK + j + 1],
                                                  kT[:, j, :], ALU.mult, ALU.mult)
                last.then_inc(rk_ready, 1)
                for j in range(4):
                    dve.wait_ge(rk_sum, j + 1)
                    V.tensor_tensor(bonT[:, j, :], bank[:, 4 + j, 0:NT], vT[:, j, :], ALU.mult)

        next_stage()
        cursor[0] = mixer_end
        bufs = []
        for q in range(2):
            b = {}
            b["X"] = take(NPAIR, P)
            b["T"] = take(NPAIR, C)
            b["Yc"] = take(NPAIR, C)
            b["tmp"] = take(NPAIR, C)
            b["Wc"] = take(NPAIR, C)
            b["eL"] = take(NPAIR, C)
            b["KqR"] = take(NPAIR, 2, C)
            b["KtBD"] = take(NPAIR, P)
            b["BtBD"] = take(NPAIR, P)
            b["KqBD"] = take(NPAIR, P)
            b["AkT"] = take(NPAIR, P)
            b["M1T"] = take(NPAIR, C)
            b["AbT"] = take(NPAIR, P)
            b["M2T"] = take(NPAIR, C)
            b["Ktok"] = take(NPAIR, P)
            b["Btok"] = take(NPAIR, P)
            b["Vtok"] = take(NPAIR, P)
            b["Vc"] = take(NPAIR, C)
            b["Un"] = take(NPAIR, C)
            b["LDtok"] = b["X"]
            b["Lc"], b["Lx"] = b["T"], b["Yc"]
            b["emL"], b["eLx"] = b["tmp"], b["Wc"]
            b["VBD"] = b["AkT"]
            b["UnBD"] = b["KtBD"]
            bufs.append(b)
        flat = arena[:, mixer_start:mixer_start + 6 * 4 * NT]
        Vx = shaped(flat[:, 0:2048], NPAIR, 512)
        Ux = shaped(flat[:, 2048:4096], NPAIR, 512)
        zso = shaped(flat[:, 4096:6144], NPAIR, 512)
        szb = bufs[1]["BtBD"]

        names = ["zeroed", "ld_turned", "ldtok_ready", "cum_done", "lc_ready", "lx_ready", "el_ready", "eml_ready",
                 "elx_ready", "ktbd_ready", "btbd_ready", "vbd_ready", "q_ready", "kqr_ready", "kqbd_ready",
                 "k_turned", "b_turned", "v_turned", "ktok_ready", "btok_ready", "vtok_ready", "vc_ready",
                 "sk_done", "sb_done", "sk_read", "sb_read", "x1_ready", "x1_turned", "t1_ready",
                 "nt_done", "yc_ready", "tnt_done", "t_ready", "t_turned", "x_ready",
                 "w_done", "wc_ready", "u_done", "un_ready", "unbd_ready", "z_done", "z_ready", "zbd_ready",
                 "y_done", "y_read", "sz_done", "sz_read", "szt_turned", "szt_ready",
                 "vx_ready", "ux_ready", "zs_done", "zso_ready", "scan_step", "pick_ready", "state_sum", "sy_read"]
        S = {n: lsem("scan_" + n) for n in names}

        groups = [(0, 1), (2, 3), (4, 5)]
        plan = {g: [(l, q) for l in range(1, 6) for q in range(2) if l < LEVELS[groups[g][q]]] for g in range(3)}
        number, final, n = {}, {}, 0
        for g in range(3):
            for l, q in plan[g]:
                number[(g, l, q)] = n
                n += 1
                final[groups[g][q]] = n

        def scan_block(g):
            pair = groups[g]

            def bk(q, i):
                return bank[:, 4 * q + i, :]

            with nc.Block() as block:
                @block.gpsimd
                def _(pool):
                    T = nc.gpsimd
                    if g == 0:
                        for q in range(2):
                            for nm in ("KtBD", "BtBD", "KqBD", "AkT", "AbT"):
                                T.memset(bufs[q][nm][:, :, :], 0.0)
                        T.memset(Zc[:, :, :], 0.0)
                        T.memset(ZBD[:, :, :], 0.0).then_inc(S["zeroed"], 1)
                        pool.wait_ge(S["zeroed"], 1)
                    for q, c in enumerate(pair):
                        b, ts = bufs[q], CHUNKS[c]
                        for i in range(2):
                            last = T.tensor_copy(diag(b["VBD"], i), half(vT, i)[:, :, ts:ts + C])
                        last.then_inc(S["vbd_ready"], 1)
                    for q, c in enumerate(pair):
                        b, ts = bufs[q], CHUNKS[c]
                        pool.wait_ge(S["eml_ready"], c + 1)
                        for i in range(2):
                            last = T.tensor_tensor(diag(b["BtBD"], i), half(bT, i)[:, :, ts:ts + C],
                                                   half(b["emL"], i), ALU.mult)
                        last.then_inc(S["btbd_ready"], 1)
                        pool.wait_ge(S["q_ready"], c + 1)
                        for i in range(2):
                            last = T.tensor_copy(diag(b["KqBD"], i), half(b["KqR"][:, :, 0, :], i))
                        last.then_inc(S["kqbd_ready"], 1)
                    for q, c in enumerate(pair):
                        b = bufs[q]
                        pool.wait_ge(S["vtok_ready"], c + 1)
                        for i in range(2):
                            last = T.tensor_copy(half(b["Vc"], i), diag(b["Vtok"], i))
                        last.then_inc(S["vc_ready"], 1)
                    for q, c in enumerate(pair):
                        b = bufs[q]
                        if c == 5:
                            pool.wait_ge(S["vc_ready"], 6)
                            pool.wait_ge(S["kqbd_ready"], 6)
                            pool.wait_ge(S["zbd_ready"], 5)
                            for j in range(NPAIR):
                                T.tensor_tensor(shaped(Vx[:, j, :], NSEQ, HD), b2(b["Vc"][:, j, :], NSEQ),
                                                b3(seqrow, HD), ALU.mult).then_inc(S["vx_ready"], 1)
                            pool.wait_ge(S["vx_ready"], NPAIR)
                        pool.wait_ge(S["un_ready"], c + 1)
                        for i in range(2):
                            last = T.tensor_copy(diag(b["UnBD"], i), half(b["Un"], i))
                        last.then_inc(S["unbd_ready"], 1)
                        if c < 5:
                            pool.wait_ge(S["z_ready"], c + 1)
                            pool.wait_ge(S["y_done"], c + 1)
                            for i in range(2):
                                last = T.tensor_copy(diag(ZBD, i), half(Zc, i))
                            last.then_inc(S["zbd_ready"], 1)

                @block.scalar
                def _(act):
                    A = nc.scalar
                    for q, c in enumerate(pair):
                        b = bufs[q]
                        act.wait_ge(S["ld_turned"], c + 1)
                        A.copy(b["LDtok"].rearrange("p j c -> p (j c)")[0:C, :], bk(q, 0)[0:C, :])\
                            .then_inc(S["ldtok_ready"], 1)
                        act.wait_ge(S["cum_done"], c + 1)
                        A.copy(b["Lc"], shaped(bk(q, 1)[:, 0:NPAIR * C], NPAIR, C)).then_inc(S["lc_ready"], 1)
                        act.wait_ge(S["lc_ready"], c + 1)
                        A.activation(b["emL"], b["Lc"], ACT.Exp, scale=-1.0).then_inc(S["eml_ready"], 1)
                        A.activation(b["eL"], b["Lc"], ACT.Exp).then_inc(S["el_ready"], 1)
                        act.wait_ge(S["lx_ready"], c + 1)
                        A.activation(b["eLx"], b["Lx"], ACT.Exp).then_inc(S["elx_ready"], 1)
                    for q, c in enumerate(pair):
                        b = bufs[q]
                        act.wait_ge(S["v_turned"], c + 1)
                        A.copy(b["Vtok"].rearrange("p j c -> p (j c)"), bk(q, 0)).then_inc(S["vtok_ready"], 1)
                        act.wait_ge(S["k_turned"], c + 1)
                        own = row16[:, 0:1] if c == 4 else row16[:, 1:2]
                        A.activation(b["Ktok"].rearrange("p j c -> p (j c)"), bk(q, 2), ACT.Identity, scale=own)\
                            .then_inc(S["ktok_ready"], 1)
                    for q, c in enumerate(pair):
                        b = bufs[q]
                        act.wait_ge(S["x1_turned"], c + 1)
                        src = shaped(bk(q, 3), NPAIR, P)
                        for i in range(2):
                            last = A.copy(half(b["T"], i), diag(src, i))
                        last.then_inc(S["t1_ready"], 1)
                    for l in range(1, 6):
                        qs = [q for q in range(2) if l < LEVELS[pair[q]]]
                        for q in qs:
                            b, m = bufs[q], number[(g, l, q)]
                            act.wait_ge(S["nt_done"], m + 1)
                            A.copy(b["Yc"], shaped(bk(q, 0)[:, 0:NPAIR * C], NPAIR, C)).then_inc(S["yc_ready"], 1)
                        for q in qs:
                            b, m = bufs[q], number[(g, l, q)]
                            act.wait_ge(S["t_turned"], m + 1)
                            src = shaped(bk(q, 2)[0:C, :], NPAIR, P)
                            for i in range(2):
                                last = A.copy(diag(b["X"], i), src[:, :, 64 * i:64 * i + 64])
                            last.then_inc(S["x_ready"], 1)
                    for q, c in enumerate(pair):
                        b, ts = bufs[q], CHUNKS[c]
                        if c == 5:
                            act.wait_ge(S["sz_done"], 1)
                            A.copy(szb.rearrange("p j c -> p (j c)"), bk(q, 3)).then_inc(S["sz_read"], 1)
                            act.wait_ge(S["szt_turned"], 1)
                            src = shaped(bk(q, 0)[0:C, :], NPAIR, P)
                            for i in range(2):
                                last = A.copy(half(b["tmp"], i), src[:, :, 64 * i:64 * i + 64])
                            last.then_inc(S["szt_ready"], 1)
                        act.wait_ge(S["u_done"], c + 1)
                        A.activation(b["Un"], shaped(bk(q, 2 if c == 5 else 1)[:, 0:NPAIR * C], NPAIR, C),
                                     ACT.Identity, scale=-1.0).then_inc(S["un_ready"], 1)
                        if c < 5:
                            n_own = min(C, NPR - ts)
                            act.wait_ge(S["y_done"], c + 1)
                            A.copy(yT[:, :, ts:ts + n_own],
                                   shaped(bk(q, 3)[:, 0:NPAIR * C], NPAIR, C)[:, :, 0:n_own])\
                                .then_inc(S["y_read"], 1)

                @block.tensor
                def _(pe):
                    M = nc.tensor
                    for q, c in enumerate(pair):
                        b, ts = bufs[q], CHUNKS[c]
                        for j in range(NPAIR):
                            mm = M.transpose(bk(q, 0)[0:C, j * P:j * P + P], ldT[:, j, ts:ts + C], ident)
                        mm.then_inc(S["ld_turned"], 1)
                    for q, c in enumerate(pair):
                        b = bufs[q]
                        pe.wait_ge(S["ldtok_ready"], c + 1)
                        for j in range(NPAIR):
                            mm = M.matmul(bk(q, 1)[:, j * C:j * C + C], b["LDtok"][0:C, j, :],
                                          incl[0:C, int(c == 5), :], start=True, stop=True)
                        mm.then_inc(S["cum_done"], 1)
                        pe.wait_ge(S["vbd_ready"], c + 1)
                        for j in range(NPAIR):
                            mm = M.transpose(bk(q, 0)[:, j * P:j * P + P], b["VBD"][:, j, :], ident)
                        mm.then_inc(S["v_turned"], 1)
                    for q, c in enumerate(pair):
                        b = bufs[q]
                        pe.wait_ge(S["ktbd_ready"], c + 1)
                        for j in range(NPAIR):
                            mm = M.transpose(bk(q, 2)[:, j * P:j * P + P], b["KtBD"][:, j, :], ident)
                        mm.then_inc(S["k_turned"], 1)
                        pe.wait_ge(S["btbd_ready"], c + 1)
                        for j in range(NPAIR):
                            mm = M.transpose(bk(q, 3)[:, j * P:j * P + P], b["BtBD"][:, j, :], ident)
                        mm.then_inc(S["b_turned"], 1)
                    for q, c in enumerate(pair):
                        b = bufs[q]
                        pe.wait_ge(S["kqr_ready"], c + 1)
                        pe.wait_ge(S["lc_ready"], c + 1)
                        for j in range(NPAIR):
                            mm = M.matmul(bk(q, 1)[:, j * P:j * P + P], b["KtBD"][:, j, :],
                                          b["KqR"][:, j, :, :], start=True, stop=True)
                        mm.then_inc(S["sk_done"], 1)
                        pe.wait_ge(S["ktok_ready"], c + 1)
                        for j in range(NPAIR):
                            mm = M.matmul(bk(q, 2)[:, j * P:j * P + P], b["BtBD"][:, j, :],
                                          b["KqR"][:, j, :, :], start=True, stop=True)
                        mm.then_inc(S["sb_done"], 1)
                    for q, c in enumerate(pair):
                        b = bufs[q]
                        pe.wait_ge(S["x1_ready"], c + 1)
                        pe.wait_ge(S["btok_ready"], c + 1)
                        for j in range(NPAIR):
                            mm = M.transpose(bk(q, 3)[:, j * P:j * P + P], b["X"][:, j, :], ident)
                        mm.then_inc(S["x1_turned"], 1)
                    for l in range(1, 6):
                        qs = [q for q in range(2) if l < LEVELS[pair[q]]]
                        for q in qs:
                            b, m = bufs[q], number[(g, l, q)]
                            if l == 1:
                                pe.wait_ge(S["t1_ready"], pair[q] + 1)
                                pe.wait_ge(S["vtok_ready"], pair[q] + 1)
                                pe.wait_ge(S["sb_read"], pair[q] + 1)
                                pe.wait_ge(S["sk_read"], pair[q] + 1)
                            for j in range(NPAIR):
                                mm = M.matmul(bk(q, 0)[:, j * C:j * C + C], b["AbT"][:, j, :], b["T"][:, j, :],
                                              start=True, stop=True)
                            mm.then_inc(S["nt_done"], 1)
                        for q in qs:
                            b, m = bufs[q], number[(g, l, q)]
                            pe.wait_ge(S["yc_ready"], m + 1)
                            if l > 1:
                                pe.wait_ge(S["x_ready"], number[(g, l - 1, q)] + 1)
                            for j in range(NPAIR):
                                mm = M.matmul(bk(q, 1)[:, j * C:j * C + C], b["X"][:, j, :], b["Yc"][:, j, :],
                                              start=True, stop=True)
                            mm.then_inc(S["tnt_done"], 1)
                        for q in qs:
                            b, m = bufs[q], number[(g, l, q)]
                            pe.wait_ge(S["t_ready"], m + 1)
                            for j in range(NPAIR):
                                mm = M.transpose(bk(q, 2)[0:C, j * P:j * P + P], b["T"][:, j, :], ident)
                            mm.then_inc(S["t_turned"], 1)
                    for q, c in enumerate(pair):
                        b = bufs[q]
                        pe.wait_ge(S["kqbd_ready"], c + 1)
                        pe.wait_ge(S["vc_ready"], c + 1)
                        pe.wait_ge(S["sk_read"], c + 1)
                        if c < 5:
                            if c == 0:
                                pe.wait_ge(S["zeroed"], 1)
                            else:
                                pe.wait_ge(S["z_ready"], c)
                            for j in range(NPAIR):
                                M.matmul(bk(q, 0)[:, j * C:j * C + C], b["KqBD"][:, j, :], Zc[:, j, :],
                                         start=True, stop=False)
                                mm = M.matmul(bk(q, 0)[:, j * C:j * C + C], b["AkT"][:, j, :], b["Vc"][:, j, :],
                                              start=False, stop=True)
                            mm.then_inc(S["w_done"], 1)
                            pe.wait_ge(S["x_ready"], final[c])
                            pe.wait_ge(S["wc_ready"], c + 1)
                            for j in range(NPAIR):
                                mm = M.matmul(bk(q, 1)[:, j * C:j * C + C], b["X"][:, j, :], b["Wc"][:, j, :],
                                              start=True, stop=True)
                            mm.then_inc(S["u_done"], 1)
                            pe.wait_ge(S["btok_ready"], c + 1)
                            pe.wait_ge(S["un_ready"], c + 1)
                            for j in range(NPAIR):
                                M.matmul(bk(q, 2)[:, j * C:j * C + C], b["Ktok"][:, j, :], b["Vc"][:, j, :],
                                         start=True, stop=False)
                                mm = M.matmul(bk(q, 2)[:, j * C:j * C + C], b["Btok"][:, j, :], b["Un"][:, j, :],
                                              start=False, stop=True)
                            mm.then_inc(S["z_done"], 1)
                            pe.wait_ge(S["unbd_ready"], c + 1)
                            if c > 0:
                                pe.wait_ge(S["zbd_ready"], c)
                            for j in range(NPAIR):
                                o = bk(q, 3)[:, j * C:j * C + C]
                                M.matmul(o, ZBD[:, j, :], b["KqR"][:, j, 1, :], start=True, stop=False)
                                M.matmul(o, b["Vtok"][:, j, :], b["M1T"][:, j, :], start=False, stop=False)
                                mm = M.matmul(o, b["UnBD"][:, j, :], b["M2T"][:, j, :], start=False, stop=True)
                            mm.then_inc(S["y_done"], 1)
                        else:
                            o = shaped(bk(q, 3), NPAIR * 2, C)
                            for j in range(NPAIR):
                                for s in range(NSEQ):
                                    mm = M.matmul(o[:, 2 * j:2 * j + 2, SL * s:SL * s + SL],
                                                  zsBD[:, NPAIR * s + j, :],
                                                  b["KqR"][:, j, :, SL * s:SL * s + SL], start=True, stop=True)
                            mm.then_inc(S["sz_done"], 1)
                            pe.wait_ge(S["x_ready"], final[c])
                            for j in range(NPAIR):
                                mm = M.matmul(bk(q, 1)[:, j * C:j * C + C], b["AkT"][:, j, :], b["Vc"][:, j, :],
                                              start=True, stop=True)
                            mm.then_inc(S["w_done"], 1)
                            pe.wait_ge(S["sz_read"], 1)
                            for j in range(NPAIR):
                                mm = M.transpose(bk(q, 0)[0:C, j * P:j * P + P], szb[:, j, 0:C], ident)
                            mm.then_inc(S["szt_turned"], 1)
                            pe.wait_ge(S["wc_ready"], c + 1)
                            for j in range(NPAIR):
                                mm = M.matmul(bk(q, 2)[:, j * C:j * C + C], b["X"][:, j, :], b["Wc"][:, j, :],
                                              start=True, stop=True)
                            mm.then_inc(S["u_done"], 1)
                            pe.wait_ge(S["unbd_ready"], c + 1)
                            for j in range(NPAIR):
                                o = bk(q, 1)[:, j * C:j * C + C]
                                M.matmul(o, b["Vtok"][:, j, :], b["M1T"][:, j, :], start=True, stop=False)
                                mm = M.matmul(o, b["UnBD"][:, j, :], b["M2T"][:, j, :], start=False, stop=True)
                            mm.then_inc(S["y_done"], 1)
                            pe.wait_ge(S["btok_ready"], c + 1)
                            for j, i in enumerate((0, 3, 2, 1)):
                                pe.wait_ge(S["vx_ready"], j + 1)
                                pe.wait_ge(S["ux_ready"], j + 1)
                                if i == 0:
                                    pe.wait_ge(S["szt_ready"], 1)
                                if i == 1:
                                    pe.wait_ge(S["sy_read"], 1)
                                M.matmul(bk(q, i), b["Ktok"][:, j, :], Vx[:, j, :], start=True, stop=False)
                                M.matmul(bk(q, i), b["Btok"][:, j, :], Ux[:, j, :], start=False, stop=True)\
                                    .then_inc(S["zs_done"], 1)

                @block.vector
                def _(dve):
                    V = nc.vector
                    dve.wait_ge(S["zeroed"], 1)
                    for q, c in enumerate(pair):
                        b, ts = bufs[q], CHUNKS[c]
                        dve.wait_ge(S["lc_ready"], c + 1)
                        V.tensor_tensor(b["Lx"], b["Lc"], ldT[:, :, ts:ts + C], ALU.subtract)\
                            .then_inc(S["lx_ready"], 1)
                        dve.wait_ge(S["eml_ready"], c + 1)
                        for i in range(2):
                            last = V.tensor_tensor(diag(b["KtBD"], i), half(kT, i)[:, :, ts:ts + C],
                                                   half(b["emL"], i), ALU.mult)
                        last.then_inc(S["ktbd_ready"], 1)
                        dve.wait_ge(S["elx_ready"], c + 1)
                        V.tensor_tensor(b["KqR"][:, :, 0, :], kkT[:, :, ts:ts + C], b["eLx"], ALU.mult)\
                            .then_inc(S["q_ready"], 1)
                        V.tensor_tensor(b["KqR"][:, :, 1, :], rT[:, :, ts:ts + C], b["eL"], ALU.mult)\
                            .then_inc(S["kqr_ready"], 1)
                        dve.wait_ge(S["b_turned"], c + 1)
                        own = row16[:, 0:1] if c == 4 else row16[:, 1:2]
                        V.tensor_scalar(b["Btok"].rearrange("p j c -> p (j c)"), bk(q, 3), own, None, ALU.mult)\
                            .then_inc(S["btok_ready"], 1)
                    for q, c in enumerate(pair):
                        b, w = bufs[q], int(c == 5)
                        dve.wait_ge(S["sk_done"], c + 1)
                        dve.wait_ge(S["v_turned"], c + 1)
                        src = shaped(bk(q, 1), NPAIR, P)
                        for i in range(2):
                            V.tensor_tensor(diag(b["AkT"], i), half(src[:, :, 0:C], i),
                                            b2(half(strict[:, w, :], i), NPAIR), ALU.mult)
                        V.tensor_tensor(b["M1T"], src[:, :, C:P], b2(incl[:, w, :], NPAIR), ALU.mult)\
                            .then_inc(S["sk_read"], 1)
                        dve.wait_ge(S["sb_done"], c + 1)
                        src = shaped(bk(q, 2), NPAIR, P)
                        for i in range(2):
                            V.tensor_tensor(diag(b["AbT"], i), half(src[:, :, 0:C], i),
                                            b2(half(strict[:, w, :], i), NPAIR), ALU.mult)
                        V.tensor_tensor(b["M2T"], src[:, :, C:P], b2(incl[:, w, :], NPAIR), ALU.mult)\
                            .then_inc(S["sb_read"], 1)
                        dve.wait_ge(S["sb_read"], c + 1)
                        dve.wait_ge(S["cum_done"], c + 1)
                        V.tensor_tensor(b["X"], b["AbT"], b2(level0, NPAIR), ALU.mult).then_inc(S["pick_ready"], 1)
                        dve.wait_ge(S["pick_ready"], c + 1)
                        V.tensor_tensor(b["X"], b2(ident, NPAIR), b["X"], ALU.subtract)\
                            .then_inc(S["x1_ready"], 1)
                    for l, q in plan[g]:
                        b, m = bufs[q], number[(g, l, q)]
                        dve.wait_ge(S["tnt_done"], m + 1)
                        V.tensor_tensor(b["tmp"], shaped(bk(q, 1)[:, 0:NPAIR * C], NPAIR, C),
                                        b2(level[:, l, :], NPAIR), ALU.mult).then_inc(S["scan_step"], 1)
                        dve.wait_ge(S["scan_step"], m + 1)
                        V.tensor_tensor(b["T"], b["T"], b["tmp"], ALU.subtract).then_inc(S["t_ready"], 1)
                    for q, c in enumerate(pair):
                        b, ts = bufs[q], CHUNKS[c]
                        dve.wait_ge(S["w_done"], c + 1)
                        if c < 5:
                            V.tensor_copy(b["Wc"], shaped(bk(q, 0)[:, 0:NPAIR * C], NPAIR, C))\
                                .then_inc(S["wc_ready"], 1)
                            dve.wait_ge(S["z_done"], c + 1)
                            V.tensor_tensor(b["tmp"], Zc, shaped(bk(q, 2)[:, 0:NPAIR * C], NPAIR, C), ALU.add)\
                                .then_inc(S["state_sum"], 1)
                            end = min(C, NPR - ts) - 1
                            dve.wait_ge(S["state_sum"], c + 1)
                            if c > 0:
                                dve.wait_ge(S["zbd_ready"], c)
                            V.tensor_tensor(Zc, b["tmp"], b["eL"][:, :, end:end + 1].broadcast_to([P, NPAIR, C]),
                                            ALU.mult).then_inc(S["z_ready"], 1)
                        else:
                            dve.wait_ge(S["szt_ready"], 1)
                            V.tensor_tensor(b["Wc"], shaped(bk(q, 1)[:, 0:NPAIR * C], NPAIR, C), b["tmp"],
                                            ALU.add).then_inc(S["wc_ready"], 1)
                            dve.wait_ge(S["un_ready"], 6)
                            for j in range(NPAIR):
                                V.tensor_tensor(shaped(Ux[:, j, :], NSEQ, HD), b2(b["Un"][:, j, :], NSEQ),
                                                b3(seqrow, HD), ALU.mult).then_inc(S["ux_ready"], 1)
                            dve.wait_ge(S["y_done"], 6)
                            V.tensor_tensor(yT[:, :, NPR:NT], shaped(bk(q, 1)[:, 0:NPAIR * C], NPAIR, C),
                                            szb[:, :, C:P], ALU.add).then_inc(S["sy_read"], 1)
                            zs = zsBD.rearrange("p (s j) v -> p s j v", j=NPAIR)
                            for j, bi in enumerate((0, 3, 2, 1)):
                                dve.wait_ge(S["zs_done"], j + 1)
                                zn = shaped(zso[:, j, :], NSEQ, HD)
                                for i in range(2):
                                    last = V.tensor_tensor(
                                        half(zn, i), half(shaped(bk(q, bi), NSEQ, HD), i),
                                        zs[64 * i:64 * i + 64, :, j, 64 * i:64 * i + 64], ALU.add)
                                last.then_inc(S["state_sum"], 1)
                                dve.wait_ge(S["state_sum"], 6 + j)
                                V.tensor_tensor(zn, zn, b3(b["eL"][:, j, SL - 1:C:SL], HD), ALU.mult)\
                                    .then_inc(S["zso_ready"], 1)

        for g in range(3):
            scan_block(g)

        next_stage()
        cursor[0] = mixer_end
        acc = take(3, DM)
        hp = take(3, DM)
        xT = take(2, KC, C)
        brows_at = cursor[0]
        t1 = take(KC, C)
        u1 = take(KC, C)
        sg = take(KC, C)
        act_ = take(2, KC, C)
        yTm = take(KC, P)
        ysm = take(DM)
        Pm = take(3, P)
        Pg = take(3, P)
        PgT = take(3, P)
        rk = take(6)
        gfin = take(DM)
        brows = arena[:, brows_at:brows_at + 3 * DM].rearrange("p (w d) -> p w d", w=3)
        flat = arena[:, mixer_start:mixer_start + 8 * 4 * NT]
        sout = shaped(zsBD.rearrange("p a b -> p (a b)"), NSEQ * NPAIR, P)
        zpT = shaped(flat[:, 7488:8000], NPAIR, P)
        zsq = shaped(flat[:, 0:4 * NT], 4, NT)
        zvar = shaped(flat[:, 4 * NT:5 * NT], NT)
        ysq = shaped(flat[:, 6144:6144 + 4 * NT], 4, NT)
        h2T = shaped(flat[:, 0:KC * NT], KC, NT)
        at = [KC * NT]

        def bit(*shape, dt=F32):
            n = 1
            for d in shape:
                n *= d
            words = (n + 1) // 2 if dt == BF16 else n
            v = flat[:, at[0]:at[0] + words]
            at[0] += words
            assert at[0] <= 4096
            if dt != F32:
                v = v.bitcast(dt)
            return shaped(v, *shape)

        wr = bit(KC, NE)
        brow = bit(NE)
        logits = bit(3, NE)
        top = bit(3, 8)
        topi = bit(3, 8, dt=U32)
        topf = bit(3, 8)
        ntop = bit(3)
        eg = bit(3, TOPK)
        esum = bit(3)
        erec = bit(3)
        hot = bit(3, NE)
        mask = bit(3, NE)
        maskbf = bit(3, NE, dt=BF16)
        cnt, extra, incA, incB, exc, sel, selt = [bit(NE) for _ in range(7)]
        ovf = bit(4)
        dg = bit(2, NOVER)
        step_n = [0]

        F = {n: lsem("f_" + n) for n in [
            "acc_in", "brows_in", "wr_in", "gffn_in", "gfin_in",
            "zmean_done", "ymean_done", "z_centered", "y_centered", "zvar_done", "yvar_done", "zvar_ready",
            "zroot_ready", "yvar_ready", "yroot_ready", "z_affine", "z_sig", "zT_ready", "yT_ready", "dstep",
            "st_turned", "st_copied", "wout_done", "acc_ready", "ms_ready", "rms_ready", "hp_ready", "h2_turned",
            "h2T_ready", "logits_done", "ntop_ready", "eg_ready", "mask_ready", "rank_done", "diag_ready",
            "tab_done", "tab_ready", "bias_turned", "bias_ready",
            "p_ready", "pg_ready", "xg_done", "x_ready", "g_read", "u_read", "d_read", "t1_ready", "sg_ready",
            "act_ready", "pgt_done", "pgt_ready", "ytm_ready", "ytr_done", "ysm_ready", "cmb_done", "cmb_read",
            "mstep", "fin_ms", "fin_root", "fin_ready", "rank_copied"]}

        def gate_src(w, e, u):
            return w[0][bass.ds(e, 1)].rearrange("o (p c) n -> p (o c) n", c=KC)[:, 2 * u:2 * u + 2, :]

        def down_src(w, e, u):
            return w[0][bass.ds(e, 1)].rearrange("o (c p) n -> p (o c) n", p=P)[:, 2 * u:2 * u + 2, :]

        UNITS = [(w, h, u) for w, h in (("w_gate", 0), ("w_up", 0), ("w_gate", 1), ("w_down", 0), ("w_up", 1),
                                        ("w_down", 1)) for u in range(4)]

        def load_expert_unit(sp, it, n, experts):
            w, h, u = UNITS[n]
            src = (down_src if w == "w_down" else gate_src)(a[w], experts[h], u)
            sp.wait_ge(unit_used, it * UPAIR + (UPRE + n - RING + 1))
            sp.dma_start(slot(UPRE + n, DM), src).then_inc(unit_landed[(UPRE + n) % RING], 16)

        def wait_expert_unit(pe, it, n):
            t = UPRE + n
            pe.wait_ge(unit_landed[t % RING], it * (16 * UPAIR // RING) + 16 * (t // RING + 1))

        def used_through(eng, it, n):
            eng.wait_ge(unit_used, it * UPAIR + (UPRE + n))

        def over_pairs(eng, body, first=PAIRS):
            n_over = eng.value_load(blocktab[0:1, NBLK:NBLK + 1], min_val=0, max_val=NOVER)
            with eng.Fori(first, PAIRS + OPAIRS) as it:
                with eng.If(n_over > (it - PAIRS) * 2):
                    body(it)

        with nc.Block() as block:
            @block.sync
            def _(sp):
                sp.dma_start(acc[0:META, 0, :], a["meta_tokens"]).then_inc(F["acc_in"], 16)
                sp.dma_start(acc[META:P, 0, :], a["x_prompt"][0, 0:P - META, :]).then_inc(F["acc_in"], 16)
                sp.dma_start(acc[:, 1, :], a["x_prompt"][0, P - META:2 * P - META, :]).then_inc(F["acc_in"], 16)
                sp.dma_start(acc[0:META, 2, :], a["x_prompt"][0, 2 * P - META:SEQ, :]).then_inc(F["acc_in"], 16)
                sp.dma_start(acc[META:META + NSA, 2, :],
                             a["x_sample"].rearrange("s t d -> (s t) d")).then_inc(F["acc_in"], 16)
                sp.dma_start(wr, a["w_router"][0].rearrange("(p c) e -> p c e", c=KC)).then_inc(F["wr_in"], 16)
                sp.dma_start(brow[0:1, :], a["b_router"]).then_inc(F["wr_in"], 16)
                sp.dma_start(gffn, a["norm_ffn"][0].rearrange("(p c) -> p c", c=KC)).then_inc(F["gffn_in"], 16)
                for i, nm in enumerate(("b_gate", "b_up", "b_down")):
                    sp.dma_start(brows[0:NE, i, :], a[nm][0]).then_inc(F["brows_in"], 16)
                sp.dma_start(gfin, a["norm_final"].rearrange("(o d) -> o d", o=1).broadcast_to([P, DM]))\
                    .then_inc(F["gfin_in"], 16)
                for n in range(UPAIR):
                    load_expert_unit(sp, 0, n, (0, 1))
                with sp.Fori(1, PAIRS) as it:
                    for n in range(UPAIR):
                        load_expert_unit(sp, it, n, (it * 2, it * 2 + 1))

                def body(it):
                    es = [sp.value_load(blocktab[0:1, bass.ds(it * 2 + h, 1)], min_val=0, max_val=NE - 1)
                          for h in range(2)]
                    for n in range(UPAIR):
                        load_expert_unit(sp, it, n, es)
                sp.wait_ge(F["tab_ready"], 1)
                over_pairs(sp, body)
                for i in range(3):
                    sp.wait_ge(F["fin_ready"], i + 1)
                    if i == 0:
                        sp.dma_start(a["y_prompt"][0, 0:P - META, :], acc[META:P, 0, :]).then_inc(out_stored, 16)
                    elif i == 1:
                        sp.dma_start(a["y_prompt"][0, P - META:2 * P - META, :], acc[:, 1, :])\
                            .then_inc(out_stored, 16)
                    else:
                        sp.dma_start(a["y_prompt"][0, 2 * P - META:SEQ, :], acc[0:META, 2, :])\
                            .then_inc(out_stored, 16)
                        sp.dma_start(a["y_sample"].rearrange("s t d -> (s t) d"), acc[META:META + NSA, 2, :])\
                            .then_inc(out_stored, 16)
                sp.wait_ge(out_stored, 16 * (stores[0] + 9 + 4))

            @block.gpsimd
            def _(pool):
                T = nc.gpsimd
                T.memset(rankm, -1.0)
                T.memset(gates, 0.0).then_inc(F["rank_copied"], 1)
                pool.wait_ge(F["z_centered"], 4)
                T.tensor_tensor(zsq, zT, zT, ALU.mult).then_inc(F["z_centered"], 1)
                pool.wait_ge(F["y_centered"], 4)
                T.tensor_tensor(ysq, yT, yT, ALU.mult).then_inc(F["y_centered"], 1)

            @block.scalar
            def _(act):
                A = nc.scalar
                for n in range(9):
                    act.wait_ge(F["st_turned"], n + 1)
                    dst = sout[0:C, 4 * n:4 * n + 4, :] if n < 8 else zpT[0:C, :, :]
                    A.copy(dst, shaped(bank[0:C, 6 + n % 2, :], 4, P)).then_inc(F["st_copied"], 1)
                act.wait_ge(F["st_copied"], 9)
                for j in range(NPAIR):
                    for h in range(2):
                        act.dma_start(a["wkv_sample"][0][:, 2 * j + h].rearrange("s v k -> v s k"),
                                      sout[0:C, NSEQ * j:NSEQ * j + NSEQ, C * h:C * h + C]).then_inc(out_stored, 16)
                act.dma_start(a["wkv_prompt"][0, 0].rearrange("h v k -> v h k"),
                              zpT[0:C, :, :].rearrange("v j (h k) -> v (j h) k", h=2)).then_inc(out_stored, 16)
                act.wait_ge(F["zvar_ready"], 1)
                A.activation(zvar, zvar, ACT.Sqrt).then_inc(F["zroot_ready"], 1)
                act.wait_ge(F["yvar_ready"], 4)
                A.activation(ysq, ysq, ACT.Sqrt).then_inc(F["yroot_ready"], 1)
                act.wait_ge(F["z_affine"], 4)
                A.activation(zsq, zT, ACT.Sigmoid).then_inc(F["z_sig"], 1)
                act.wait_ge(F["bias_turned"], 1)
                A.copy(biasT[:, 0:2, :, :].rearrange("p w c e -> p (w c e)"), bank[:, 6, :])\
                    .then_inc(F["bias_ready"], 1)
                A.copy(biasT[:, 2:3, :, :].rearrange("p w c e -> p (w c e)"), bank[:, 7, 0:KC * NE])\
                    .then_inc(F["bias_ready"], 1)
                for i, (t0, n) in enumerate(TILES):
                    act.wait_ge(F["ms_ready"], i + 1)
                    A.activation(small[0:n, 20 + i:21 + i], small[0:n, 16 + i:17 + i], ACT.Sqrt)\
                        .then_inc(F["rms_ready"], 1)
                for i, (t0, n) in enumerate(TILES):
                    act.wait_ge(F["ntop_ready"], i + 1)
                    A.activation(eg[0:n, i, :], top[0:n, i, 0:TOPK], ACT.Exp, bias=ntop[0:n, i:i + 1],
                                 accum_out=esum[0:n, i:i + 1]).then_inc(F["eg_ready"], 1)
                def sigmoid(it, h):
                    act.wait_ge(F["t1_ready"], it * 2 + (h + 1))
                    A.activation(sg, t1, ACT.Sigmoid, scale=ALPHA).then_inc(F["sg_ready"], 1)

                def body(it):
                    sigmoid(it, 0)
                    sigmoid(it, 1)
                    act.wait_ge(F["pgt_done"], it + 1)
                    act.wait_ge(F["cmb_done"], it * 6 + 1)
                    A.copy(PgT.rearrange("p i t -> p (i t)")[:, 0:NT], bank[:, 6, 0:NT]).then_inc(F["pgt_ready"], 1)
                    for b in range(2):
                        act.wait_ge(F["ytr_done"], it * 2 + (b + 2))
                        A.copy(ysm[:, 512 * b:512 * b + 512], bank[:, 4 + b, :]).then_inc(F["ysm_ready"], 1)

                with act.Fori(0, PAIRS) as it:
                    body(it)
                act.wait_ge(F["tab_ready"], 1)
                over_pairs(act, body)
                for i, (t0, n) in enumerate(TILES):
                    act.wait_ge(F["fin_ms"], i + 1)
                    A.activation(small[0:n, 36 + i:37 + i], small[0:n, 32 + i:33 + i], ACT.Sqrt)\
                        .then_inc(F["fin_root"], 1)

            @block.tensor
            def _(pe):
                M = nc.tensor
                for j in range(4):
                    mm = M.matmul(bank[:, 4, 0:NT], ones, zT[:, j, :], start=(j == 0), stop=(j == 3))
                mm.then_inc(F["zmean_done"], 1)
                for j in range(4):
                    M.matmul(bank[:, j, 0:NT], headones, yT[:, j, :], start=True, stop=True)\
                        .then_inc(F["ymean_done"], 1)
                for n in range(9):
                    if n >= 2:
                        pe.wait_ge(F["st_copied"], n - 1)
                    for q in range(4):
                        src = zso[:, n // 2, C * (4 * (n % 2) + q):C * (4 * (n % 2) + q) + C] if n < 8 \
                            else Zc[:, q, :]
                        mm = M.transpose(bank[0:C, 6 + n % 2, q * P:q * P + P], src, ident)
                    mm.then_inc(F["st_turned"], 1)
                pe.wait_ge(F["z_centered"], 5)
                for j in range(4):
                    mm = M.matmul(bank[:, 5, 0:NT], ones, zsq[:, j, :], start=(j == 0), stop=(j == 3))
                mm.then_inc(F["zvar_done"], 1)
                pe.wait_ge(F["y_centered"], 5)
                for j in range(4):
                    M.matmul(bank[:, j, 0:NT], headones, ysq[:, j, :], start=True, stop=True)\
                        .then_inc(F["yvar_done"], 1)
                pe.wait_ge(F["brows_in"], 48)
                pe.wait_ge(F["st_copied"], 9)
                for w in range(3):
                    for c in range(KC):
                        o = (w % 2) * KC * NE + c * NE
                        mm = M.transpose(bank[:, 6 + w // 2, o:o + NE], brows[0:NE, w, c * P:c * P + P],
                                         ident[0:NE, 0:NE])
                mm.then_inc(F["bias_turned"], 1)
                pe.wait_ge(F["zT_ready"], 1)
                for u in range(UNITS_OUT):
                    t = UNITS_IN + u
                    wait_unit(pe, t)
                    w = slot(t, DM)
                    if u == 2:
                        pe.wait_ge(F["yT_ready"], 1)
                    if u == 0:
                        pe.wait_ge(F["yvar_ready"], 4)
                    for c in range(2):
                        cc = 2 * OUT_ORDER[u] + c
                        src = zT[:, cc - 4, :] if cc >= 4 else yT[:, cc, :]
                        for i, (t0, n) in enumerate(TILES):
                            for hb in range(2):
                                mm = M.matmul(bank[0:n, 2 * i + hb, :], src[:, t0:t0 + n],
                                              w[:, c, 512 * hb:512 * hb + 512],
                                              start=(u == 0 and c == 0), stop=(u == 3 and c == 1))
                    mm.then_inc(unit_used, 1)
                for i, (t0, n) in enumerate(TILES):
                    pe.wait_ge(F["hp_ready"], i + 1)
                    if i == 0:
                        pe.wait_ge(F["acc_ready"], 6)
                    for hb in range(2):
                        if i >= 1:
                            pe.wait_ge(F["h2T_ready"], 2 * i - 1 + hb)
                        for c in range(4):
                            mm = M.transpose(bank[:, hb, c * P:c * P + n],
                                             hp[0:n, i, (4 * hb + c) * P:(4 * hb + c + 1) * P], ident[0:n, 0:n])
                        mm.then_inc(F["h2_turned"], 1)
                pe.wait_ge(F["wr_in"], 32)
                for i, (t0, n) in enumerate(TILES):
                    pe.wait_ge(F["h2T_ready"], 2 * i + 2)
                    for c in range(KC):
                        M.matmul(bank[0:n, 2, NE * i:NE * i + NE], h2T[:, c, t0:t0 + n], wr[:, c, :],
                                 start=(c == 0), stop=False)
                    mm = M.matmul(bank[0:n, 2, NE * i:NE * i + NE], ones[0:1, 0:n], brow[0:1, :],
                                  start=False, stop=True)
                mm.then_inc(F["logits_done"], 1)
                pe.wait_ge(F["mask_ready"], 1)
                for i, (t0, n) in enumerate(TILES):
                    o = bank[0:n, 3, NE * i:NE * i + NE]
                    for k in range(i):
                        M.matmul(o, onesbf[0:P, 0:n], maskbf[0:P, k, :], start=(k == 0), stop=False)
                    M.matmul(o, tribf[0:n, 0:n], maskbf[0:n, i, :], start=(i == 0), stop=True)
                for i, (t0, n) in enumerate(TILES):
                    mm = M.matmul(bank[:, 3, NE * 3:NE * 4], onesbf[0:n, :], maskbf[0:n, i, :],
                                  start=(i == 0), stop=(i == 2))
                mm.then_inc(F["rank_done"], 1)
                pe.wait_ge(F["diag_ready"], 1)
                M.matmul(bank[:, 2, 0:2 * NOVER], ones[0:NOVER, :], dg[0:NOVER, :, :].rearrange("p a b -> p (a b)"),
                         start=True, stop=True).then_inc(F["tab_done"], 1)

                def gather(it, h, first=False):
                    if h == 0:
                        pe.wait_ge(F["p_ready"], it + 1)
                    o = bank[:, 7 * h, :]
                    for c in range(KC):
                        for i, (t0, n) in enumerate(TILES):
                            mm = M.matmul(o[:, c * C:c * C + C], hp[0:n, i, c * P:c * P + P],
                                          Pm[0:n, i, C * h:C * h + C], start=(i == 0), stop=(i == 2))
                    mm.then_inc(F["xg_done"], 1)

                def product(it, first, o, rhs):
                    for u in range(4):
                        wait_expert_unit(pe, it, first + u)
                        w = slot(UPRE + first + u, DM)
                        for c in range(2):
                            for m in range(KC):
                                mm = M.matmul(o[:, m * C:m * C + C], w[:, c, m * P:m * P + P], rhs[:, 2 * u + c, :],
                                              start=(u == 0 and c == 0 and m == 0),
                                              stop=(u == 3 and c == 1 and m == KC - 1), skip_group_check=True)
                        mm.then_inc(unit_used, 1)

                def body(it):
                    pe.wait_ge(F["x_ready"], it * 2 + 2)
                    pe.wait_ge(F["g_read"], it * 2 + 1)
                    product(it, 0, bank[:, 1, :], xT[:, 0])
                    pe.wait_ge(F["u_read"], it * 2 + 1)
                    product(it, 4, bank[:, 2, :], xT[:, 0])
                    pe.wait_ge(F["g_read"], it * 2 + 2)
                    product(it, 8, bank[:, 1, :], xT[:, 1])
                    pe.wait_ge(F["act_ready"], it * 2 + 1)
                    pe.wait_ge(F["d_read"], it * 2 + 1)
                    product(it, 12, bank[:, 3, :], act_[:, 0])
                    pe.wait_ge(F["u_read"], it * 2 + 2)
                    product(it, 16, bank[:, 2, :], xT[:, 1])
                    pe.wait_ge(F["pg_ready"], it + 1)
                    pe.wait_ge(F["cmb_read"], it * 6 + 2)
                    for i, (t0, n) in enumerate(TILES):
                        mm = M.transpose(bank[:, 6, i * P:i * P + n], Pg[0:n, i, :], ident[0:n, 0:n])
                    mm.then_inc(F["pgt_done"], 1)
                    gather(it + 1, 0)
                    gather(it + 1, 1)
                    pe.wait_ge(F["act_ready"], it * 2 + 2)
                    pe.wait_ge(F["d_read"], it * 2 + 2)
                    product(it, 20, bank[:, 3, :], act_[:, 1])
                    pe.wait_ge(F["ytm_ready"], it * 2 + 2)
                    pe.wait_ge(F["ysm_ready"], it * 2 + 1)
                    for b in range(2):
                        for c in range(4):
                            mm = M.transpose(bank[:, 4 + b, c * P:c * P + P], yTm[:, 4 * b + c, :], ident)
                        mm.then_inc(F["ytr_done"], 1)
                    pe.wait_ge(F["pgt_ready"], it + 1)
                    pe.wait_ge(F["x_ready"], it * 2 + 4)
                    for hb in range(2):
                        pe.wait_ge(F["ysm_ready"], it * 2 + (hb + 2))
                        for i, (t0, n) in enumerate(TILES):
                            k = 3 * hb + i
                            pe.wait_ge(F["cmb_read"], it * 6 + (k + 1))
                            M.matmul(bank[0:n, 6 + k % 2, :], PgT[:, i, 0:n], ysm[:, 512 * hb:512 * hb + 512],
                                     start=True, stop=True).then_inc(F["cmb_done"], 1)

                pe.sem_inc(F["cmb_done"], 1)
                pe.sem_inc(F["ytr_done"], 1)
                gather(0, 0)
                gather(0, 1)
                with pe.Fori(0, PAIRS) as it:
                    body(it)
                pe.wait_ge(F["tab_ready"], 1)
                over_pairs(pe, body)

            @block.vector
            def _(dve):
                V = nc.vector
                link = chain(dve, F["dstep"])
                dve.wait_ge(F["zmean_done"], 1)
                for j in range(4):
                    V.scalar_tensor_tensor(zT[:, j, :], bank[:, 4, 0:NT], -1.0 / CB, zT[:, j, :],
                                           ALU.mult, ALU.add).then_inc(F["z_centered"], 1)
                for j in range(4):
                    dve.wait_ge(F["ymean_done"], j + 1)
                    V.scalar_tensor_tensor(yT[:, j, :], bank[:, j, 0:NT], -1.0 / HD, yT[:, j, :],
                                           ALU.mult, ALU.add).then_inc(F["y_centered"], 1)
                dve.wait_ge(F["zvar_done"], 1)
                V.tensor_scalar(zvar, bank[:, 5, 0:NT], 1.0 / CB, LN_EPS, ALU.mult, ALU.add)\
                    .then_inc(F["zvar_ready"], 1)
                dve.wait_ge(F["yvar_done"], 4)
                for j in range(4):
                    V.tensor_scalar(ysq[:, j, :], bank[:, j, 0:NT], 1.0 / HD, GN_EPS, ALU.mult, ALU.add)\
                        .then_inc(F["yvar_ready"], 1)
                dve.wait_ge(F["zroot_ready"], 1)
                link(V.reciprocal(zvar, zvar))
                link(V.tensor_tensor(zT, zT, b2(zvar, 4), ALU.mult))
                for j in range(4):
                    V.tensor_scalar(zT[:, j, :], zT[:, j, :], vecA[:, V_CLW + j:V_CLW + j + 1],
                                    vecA[:, V_CLB + j:V_CLB + j + 1], ALU.mult, ALU.add).then_inc(F["z_affine"], 1)
                dve.wait_ge(F["yroot_ready"], 1)
                link(V.reciprocal(ysq, ysq))
                dve.wait_ge(F["z_sig"], 1)
                V.tensor_tensor(zT, zT, zsq, ALU.mult).then_inc(F["zT_ready"], 1)
                link(V.tensor_tensor(yT, yT, ysq, ALU.mult))
                for j in range(4):
                    last = V.tensor_scalar(yT[:, j, :], yT[:, j, :], vecA[:, V_LW + j:V_LW + j + 1],
                                           vecA[:, V_LB + j:V_LB + j + 1], ALU.mult, ALU.add)
                link(last)
                link(V.tensor_tensor(yT, yT, bonT, ALU.add))
                V.tensor_tensor(yT, yT, gT, ALU.mult).then_inc(F["yT_ready"], 1)
                dve.wait_ge(F["acc_in"], 16 * 5)
                dve.wait_ge(unit_used, UPRE)
                for i, (t0, n) in enumerate(TILES):
                    for hb in range(2):
                        o = acc[0:n, i, 512 * hb:512 * hb + 512]
                        V.tensor_tensor(o, o, bank[0:n, 2 * i + hb, :], ALU.add).then_inc(F["acc_ready"], 1)
                for i, (t0, n) in enumerate(TILES):
                    dve.wait_ge(F["acc_ready"], 2 * i + 2)
                    link(V.tensor_tensor_reduce(out=ysm[0:n, :], in0=acc[0:n, i, :], in1=acc[0:n, i, :], scale=1.0,
                                                scalar=0.0, op0=ALU.mult, op1=ALU.add,
                                                accum_out=small[0:n, 24 + i:25 + i]))
                    V.tensor_scalar(small[0:n, 16 + i:17 + i], small[0:n, 24 + i:25 + i], 1.0 / DM, RMS_EPS,
                                    ALU.mult, ALU.add).then_inc(F["ms_ready"], 1)
                for i, (t0, n) in enumerate(TILES):
                    dve.wait_ge(F["rms_ready"], i + 1)
                    link(V.reciprocal(small[0:n, 28 + i:29 + i], small[0:n, 20 + i:21 + i]))
                    V.tensor_scalar(hp[0:n, i, :].rearrange("t (c p) -> t c p", c=KC),
                                    acc[0:n, i, :].rearrange("t (p c) -> t c p", c=KC),
                                    small[0:n, 28 + i:29 + i], None, ALU.mult).then_inc(F["hp_ready"], 1)
                dve.wait_ge(F["gffn_in"], 16)
                for i, (t0, n) in enumerate(TILES):
                    for hb in range(2):
                        dve.wait_ge(F["h2_turned"], 2 * i + hb + 1)
                        V.tensor_tensor(h2T[:, 4 * hb:4 * hb + 4, t0:t0 + n],
                                        shaped(bank[:, hb, :], 4, P)[:, :, 0:n],
                                        b3(gffn[:, 4 * hb:4 * hb + 4], n), ALU.mult).then_inc(F["h2T_ready"], 1)
                dve.wait_ge(F["logits_done"], 1)
                dve.wait_ge(F["rank_copied"], 1)
                for i, (t0, n) in enumerate(TILES):
                    link(V.tensor_copy(logits[0:n, i, :], bank[0:n, 2, NE * i:NE * i + NE]))
                    link(V.max(out=top[0:n, i, :], in_=logits[0:n, i, :]))
                    V.tensor_scalar(ntop[0:n, i:i + 1], top[0:n, i, 0:1], -1.0, None, ALU.mult)\
                        .then_inc(F["ntop_ready"], 1)
                    link(V.max_index(out=topi[0:n, i, :], in_max=top[0:n, i, :], in_values=logits[0:n, i, :]))
                    link(V.tensor_copy(topf[0:n, i, :], topi[0:n, i, :]))
                for i, (t0, n) in enumerate(TILES):
                    dve.wait_ge(F["eg_ready"], i + 1)
                    link(V.reciprocal(erec[0:n, i:i + 1], esum[0:n, i:i + 1]))
                    link(V.tensor_scalar(eg[0:n, i, :], eg[0:n, i, :], erec[0:n, i:i + 1], None, ALU.mult))
                    link(V.tensor_scalar(mask[0:n, i, :], exp_iota[0:n, :], topf[0:n, i, 0:1], None, ALU.is_equal))
                    link(V.tensor_scalar(gates[0:n, i, :], mask[0:n, i, :], eg[0:n, i, 0:1], None, ALU.mult))
                    for k in range(1, TOPK):
                        link(V.tensor_scalar(hot[0:n, i, :], exp_iota[0:n, :], topf[0:n, i, k:k + 1], None,
                                             ALU.is_equal))
                        V.tensor_tensor(mask[0:n, i, :], mask[0:n, i, :], hot[0:n, i, :], ALU.add)
                        link(V.scalar_tensor_tensor(gates[0:n, i, :], hot[0:n, i, :], eg[0:n, i, k:k + 1],
                                                    gates[0:n, i, :], ALU.mult, ALU.add))
                    last = V.tensor_copy(maskbf[0:n, i, :], mask[0:n, i, :])
                last.then_inc(F["mask_ready"], 1)
                dve.wait_ge(F["rank_done"], 1)
                for i, (t0, n) in enumerate(TILES):
                    link(V.scalar_tensor_tensor(rankm[0:n, i, :], bank[0:n, 3, NE * i:NE * i + NE], 1.0,
                                                mask[0:n, i, :], ALU.add, ALU.mult))
                    V.tensor_scalar(rankm[0:n, i, :], rankm[0:n, i, :], -1.0, None, ALU.add)
                link(V.tensor_copy(cnt, bank[:, 3, NE * 3:NE * 4]))
                link(V.tensor_scalar(extra, cnt, float(C), None, ALU.is_gt))
                for b in range(2, -(-NT // C)):
                    link(V.scalar_tensor_tensor(extra, cnt, float(C * b), extra, ALU.is_gt, ALU.add))
                link(V.tensor_copy(incA, extra))
                src, dst = incA, incB
                for d in (1, 2, 4, 8, 16):
                    V.tensor_copy(dst[:, 0:d], src[:, 0:d])
                    link(V.tensor_tensor(dst[:, d:NE], src[:, d:NE], src[:, 0:NE - d], ALU.add))
                    src, dst = dst, src
                link(V.tensor_tensor(exc, src, extra, ALU.subtract))
                link(V.tensor_scalar(selt, exc, rowf, None, ALU.is_le))
                link(V.scalar_tensor_tensor(sel, src, rowf, selt, ALU.is_gt, ALU.mult))
                link(V.tensor_tensor_reduce(out=selt, in0=sel, in1=exp_iota, scale=1.0, scalar=0.0, op0=ALU.mult,
                                            op1=ALU.add, accum_out=ovf[:, 0:1]))
                link(V.tensor_tensor_reduce(out=selt, in0=sel, in1=exc, scale=1.0, scalar=0.0, op0=ALU.mult,
                                            op1=ALU.add, accum_out=ovf[:, 1:2]))
                link(V.tensor_tensor_reduce(out=selt, in0=sel, in1=sel, scale=1.0, scalar=0.0, op0=ALU.mult,
                                            op1=ALU.add, accum_out=ovf[:, 2:3]))
                link(V.tensor_tensor(ovf[:, 1:2], rowf, ovf[:, 1:2], ALU.subtract))
                link(V.tensor_scalar(ovf[:, 1:2], ovf[:, 1:2], 1.0, float(C), ALU.add, ALU.mult))
                link(V.tensor_scalar(ovf[:, 3:4], ovf[:, 2:3], -8192.0, 8192.0, ALU.mult, ALU.add))
                link(V.tensor_tensor(ovf[:, 1:2], ovf[:, 1:2], ovf[:, 3:4], ALU.add))
                V.tensor_scalar(dg[0:NOVER, 0, :], ident[0:NOVER, 0:NOVER], ovf[0:NOVER, 0:1], None, ALU.mult)
                V.tensor_scalar(dg[0:NOVER, 1, :], ident[0:NOVER, 0:NOVER], ovf[0:NOVER, 1:2], None, ALU.mult)\
                    .then_inc(F["diag_ready"], 1)
                V.tensor_copy(blocktab[:, 0:NE], exp_iota)
                V.memset(blockbase[:, 0:NE], 0.0)
                V.memset(blockbase[:, NE + NOVER:NBLK], 8192.0)
                V.memset(blocktab[:, NE + NOVER:NBLK], 0)
                V.tensor_copy(blocktab[:, NBLK:NBLK + 1], src[:, NE - 1:NE])
                dve.wait_ge(F["tab_done"], 1)
                V.tensor_copy(blocktab[:, NE:NE + NOVER], bank[:, 2, 0:NOVER])
                V.tensor_copy(blockbase[:, NE:NE + NOVER], bank[:, 2, NOVER:2 * NOVER]).then_inc(F["tab_ready"], 1)
                dve.wait_ge(F["tab_ready"], 1)

                def experts_of(it):
                    return [dve.value_load(blocktab[0:1, bass.ds(it * 2 + h, 1)], min_val=0, max_val=NE - 1)
                            for h in range(2)]

                def make_p(it, es, stepped):
                    for h in range(2):
                        stepped(V.tensor_scalar(rk[:, 3 * h:3 * h + 3], rankm[:, :, bass.ds(es[h], 1)],
                                                blockbase[:, bass.ds(it * 2 + h, 1)], None, ALU.subtract))
                        for i, (t0, n) in enumerate(TILES):
                            last = V.tensor_scalar(Pm[0:n, i, C * h:C * h + C], slot_iota[0:n, :],
                                                   rk[0:n, 3 * h + i:3 * h + i + 1], None, ALU.is_equal)
                    last.then_inc(F["p_ready"], 1)

                def make_pg(es):
                    for h in range(2):
                        for i, (t0, n) in enumerate(TILES):
                            last = V.tensor_scalar(Pg[0:n, i, C * h:C * h + C], slot_iota[0:n, :],
                                                   rk[0:n, 3 * h + i:3 * h + i + 1],
                                                   gates[0:n, i, bass.ds(es[h], 1)], ALU.is_equal, ALU.mult)
                    last.then_inc(F["pg_ready"], 1)

                def take_x(it, h):
                    dve.wait_ge(F["xg_done"], it * 2 + (h + 1))
                    V.tensor_tensor(xT[:, h], shaped(bank[:, 7 * h, :], KC, C), b3(gffn, C), ALU.mult)\
                        .then_inc(F["x_ready"], 1)

                STEPS = 6

                def body(it):
                    n = [0]

                    def stepped(ins):
                        n[0] += 1
                        ins.then_inc(F["mstep"], 1)
                        dve.wait_ge(F["mstep"], it * STEPS + (2 + n[0]))

                    es, es_next = experts_of(it), experts_of(it + 1)

                    def bias(w, h):
                        return biasT[:, w, :, bass.ds(es[h], 1)].broadcast_to([P, KC, C])

                    def gate(h, through):
                        used_through(dve, it, through)
                        g = V.tensor_tensor(t1, shaped(bank[:, 1, :], KC, C), bias(0, h), ALU.add)
                        g.then_inc(F["g_read"], 1)
                        dve.wait_ge(F["g_read"], it * 2 + (h + 2))
                        V.tensor_scalar(t1, t1, LIMIT, None, ALU.min).then_inc(F["t1_ready"], 1)

                    def up(h, through):
                        used_through(dve, it, through)
                        V.tensor_tensor(u1, shaped(bank[:, 2, :], KC, C), bias(1, h), ALU.add)\
                            .then_inc(F["u_read"], 1)
                        dve.wait_ge(F["u_read"], it * 2 + (h + 2))
                        stepped(V.tensor_scalar(u1, u1, LIMIT, -LIMIT, ALU.min, ALU.max))
                        stepped(V.scalar_tensor_tensor(u1, u1, 1.0, t1, ALU.add, ALU.mult))
                        dve.wait_ge(F["sg_ready"], it * 2 + (h + 1))
                        V.tensor_tensor(act_[:, h], u1, sg, ALU.mult).then_inc(F["act_ready"], 1)

                    def down(h, through):
                        used_through(dve, it, through)
                        if h == 0:
                            dve.wait_ge(F["ytr_done"], it * 2 + 1)
                        V.tensor_tensor(yTm[:, :, C * h:C * h + C], shaped(bank[:, 3, :], KC, C), bias(2, h),
                                        ALU.add).then_inc(F["ytm_ready"], 1)
                        dve.wait_ge(F["ytm_ready"], it * 2 + (h + 1))
                        dve.sem_inc(F["d_read"], 1)

                    gate(0, 4)
                    dve.wait_ge(F["xg_done"], it * 2 + 2)
                    make_p(it + 1, es_next, stepped)
                    up(0, 8)
                    gate(1, 12)
                    down(0, 16)
                    up(1, 20)
                    take_x(it + 1, 0)
                    take_x(it + 1, 1)
                    dve.wait_ge(F["pgt_done"], it + 1)
                    make_pg(es_next)
                    down(1, 24)
                    for hb in range(2):
                        for i, (t0, m) in enumerate(TILES):
                            k = 3 * hb + i
                            dve.wait_ge(F["cmb_done"], it * 6 + (k + 2))
                            o = acc[0:m, i, 512 * hb:512 * hb + 512]
                            V.tensor_tensor(o, o, bank[0:m, 6 + k % 2, :], ALU.add).then_inc(F["cmb_read"], 1)
                    assert n[0] == STEPS

                for nm, k in (("g_read", 1), ("u_read", 1), ("d_read", 1), ("cmb_read", 2), ("ysm_ready", 1)):
                    dve.sem_inc(F[nm], k)
                first = [0]

                def stepped0(ins):
                    first[0] += 1
                    ins.then_inc(F["mstep"], 1)
                    dve.wait_ge(F["mstep"], first[0])
                dve.wait_ge(F["bias_ready"], 2)
                es0 = experts_of(0)
                make_p(0, es0, stepped0)
                make_pg(es0)
                take_x(0, 0)
                take_x(0, 1)
                with dve.Fori(0, PAIRS) as it:
                    body(it)
                over_pairs(dve, body)
                dve.wait_ge(F["gfin_in"], 16)
                for i, (t0, n) in enumerate(TILES):
                    link(V.tensor_tensor_reduce(out=hp[0:n, i, :], in0=acc[0:n, i, :], in1=acc[0:n, i, :], scale=1.0,
                                                scalar=0.0, op0=ALU.mult, op1=ALU.add,
                                                accum_out=small[0:n, 40 + i:41 + i]))
                    V.tensor_scalar(small[0:n, 32 + i:33 + i], small[0:n, 40 + i:41 + i], 1.0 / DM, RMS_EPS,
                                    ALU.mult, ALU.add).then_inc(F["fin_ms"], 1)
                for i, (t0, n) in enumerate(TILES):
                    dve.wait_ge(F["fin_root"], i + 1)
                    link(V.reciprocal(small[0:n, 44 + i:45 + i], small[0:n, 36 + i:37 + i]))
                    V.scalar_tensor_tensor(acc[0:n, i, :], acc[0:n, i, :], small[0:n, 44 + i:45 + i], gfin[0:n, :],
                                           ALU.mult, ALU.mult).then_inc(F["fin_ready"], 1)


_INS = ['x_prompt', 'x_sample', 'state_wkv', 'state_shift', 'state_conv', 'meta_tokens', 'norm_mix', 'w_in',
        'tshift_mu', 'decay_w0', 'decay_w2', 'iclr_a0', 'iclr_a2', 'gate_g2', 'k_k', 'k_a', 'r_k', 'lnx_w', 'lnx_b',
        'glu_b', 'dw_weight', 'dw_bias', 'conv_ln_w', 'conv_ln_b', 'w_out', 'norm_ffn', 'w_router', 'b_router',
        'w_gate', 'b_gate', 'w_up', 'b_up', 'w_down', 'b_down', 'norm_final']
_OUTS = [("y_prompt", (1, SEQ, DM)), ("y_sample", (NSEQ, SL, DM)), ("wkv_prompt", (1, 1, NH, HD, HD)),
         ("shift_prompt", (1, 1, SHC)), ("conv_prompt", (1, 1, HIST, CB)), ("wkv_sample", (1, NSEQ, NH, HD, HD)),
         ("shift_sample", (1, NSEQ, SHC)), ("conv_sample", (1, NSEQ, HIST, CB))]


def kernel(**inputs):
    import numpy as _np
    import concourse.bacc as _bacc
    from concourse.bass_utils import run_bass_kernel_spmd as _run

    nc = _bacc.Bacc("TRN2", target_bir_lowering=False, num_devices=1)
    arrays, aps = {}, {}
    for name in _INS:
        v = _np.ascontiguousarray(inputs[name])
        arrays[f"in_{name}_dram"] = v
        aps[name] = nc.dram_tensor(f"in_{name}_dram", v.shape, mybir.dt.from_np(v.dtype), kind="ExternalInput").ap()
    for name, shape in _OUTS:
        aps[name] = nc.dram_tensor(f"out_{name}_dram", shape, F32, kind="ExternalOutput").ap()
    build(nc, aps)
    r = _run(nc, [arrays], core_ids=[0])
    return tuple(r.results[0][f"out_{name}_dram"] for name, _ in _OUTS)
```

```python
from contextlib import ExitStack

import concourse.bass as bass
from concourse import mybir

ALU = mybir.AluOpType
ACT = mybir.ActivationFunctionType
AX = mybir.AxisListType
F32 = mybir.dt.float32
BF16 = mybir.dt.bfloat16
I32 = mybir.dt.int32
U32 = mybir.dt.uint32

P = 128
DM = 1024
KC = DM // P
META, SEQ = 16, 256
NPR = META + SEQ
NSEQ, SL = 8, 8
NSA = NSEQ * SL
NT = NPR + NSA
TILES = [(0, 128), (128, 128), (256, NT - 256)]
CA, CB = 512, 512
NH, HD = 8, 64
NPAIR = NH // 2
NBA = 14
SHC = NBA * P
CW = 31
HIST = CW - 1
NE, TOPK = 32, 4
LIMIT, ALPHA = 7.0, 1.702
RMS_EPS, LN_EPS, GN_EPS = 1e-5, 1e-5, 64e-5
HALF_DECAY = 0.6065306597126334

UNIT = 2048
RING = 8
UNITS_IN = 11
UNITS_OUT = 4
UPRE = UNITS_IN + UNITS_OUT
UPAIR = 24
C = 64
NOVER = 20
NBLK = NE + NOVER + 2
PAIRS, OPAIRS = NE // 2, NOVER // 2
OUT_ORDER = [2, 3, 0, 1]
IN_ORDER = [7, 9, 8, 10, 6, 2, 3, 0, 1, 4, 5]
CHUNKS = [0, 64, 128, 192, 256, NPR]
LEVELS = [6, 6, 6, 6, 4, 3]
EXTP = HIST + NPR
EXTS = HIST + SL



def build(nc, a):
    ctx = ExitStack()
    with ctx:
        stage_sems = []

        def sem(name):
            return ctx.enter_context(nc.semaphore(name))

        def lsem(name):
            stage_sems.append(nc.alloc_semaphore(name))
            return stage_sems[-1]

        def next_stage():
            nc.clear_and_free_semaphores(list(stage_sems))
            stage_sems.clear()
            nc.all_engine_barrier()

        bank = ctx.enter_context(nc.psum_tensor("bank", [P, 8, 512], F32))
        ring = ctx.enter_context(nc.sbuf_tensor("ring", [P, RING, UNIT], F32))
        arena_words = 36800
        arena = ctx.enter_context(nc.sbuf_tensor("arena", [P, arena_words], F32))
        cursor = [0]

        def shaped(v, *shape):
            if len(shape) == 2:
                return v.rearrange("p (a b) -> p a b", b=shape[1])
            if len(shape) == 3:
                return v.rearrange("p (a b c) -> p a b c", b=shape[1], c=shape[2])
            return v

        def take(*shape, dt=F32):
            n = 1
            for d in shape:
                n *= d
            words = (n + 1) // 2 if dt == BF16 else n
            v = arena[:, cursor[0]:cursor[0] + words]
            cursor[0] += words
            assert cursor[0] <= arena_words, (cursor[0], arena_words)
            if dt != F32:
                v = v.bitcast(dt)
            return shaped(v, *shape)

        def b3(ap, n):
            return ap.unsqueeze(2).broadcast_to([ap.shape[0], ap.shape[1], n])

        def b2(ap, n):
            return ap.unsqueeze(1).broadcast_to([ap.shape[0], n, ap.shape[1]])

        ident = take(P)
        ones = take(P)
        headones = take(P)
        strict = take(2, C)
        incl = take(2, C)
        identc = take(C)
        level = take(6, C)
        seqrow = take(NSEQ)
        row16 = take(2)
        rowf = take(1)
        tribf = take(P, dt=BF16)
        onesbf = take(P, dt=BF16)
        vecA = take(80)
        vecW = take(CW * 4)
        vecS = take(NSEQ * NBA)
        slot_iota = take(C)
        exp_iota = take(NE)
        bias3 = take(3, DM, dt=BF16)
        expert_row = take(NE)
        gffn = take(KC)
        small = take(64)
        rankm = take(3, NE)
        gates = take(3, NE)
        blockbase = take(NBLK)
        blocktab = take(NBLK + 2, dt=I32)
        Zc = take(NPAIR, HD)
        ZBD = take(NPAIR, P)
        mixer_start = cursor[0]
        rT, kT, vT, ldT, kkT, bT, gT, bonT, yT, zT = [take(4, NT) for _ in range(10)]
        zsBD = take(NSEQ * NPAIR, P)
        mixer_end = cursor[0]

        V_NORM, V_MU, V_W0, V_A0, V_KK, V_KA, V_RK, V_GLU, V_DWB, V_CLW, V_CLB, V_LW, V_LB, V_OMKA = \
            0, 8, 22, 26, 30, 34, 38, 42, 50, 54, 58, 62, 66, 70
        NVEC = 70

        unit_landed = [sem(f"unit_landed{i}") for i in range(RING)]
        unit_used = sem("unit_used")
        out_stored = sem("out_stored")
        stores = [0]

        def slot(t, n):
            return ring[:, t % RING, :].rearrange("p (c n) -> p c n", n=n)

        def load_unit(sp, t):
            if t >= RING:
                sp.wait_ge(unit_used, t - RING + 1)
            if t < UNITS_IN:
                n = IN_ORDER[t]
                src = a["w_in"][0].rearrange("(c p) n -> p c n", p=P)[:, :, n * 256:(n + 1) * 256]
                sp.dma_start(slot(t, 256), src).then_inc(unit_landed[t % RING], 16)
            else:
                u = OUT_ORDER[t - UNITS_IN]
                src = a["w_out"][0].rearrange("(c p) n -> p c n", p=P)[:, 2 * u:2 * u + 2, :]
                sp.dma_start(slot(t, DM), src).then_inc(unit_landed[t % RING], 16)

        def wait_unit(eng, t):
            eng.wait_ge(unit_landed[t % RING], 16 * (t // RING + 1))

        def diag(ap, i):
            return ap[64 * i:64 * i + 64, :, 64 * i:64 * i + 64]

        def half(ap, i):
            return ap[64 * i:64 * i + 64]

        def chain(eng, s):
            n = [0]

            def link(ins):
                n[0] += 1
                ins.then_inc(s, 1)
                eng.wait_ge(s, n[0])
            return link

        cursor[0] = mixer_end
        xt = take(3, DM)
        hT = take(KC, NT)
        ext = take(4, EXTP + NSEQ * EXTS)
        edge = take(2, NPR + 1 + NSEQ * (SL + 1))
        diff = take(2, NT)
        uval = take(2, NT)
        usig = take(2, NT)
        uflat = take(4, NSA)
        tmpA = take(4, NT)
        lastc = take(NBA * (1 + NSEQ))
        loraw = take(2, CA)
        s0c = shaped(xt.rearrange("p a b -> p (a b)")[:, 2 * CB:2 * CB + NSEQ * NPAIR * HD], NSEQ * NPAIR, HD)
        vrow = shaped(tmpA.rearrange("p a b -> p (a b)")[:, 0:384], 3, P)
        cbuf = shaped(zT.rearrange("p a b -> p (a b)")[:, 0:1024], 2, CB)
        junk = shaped(gT.rearrange("p a b -> p (a b)")[:, 0:DM])
        yi = yT.rearrange("p a b -> p (a b)")
        icol, irow, ixor, itmp, rowm = [yi[:, P * i:P * i + P].bitcast(I32) for i in range(5)]
        geq = shaped(yi[:, 640:640 + 7 * C], 7, C)
        lor_in = bonT[:, 0:2, :]
        lor_tanh, lor_sig = bonT[0:64, 2, :], bonT[:, 3, :]
        lastT = shaped(usig.rearrange("p a b -> p (a b)")[:, 0:P])
        cpT = shaped(xt.rearrange("p a b -> p (a b)")[:, 0:CB])
        csT = shaped(xt.rearrange("p a b -> p (a b)")[:, CB:2 * CB])

        def ext_prompt(j, lo, n):
            return ext[:, j, lo:lo + n]

        def ext_sample(j, lo, n):
            return ext[:, j, EXTP:].rearrange("p (s t) -> p s t", t=EXTS)[:, :, lo:lo + n]

        def edge_prompt(b, lo, n):
            return edge[:, b, lo:lo + n]

        def edge_sample(b, lo, n):
            return edge[:, b, NPR + 1:].rearrange("p (s t) -> p s t", t=SL + 1)[:, :, lo:lo + n]

        def by_seq(ap):
            return ap[:, NPR:NT].rearrange("p (s t) -> p s t", t=SL)

        x_in = lsem("x_in")
        rows_in = lsem("rows_in")
        hist_in = lsem("hist_in")
        s0_in = lsem("s0_in")
        lora_in = lsem("lora_in")
        iota_done = lsem("iota_done")
        consts_done = lsem("consts_done")
        dve_step = lsem("dve_step")
        rows_turned = lsem("rows_turned")
        vec_ready = lsem("vec_ready")
        hist_turned = lsem("hist_turned")
        hist_ready = lsem("hist_ready")
        ms_ready = lsem("ms_ready")
        rms_ready = lsem("rms_ready")
        xn_ready = lsem("xn_ready")
        x_turned = lsem("x_turned")
        hT_ready = lsem("hT_ready")
        proj_first = lsem("proj_first")
        proj_read = lsem("proj_read")
        uv_ready = lsem("uv_ready")
        u_ready = lsem("u_ready")
        edge_ready = lsem("edge_ready")
        diff_ready = lsem("diff_ready")
        last_taken = lsem("last_taken")
        shifted = lsem("shifted")
        lora_act = lsem("lora_act")
        lora_w = lsem("lora_w")
        lora_a = lsem("lora_a")
        lora_g = lsem("lora_g")
        decay_sig = lsem("decay_sig")
        rate_sig = lsem("rate_sig")
        gate_read = lsem("gate_read")
        kk_sq = lsem("kk_sq")
        kk_sum = lsem("kk_sum")
        kk_root = lsem("kk_root")
        rk_ready = lsem("rk_ready")
        rk_sum = lsem("rk_sum")
        last_turned = lsem("last_turned")
        last_copied = lsem("last_copied")
        cout_turned = lsem("cout_turned")
        cout_copied = lsem("cout_copied")
        s0_turned = lsem("s0_turned")
        s0_read = lsem("s0_read")
        pool_step = lsem("pool_step")
        conv_step = lsem("conv_step")

        order = [2 * n + b for n in IN_ORDER for b in range(2)]
        a_index = {cb: i for i, cb in enumerate(cb for cb in order if cb < NBA)}
        u_index = {cb: i for i, cb in enumerate(cb for cb in order if cb >= NBA + 4)}

        def wait_proj(eng, n):
            if n % 2:
                eng.wait_ge(unit_used, n // 2 + 1)
            else:
                eng.wait_ge(proj_first, n // 2 + 1)

        with nc.Block() as block:
            @block.sync
            def _(sp):
                sp.dma_start(xt[0:META, 0, :], a["meta_tokens"]).then_inc(x_in, 16)
                sp.dma_start(xt[META:P, 0, :], a["x_prompt"][0, 0:P - META, :]).then_inc(x_in, 16)
                sp.dma_start(xt[:, 1, :], a["x_prompt"][0, P - META:2 * P - META, :]).then_inc(x_in, 16)
                sp.dma_start(xt[0:META, 2, :], a["x_prompt"][0, 2 * P - META:SEQ, :]).then_inc(x_in, 16)
                sp.dma_start(xt[META:META + NSA, 2, :],
                             a["x_sample"].rearrange("s t d -> (s t) d")).then_inc(x_in, 16)
                for t in range(RING):
                    load_unit(sp, t)
                sp.wait_ge(hT_ready, 6)
                sp.dma_start(s0c[:, :, :].rearrange("p (s j) k -> p s j k", j=NPAIR),
                             a["state_wkv"][0].rearrange("s (j h) v k -> (h v) s j k", h=2)) \
                    .then_inc(s0_in, 16)
                sp.dma_start(a["conv_sample"][0][:, 0:HIST - SL, :],
                             a["state_conv"][0][:, SL:HIST, :]).then_inc(out_stored, 16)
                for t in range(RING, UPRE):
                    load_unit(sp, t)
                sp.wait_ge(last_copied, 1)
                sp.dma_start(a["shift_prompt"][0, 0].rearrange("(b p) -> b p", p=P),
                             lastT[0:NBA, :]).then_inc(out_stored, 16)
                sp.dma_start(a["shift_sample"][0].rearrange("s (b p) -> (s b) p", p=P),
                             lastT[NBA:NBA * (1 + NSEQ), :]).then_inc(out_stored, 16)
                sp.wait_ge(cout_copied, 2)
                sp.dma_start(a["conv_prompt"][0, 0], cpT[0:HIST, :]).then_inc(out_stored, 16)
                for s in range(NSEQ):
                    sp.dma_start(a["conv_sample"][0, s, HIST - SL:HIST, :],
                                 csT[SL * s:SL * s + SL, :]).then_inc(out_stored, 16)
                sp.wait_ge(out_stored, 16 * (4 + NSEQ))

            stores[0] = 4 + NSEQ

            @block.gpsimd
            def _(pool):
                nc.gpsimd.iota(icol, [[1, P]], base=0, channel_multiplier=0).then_inc(iota_done, 1)
                nc.gpsimd.iota(irow, [[0, P]], base=0, channel_multiplier=1).then_inc(iota_done, 1)
                link = chain(pool, pool_step)
                nc.gpsimd.memset(edge[:, :, 0:1], 0.0)
                nc.gpsimd.memset(ext[:, :, 0:HIST], 0.0)
                link(nc.gpsimd.memset(zsBD[:, :, :], 0.0))
                n_u = 0
                pool.wait_ge(hist_ready, 8)
                for n, cb in enumerate(order):
                    if cb >= NBA + 4:
                        j = cb - NBA - 4
                        pool.wait_ge(uv_ready, n + 1)
                        nc.gpsimd.tensor_tensor(ext_prompt(j, HIST, NPR), uval[:, j % 2, 0:NPR],
                                                usig[:, j % 2, 0:NPR], ALU.mult)
                        nc.gpsimd.tensor_tensor(ext_sample(j, HIST, SL), by_seq(uval[:, j % 2, :]),
                                                by_seq(usig[:, j % 2, :]), ALU.mult)
                        nc.gpsimd.tensor_tensor(uflat[:, j, :], uval[:, j % 2, NPR:NT],
                                                usig[:, j % 2, NPR:NT], ALU.mult).then_inc(u_ready, 1)
                        n_u += 1
                    elif cb < NBA:
                        i = a_index[cb]
                        b = i % 2
                        pool.wait_ge(edge_ready, i + 1)
                        if i >= 2:
                            pool.wait_ge(shifted, i - 1)
                        nc.gpsimd.tensor_tensor(diff[:, b, 0:NPR], edge_prompt(b, 0, NPR),
                                                edge_prompt(b, 1, NPR), ALU.subtract)
                        nc.gpsimd.tensor_tensor(by_seq(diff[:, b, :]), edge_sample(b, 0, SL),
                                                edge_sample(b, 1, SL), ALU.subtract).then_inc(diff_ready, 1)
                        nc.gpsimd.tensor_copy(lastc[:, cb:cb + 1], edge_prompt(b, NPR, 1))
                        nc.gpsimd.tensor_copy(lastc[:, NBA:].rearrange("p (s b) -> p s b", b=NBA)[:, :, cb:cb + 1],
                                              edge_sample(b, SL, 1)).then_inc(last_taken, 1)

            @block.scalar
            def _(act):
                at = 0
                for name, n in [("norm_mix", 8), ("tshift_mu", 14), ("decay_w0", 4), ("iclr_a0", 4), ("k_k", 4),
                                ("k_a", 4), ("r_k", 4), ("glu_b", 8), ("dw_bias", 4), ("conv_ln_w", 4),
                                ("conv_ln_b", 4), ("lnx_w", 4), ("lnx_b", 4)]:
                    src = a[name][0]
                    if name == "r_k":
                        src = src.rearrange("h k -> (h k)")
                    act.dma_start(vrow[at:at + n, 0, :], src.rearrange("(c p) -> c p", p=P)).then_inc(rows_in, 16)
                    at += n
                act.dma_start(vrow[0:CW * 4, 1, :],
                              a["dw_weight"][0].rearrange("t (c p) -> (t c) p", p=P)).then_inc(rows_in, 16)
                act.dma_start(vrow[0:NSEQ * NBA, 2, :],
                              a["state_shift"][0].rearrange("s (c p) -> (s c) p", p=P)).then_inc(rows_in, 16)
                act.dma_start(cbuf[0:120, :, :],
                              a["state_conv"][0].rearrange("(g s) t c -> (s t) g c", g=2)).then_inc(hist_in, 16)
                act.dma_start(loraw[0:64, 0, :], a["decay_w2"][0]).then_inc(lora_in, 16)
                act.dma_start(loraw[64:128, 0, :], a["iclr_a2"][0]).then_inc(lora_in, 16)
                act.dma_start(loraw[:, 1, :], a["gate_g2"][0]).then_inc(lora_in, 16)
                act.wait_ge(rows_turned, 1)
                nc.scalar.copy(vecA[:, 0:NVEC], bank[:, 7, 0:NVEC])
                nc.scalar.copy(vecW[:, :], bank[:, 7, P:P + CW * 4])
                nc.scalar.copy(vecS[:, :], bank[:, 7, 2 * P:2 * P + NSEQ * NBA]).then_inc(vec_ready, 1)
                for g in range(2):
                    act.wait_ge(hist_turned, g + 1)
                    for j in range(4):
                        nc.scalar.copy(ext_sample(j, 0, HIST)[:, 4 * g:4 * g + 4, :],
                                       bank[:, 5 + g, j * 120:j * 120 + 120]
                                       .rearrange("p (s t) -> p s t", t=HIST)).then_inc(hist_ready, 1)
                for i, (t0, n) in enumerate(TILES):
                    act.wait_ge(ms_ready, i + 1)
                    nc.scalar.activation(small[0:n, 4 + i:5 + i], small[0:n, i:i + 1], ACT.Sqrt)\
                        .then_inc(rms_ready, 1)
                for n, cb in enumerate(order):
                    wait_proj(act, n)
                    src = bank[:, n % 4, 0:NT]
                    if cb >= NBA:
                        j = cb - NBA
                        if j < 4:
                            if j >= 2:
                                act.wait_ge(u_ready, j - 1)
                            nc.scalar.activation(uval[:, j % 2, :], src, ACT.Identity,
                                                 bias=vecA[:, V_GLU + j:V_GLU + j + 1]).then_inc(uv_ready, 1)
                        else:
                            if j >= 6:
                                act.wait_ge(u_ready, j - 5)
                            nc.scalar.activation(usig[:, j % 2, :], src, ACT.Sigmoid,
                                                 bias=vecA[:, V_GLU + j:V_GLU + j + 1]).then_inc(uv_ready, 1)
                        act.wait_ge(uv_ready, n + 1)
                    else:
                        i = a_index[cb]
                        b = i % 2
                        if i >= 2:
                            act.wait_ge(shifted, i - 1)
                            act.wait_ge(last_taken, i - 1)
                        nc.scalar.copy(edge_prompt(b, 1, NPR), src[:, 0:NPR])
                        nc.scalar.copy(edge_sample(b, 0, 1),
                                       vecS.rearrange("p (s b) -> p s b", b=NBA)[:, :, cb:cb + 1])
                        nc.scalar.copy(edge_sample(b, 1, SL), by_seq(src)).then_inc(edge_ready, 1)
                        act.wait_ge(edge_ready, i + 1)
                    nc.scalar.sem_inc(proj_read, 1)
                act.wait_ge(shifted, a_index[13] + 1)
                nc.scalar.activation(lor_tanh, lor_in[0:64, 0, :], ACT.Tanh).then_inc(lora_act, 1)
                nc.scalar.activation(lor_sig, lor_in[:, 1, :], ACT.Sigmoid).then_inc(lora_act, 1)
                for j in range(4):
                    act.wait_ge(lora_w, j + 1)
                    nc.scalar.activation(ldT[:, j, :], bank[:, j, 0:NT], ACT.Sigmoid,
                                         bias=vecA[:, V_W0 + j:V_W0 + j + 1]).then_inc(decay_sig, 1)
                for j in range(4):
                    act.wait_ge(lora_a, j + 1)
                    nc.scalar.activation(bT[:, j, :], bank[:, 4 + j, 0:NT], ACT.Sigmoid,
                                         bias=vecA[:, V_A0 + j:V_A0 + j + 1]).then_inc(rate_sig, 1)
                for j in range(4):
                    act.wait_ge(lora_g, j + 1)
                    nc.scalar.copy(gT[:, j, :], bank[:, j, 0:NT]).then_inc(gate_read, 1)
                for j in range(4):
                    act.wait_ge(kk_sum, j + 1)
                    nc.scalar.activation(tmpA[:, j, :], bank[:, 4 + j, 0:NT], ACT.Sqrt).then_inc(kk_root, 1)
                act.wait_ge(last_turned, 1)
                nc.scalar.copy(lastT[0:NBA * (1 + NSEQ), :], bank[0:NBA * (1 + NSEQ), 0, 0:P])\
                    .then_inc(last_copied, 1)
                act.wait_ge(cout_turned, 1)
                nc.scalar.copy(cpT[0:HIST, :], bank[0:HIST, 1, :]).then_inc(cout_copied, 1)
                act.wait_ge(cout_turned, 2)
                nc.scalar.copy(csT[0:NSA, :], bank[0:NSA, 2, :]).then_inc(cout_copied, 1)
                for g in range(8):
                    act.wait_ge(s0_turned, g + 1)
                    src = shaped(bank[0:64, g % 2, :], 4, P)
                    for i in range(2):
                        nc.scalar.copy(zsBD[64 * i:64 * i + 64, 4 * g:4 * g + 4, 64 * i:64 * i + 64],
                                       src[:, :, 64 * i:64 * i + 64]).then_inc(s0_read, 1)

            @block.tensor
            def _(pe):
                pe.wait_ge(consts_done, 1)
                pe.wait_ge(rows_in, 16 * 15)
                nc.tensor.transpose(bank[:, 7, 0:NVEC], vrow[0:NVEC, 0, :], ident[0:NVEC, 0:NVEC])
                nc.tensor.transpose(bank[:, 7, P:P + CW * 4], vrow[0:CW * 4, 1, :], ident[0:CW * 4, 0:CW * 4])
                nc.tensor.transpose(bank[:, 7, 2 * P:2 * P + NSEQ * NBA], vrow[0:NSEQ * NBA, 2, :],
                                    ident[0:NSEQ * NBA, 0:NSEQ * NBA]).then_inc(rows_turned, 1)
                pe.wait_ge(hist_in, 16)
                for g in range(2):
                    for j in range(4):
                        mm = nc.tensor.transpose(bank[:, 5 + g, j * 120:j * 120 + 120],
                                                 cbuf[0:120, g, j * P:j * P + P], ident[0:120, 0:120])
                    mm.then_inc(hist_turned, 1)
                for i, (t0, n) in enumerate(TILES):
                    pe.wait_ge(xn_ready, i + 1)
                    for hb in range(2):
                        if i >= 1:
                            pe.wait_ge(hT_ready, 2 * i - 1 + hb)
                        for c in range(4):
                            mm = nc.tensor.transpose(bank[:, 3 + hb, c * P:c * P + n],
                                                     xt[0:n, i, (4 * hb + c) * P:(4 * hb + c + 1) * P],
                                                     ident[0:n, 0:n])
                        mm.then_inc(x_turned, 1)
                pe.wait_ge(hT_ready, 6)
                for n, cb in enumerate(order):
                    t, b = n // 2, n % 2
                    if b == 0:
                        wait_unit(pe, t)
                    if n >= 4:
                        pe.wait_ge(proj_read, n - 3)
                    w = slot(t, 256)
                    for c in range(KC):
                        mm = nc.tensor.matmul(bank[:, n % 4, 0:NT], w[:, c, b * P:b * P + P], hT[:, c, :],
                                              start=(c == 0), stop=(c == KC - 1))
                    mm.then_inc(unit_used if b else proj_first, 1)
                pe.wait_ge(lora_in, 48)
                pe.wait_ge(lora_act, 2)
                pe.wait_ge(proj_read, 22)
                for j in range(4):
                    nc.tensor.matmul(bank[:, j, 0:NT], loraw[0:64, 0, j * P:j * P + P], lor_tanh,
                                     start=True, stop=True).then_inc(lora_w, 1)
                for j in range(4):
                    nc.tensor.matmul(bank[:, 4 + j, 0:NT], loraw[64:128, 0, j * P:j * P + P], lor_in[64:128, 0, :],
                                     start=True, stop=True).then_inc(lora_a, 1)
                for j in range(4):
                    pe.wait_ge(decay_sig, j + 1)
                    nc.tensor.matmul(bank[:, j, 0:NT], loraw[:, 1, j * P:j * P + P], lor_sig,
                                     start=True, stop=True).then_inc(lora_g, 1)
                for j in range(4):
                    pe.wait_ge(rate_sig, j + 1)
                    pe.wait_ge(kk_sq, 1)
                    nc.tensor.matmul(bank[:, 4 + j, 0:NT], headones, tmpA[:, j, :],
                                     start=True, stop=True).then_inc(kk_sum, 1)
                pe.wait_ge(gate_read, 4)
                pe.wait_ge(last_taken, NBA)
                nc.tensor.transpose(bank[0:NBA * (1 + NSEQ), 0, 0:P], lastc[:, :], ident).then_inc(last_turned, 1)
                for j in range(4):
                    mm = nc.tensor.transpose(bank[0:HIST, 1, j * P:j * P + P], ext_prompt(j, NPR, HIST), ident)
                mm.then_inc(cout_turned, 1)
                for j in range(4):
                    mm = nc.tensor.transpose(bank[0:NSA, 2, j * P:j * P + P], uflat[:, j, :], ident)
                mm.then_inc(cout_turned, 1)
                pe.wait_ge(kk_root, 4)
                pe.wait_ge(rk_ready, 1)
                for j in range(4):
                    nc.tensor.matmul(bank[:, 4 + j, 0:NT], headones, tmpA[:, j, :],
                                     start=True, stop=True).then_inc(rk_sum, 1)
                pe.wait_ge(s0_in, 16)
                pe.wait_ge(last_copied, 1)
                pe.wait_ge(cout_copied, 1)
                for g in range(8):
                    if g >= 2:
                        pe.wait_ge(s0_read, 2 * (g - 1))
                    for q in range(4):
                        mm = nc.tensor.transpose(bank[0:64, g % 2, q * P:q * P + P], s0c[:, 4 * g + q, :], ident)
                    mm.then_inc(s0_turned, 1)

            @block.vector
            def _(dve):
                link = chain(dve, dve_step)
                V = nc.vector
                dve.wait_ge(iota_done, 2)
                link(V.tensor_tensor(ixor, icol, irow, ALU.bitwise_xor))
                V.tensor_scalar(ident, ixor, 0.0, None, ALU.is_equal)
                V.tensor_scalar(headones, ixor, 64.0, None, ALU.is_lt)
                link(V.memset(ones, 1.0))
                V.memset(onesbf, 1.0).then_inc(consts_done, 1)
                V.tensor_tensor(tribf, irow, icol, ALU.is_lt)
                V.tensor_copy(rowf, irow[:, 0:1])
                V.tensor_copy(slot_iota, icol[:, 0:C])
                V.tensor_copy(exp_iota, icol[:, 0:NE])
                link(V.tensor_scalar(rowm, irow, 63, None, ALU.bitwise_and))
                link(V.tensor_scalar(itmp, ixor, 63, None, ALU.bitwise_and))
                for l in range(7):
                    last = V.tensor_scalar(geq[:, l, :], itmp[:, 0:C], float(2 ** l), None, ALU.is_ge)
                V.tensor_tensor(strict[:, 0, :], rowm[:, 0:C], icol[:, 0:C], ALU.is_lt)
                V.tensor_tensor(incl[:, 0, :], rowm[:, 0:C], icol[:, 0:C], ALU.is_le)
                V.tensor_tensor(identc, rowm[:, 0:C], icol[:, 0:C], ALU.is_equal)
                V.tensor_scalar(row16[:, 0:1], rowm[:, 0:1], 16.0, None, ALU.is_lt)
                link(V.memset(row16[:, 1:2], 1.0))
                link(V.tensor_tensor(level[:, :, :], geq[:, 0:6, :], geq[:, 1:7, :], ALU.subtract))
                link(V.tensor_tensor(level[:, :, :], level[:, :, :], b2(strict[:, 0, :], 6), ALU.mult))
                link(V.tensor_scalar(itmp, irow, NE - 1, None, ALU.bitwise_and))
                V.tensor_tensor(expert_row, itmp[:, 0:NE], icol[:, 0:NE], ALU.is_equal)
                link(V.tensor_scalar(geq[:, 3, :], geq[:, 3, :], -1.0, 1.0, ALU.mult, ALU.add))
                V.tensor_tensor(strict[:, 1, :], strict[:, 0, :], geq[:, 3, :], ALU.mult)
                V.tensor_tensor(incl[:, 1, :], incl[:, 0, :], geq[:, 3, :], ALU.mult)
                link(V.tensor_scalar(itmp, rowm, 3, None, ALU.logical_shift_right))
                link(V.tensor_tensor(seqrow, itmp[:, 0:NSEQ], icol[:, 0:NSEQ], ALU.is_equal))
                dve.wait_ge(x_in, 16 * 5)
                for i, (t0, n) in enumerate(TILES):
                    link(V.tensor_tensor_reduce(out=junk[0:n, :], in0=xt[0:n, i, :], in1=xt[0:n, i, :], scale=1.0,
                                                scalar=0.0, op0=ALU.mult, op1=ALU.add,
                                                accum_out=small[0:n, 8 + i:9 + i]))
                    V.tensor_scalar(small[0:n, i:i + 1], small[0:n, 8 + i:9 + i], 1.0 / DM, RMS_EPS,
                                    ALU.mult, ALU.add).then_inc(ms_ready, 1)
                for i, (t0, n) in enumerate(TILES):
                    dve.wait_ge(rms_ready, i + 1)
                    link(V.reciprocal(small[0:n, 12 + i:13 + i], small[0:n, 4 + i:5 + i]))
                    V.tensor_scalar(xt[0:n, i, :], xt[0:n, i, :], small[0:n, 12 + i:13 + i], None,
                                    ALU.mult).then_inc(xn_ready, 1)
                dve.wait_ge(vec_ready, 1)
                for i, (t0, n) in enumerate(TILES):
                    for hb in range(2):
                        dve.wait_ge(x_turned, 2 * i + hb + 1)
                        V.tensor_tensor(hT[:, 4 * hb:4 * hb + 4, t0:t0 + n],
                                        shaped(bank[:, 3 + hb, :], 4, P)[:, :, 0:n],
                                        b3(vecA[:, V_NORM + 4 * hb:V_NORM + 4 * hb + 4], n),
                                        ALU.mult).then_inc(hT_ready, 1)
                link(V.tensor_scalar(vecA[:, V_OMKA:V_OMKA + 4], vecA[:, V_KA:V_KA + 4], -1.0, 1.0,
                                     ALU.mult, ALU.add))

                def conv_steps():
                    for tap in range(CW):
                        for j in range(4):
                            w = vecW[:, 4 * tap + j:4 * tap + j + 1]
                            if tap == 0:
                                dve.wait_ge(u_ready, j + 1)
                                bias = vecA[:, V_DWB + j:V_DWB + j + 1]
                                V.tensor_scalar(zT[:, j, 0:NPR], ext_prompt(j, tap, NPR), w, bias,
                                                ALU.mult, ALU.add)
                                V.tensor_scalar(by_seq(zT[:, j, :]), ext_sample(j, tap, SL), w, bias,
                                                ALU.mult, ALU.add).then_inc(conv_step, 1)
                            else:
                                dve.wait_ge(conv_step, 4 * (tap - 1) + j + 1)
                                V.scalar_tensor_tensor(zT[:, j, 0:NPR], ext_prompt(j, tap, NPR), w,
                                                       zT[:, j, 0:NPR], ALU.mult, ALU.add)
                                V.scalar_tensor_tensor(by_seq(zT[:, j, :]), ext_sample(j, tap, SL), w,
                                                       by_seq(zT[:, j, :]), ALU.mult, ALU.add)\
                                    .then_inc(conv_step, 1)
                            yield

                conv = conv_steps()
                share = -(-CW * 4 // NBA)
                a_order = sorted(a_index, key=a_index.get)
                for i, cb in enumerate(a_order):
                    b = i % 2
                    dst = [rT, kT, vT][cb // 4][:, cb % 4, :] if cb < 12 else lor_in[:, cb - 12, :]
                    mu = vecA[:, V_MU + cb:V_MU + cb + 1]
                    dve.wait_ge(diff_ready, i + 1)
                    V.scalar_tensor_tensor(dst[:, 0:NPR], diff[:, b, 0:NPR], mu, edge_prompt(b, 1, NPR),
                                           ALU.mult, ALU.add)
                    V.scalar_tensor_tensor(by_seq(dst), by_seq(diff[:, b, :]), mu, edge_sample(b, 1, SL),
                                           ALU.mult, ALU.add).then_inc(shifted, 1)
                    for _ in range(share):
                        next(conv, None)
                for _ in conv:
                    pass
                dve.wait_ge(shifted, NBA)
                for j in range(4):
                    last = V.tensor_scalar(kkT[:, j, :], kT[:, j, :], vecA[:, V_KK + j:V_KK + j + 1], None, ALU.mult)
                link(last)
                V.tensor_tensor(tmpA[:, :, :], kkT[:, :, :], kkT[:, :, :], ALU.mult).then_inc(kk_sq, 1)
                dve.wait_ge(decay_sig, 4)
                V.tensor_scalar(ldT[:, :, :], ldT[:, :, :], -HALF_DECAY, None, ALU.mult)
                dve.wait_ge(kk_root, 4)
                link(V.tensor_scalar(tmpA[:, :, :], tmpA[:, :, :], 1e-12, None, ALU.max))
                link(V.reciprocal(tmpA[:, :, :], tmpA[:, :, :]))
                link(V.tensor_tensor(kkT[:, :, :], kkT[:, :, :], tmpA[:, :, :], ALU.mult))
                dve.wait_ge(rate_sig, 4)
                for j in range(4):
                    last = V.tensor_scalar(tmpA[:, j, :], bT[:, j, :], vecA[:, V_KA + j:V_KA + j + 1],
                                           vecA[:, V_OMKA + j:V_OMKA + j + 1], ALU.mult, ALU.add)
                link(last)
                V.tensor_tensor(bT[:, :, :], kkT[:, :, :], bT[:, :, :], ALU.mult)
                link(V.tensor_tensor(kT[:, :, :], kT[:, :, :], tmpA[:, :, :], ALU.mult))
                for j in range(4):
                    last = V.scalar_tensor_tensor(tmpA[:, j, :], rT[:, j, :], vecA[:, V_RK + j:V_RK + j + 1],
                                                  kT[:, j, :], ALU.mult, ALU.mult)
                last.then_inc(rk_ready, 1)
                for j in range(4):
                    dve.wait_ge(rk_sum, j + 1)
                    V.tensor_tensor(bonT[:, j, :], bank[:, 4 + j, 0:NT], vT[:, j, :], ALU.mult)

        next_stage()
        cursor[0] = mixer_end
        bufs = []
        for q in range(2):
            b = {}
            b["X"] = take(NPAIR, P)
            b["A"] = take(NPAIR, C)
            b["n"] = [take(NPAIR, C) for _ in range(2)]
            b["tmp"] = take(NPAIR, C)
            b["nraw"] = take(NPAIR, C)
            b["eL"] = take(NPAIR, C)
            b["KqR"] = take(NPAIR, 2, C)
            b["KtBD"] = take(NPAIR, P)
            b["BtBD"] = take(NPAIR, P)
            b["KqBD"] = take(NPAIR, P)
            b["AkT"] = take(NPAIR, P)
            b["M1T"] = take(NPAIR, C)
            b["M2T"] = take(NPAIR, C)
            b["Ktok"] = take(NPAIR, P)
            b["Btok"] = take(NPAIR, P)
            b["Vtok"] = take(NPAIR, P)
            b["Vc"] = take(NPAIR, C)
            b["Un"] = take(NPAIR, C)
            b["LDtok"] = b["Btok"]
            b["Lc"], b["Lx"] = b["A"], b["n"][1]
            b["emL"], b["eLx"], b["Wc"] = b["tmp"], b["n"][0], b["n"][0]
            b["VBD"] = b["AkT"]
            b["AT"] = b["UnBD"] = b["KtBD"]
            b["E"] = b["BtBD"]
            bufs.append(b)
        flat = arena[:, mixer_start:mixer_start + 6 * 4 * NT]
        Vx = shaped(flat[:, 0:2048], NPAIR, 512)
        Ux = shaped(flat[:, 2048:4096], NPAIR, 512)
        zso = shaped(flat[:, 4096:6144], NPAIR, 512)
        szb = bufs[1]["BtBD"]

        names = ["zeroed", "ld_turned", "ldtok_ready", "cum_done", "lc_ready", "lx_ready", "el_ready", "eml_ready",
                 "elx_ready", "ktbd_ready", "btbd_ready", "vbd_ready", "q_ready", "kqr_ready", "kqbd_ready",
                 "k_turned", "b_turned", "v_turned", "ktok_ready", "btok_ready", "vtok_ready", "vc_ready",
                 "sk_done", "sb_done", "sk_read", "sb_read", "n0_ready", "n0_turned", "nraw_ready", "a0_ready",
                 "at0_ready", "nl_ready", "an_done", "e_ready", "atn_done", "at_ready", "an2_done", "a_ready",
                 "x_ready",
                 "w_done", "wc_ready", "u_done", "un_ready", "unbd_ready", "z_done", "z_ready", "zbd_used",
                 "zbd_ready",
                 "y_done", "y_read", "sz_done", "sz_read", "szt_turned", "szt_ready",
                 "vx_ready", "ux_ready", "zs_done", "zso_ready", "state_sum", "sy_read"]
        S = {n: lsem("scan_" + n) for n in names}

        groups = [(0, 1), (2, 3), (4, 5)]
        plan = {g: [(l, q) for l in range(1, 6) for q in range(2) if l < LEVELS[groups[g][q]]] for g in range(3)}
        number, inner, whole = {}, {}, {}
        for g in range(3):
            for l, q in plan[g]:
                number[(g, l, q)] = len(number)
                if l < LEVELS[groups[g][q]] - 1:
                    inner[(g, l, q)] = len(inner)
                else:
                    whole[groups[g][q]] = len(whole) + 1

        def scan_block(g):
            pair = groups[g]

            def bk(q, i):
                return bank[:, 4 * q + i, :]

            with nc.Block() as block:
                @block.gpsimd
                def _(pool):
                    T = nc.gpsimd
                    if g == 0:
                        for q in range(2):
                            for nm in ("X", "KtBD", "BtBD", "KqBD", "AkT"):
                                T.memset(bufs[q][nm][:, :, :], 0.0)
                        T.memset(Zc[:, :, :], 0.0)
                        T.memset(ZBD[:, :, :], 0.0).then_inc(S["zeroed"], 1)
                        pool.wait_ge(S["zeroed"], 1)
                    for q, c in enumerate(pair):
                        b, ts = bufs[q], CHUNKS[c]
                        for i in range(2):
                            last = T.tensor_copy(diag(b["VBD"], i), half(vT, i)[:, :, ts:ts + C])
                        last.then_inc(S["vbd_ready"], 1)
                    for q, c in enumerate(pair):
                        b, ts = bufs[q], CHUNKS[c]
                        pool.wait_ge(S["eml_ready"], c + 1)
                        for i in range(2):
                            last = T.tensor_tensor(diag(b["BtBD"], i), half(bT, i)[:, :, ts:ts + C],
                                                   half(b["emL"], i), ALU.mult)
                        last.then_inc(S["btbd_ready"], 1)
                        pool.wait_ge(S["q_ready"], c + 1)
                        for i in range(2):
                            last = T.tensor_copy(diag(b["KqBD"], i), half(b["KqR"][:, :, 0, :], i))
                        last.then_inc(S["kqbd_ready"], 1)
                    for q, c in enumerate(pair):
                        b = bufs[q]
                        pool.wait_ge(S["vtok_ready"], c + 1)
                        for i in range(2):
                            last = T.tensor_copy(half(b["Vc"], i), diag(b["Vtok"], i))
                        last.then_inc(S["vc_ready"], 1)
                    for l, q in plan[g]:
                        b, m = bufs[q], number[(g, l, q)]
                        if l == 1:
                            pool.wait_ge(S["nraw_ready"], pair[q] + 1)
                            pool.wait_ge(S["vc_ready"], pair[1] + 1)
                        if l >= 3:
                            pool.wait_ge(S["an_done"], number[(g, l - 2, q)] + 1)
                        T.tensor_tensor(b["n"][l % 2], b["nraw"], b2(level[:, l, :], NPAIR), ALU.mult)\
                            .then_inc(S["nl_ready"], 1)
                    if pair[1] == 5:
                        b = bufs[1]
                        for j in range(NPAIR):
                            T.tensor_tensor(shaped(Vx[:, j, :], NSEQ, HD), b2(b["Vc"][:, j, :], NSEQ),
                                            b3(seqrow, HD), ALU.mult).then_inc(S["vx_ready"], 1)

                @block.scalar
                def _(act):
                    A = nc.scalar
                    for q, c in enumerate(pair):
                        b = bufs[q]
                        act.wait_ge(S["ld_turned"], c + 1)
                        A.copy(b["LDtok"].rearrange("p j c -> p (j c)")[0:C, :], bk(q, 0)[0:C, :])\
                            .then_inc(S["ldtok_ready"], 1)
                        act.wait_ge(S["cum_done"], c + 1)
                        A.copy(b["Lc"], shaped(bk(q, 1)[:, 0:NPAIR * C], NPAIR, C)).then_inc(S["lc_ready"], 1)
                        act.wait_ge(S["lc_ready"], c + 1)
                        A.activation(b["emL"], b["Lc"], ACT.Exp, scale=-1.0).then_inc(S["eml_ready"], 1)
                        A.activation(b["eL"], b["Lc"], ACT.Exp).then_inc(S["el_ready"], 1)
                        act.wait_ge(S["lx_ready"], c + 1)
                        A.activation(b["eLx"], b["Lx"], ACT.Exp).then_inc(S["elx_ready"], 1)
                    for q, c in enumerate(pair):
                        b = bufs[q]
                        act.wait_ge(S["v_turned"], c + 1)
                        A.copy(b["Vtok"].rearrange("p j c -> p (j c)"), bk(q, 0)).then_inc(S["vtok_ready"], 1)
                        act.wait_ge(S["k_turned"], c + 1)
                        own = row16[:, 0:1] if c == 4 else row16[:, 1:2]
                        A.activation(b["Ktok"].rearrange("p j c -> p (j c)"), bk(q, 2), ACT.Identity, scale=own)\
                            .then_inc(S["ktok_ready"], 1)
                    for l, q in plan[g]:
                        b, m = bufs[q], number[(g, l, q)]
                        if (g, l, q) in inner:
                            act.wait_ge(S["atn_done"], inner[(g, l, q)] + 1)
                            src = shaped(bk(q, 2)[0:C, :], NPAIR, P)
                            for i in range(2):
                                last = A.copy(diag(b["AT"], i), src[:, :, 64 * i:64 * i + 64])
                            last.then_inc(S["at_ready"], 1)
                            act.wait_ge(S["an2_done"], m + 1)
                            A.copy(b["A"], shaped(bk(q, 1)[:, 0:NPAIR * C], NPAIR, C)).then_inc(S["a_ready"], 1)
                        else:
                            act.wait_ge(S["an2_done"], m + 1)
                            for i in range(2):
                                last = A.copy(diag(b["X"], i), half(shaped(bk(q, 1)[:, 0:NPAIR * C], NPAIR, C), i))
                            last.then_inc(S["x_ready"], 1)
                    for q, c in enumerate(pair):
                        b, ts = bufs[q], CHUNKS[c]
                        if c == 5:
                            act.wait_ge(S["sz_done"], 1)
                            A.copy(szb.rearrange("p j c -> p (j c)"), bk(q, 3)).then_inc(S["sz_read"], 1)
                            act.wait_ge(S["szt_turned"], 1)
                            src = shaped(bk(q, 0)[0:C, :], NPAIR, P)
                            for i in range(2):
                                last = A.copy(half(b["tmp"], i), src[:, :, 64 * i:64 * i + 64])
                            last.then_inc(S["szt_ready"], 1)
                        act.wait_ge(S["u_done"], c + 1)
                        u = shaped(bk(q, 2 if c == 5 else 1)[:, 0:NPAIR * C], NPAIR, C)
                        A.activation(b["Un"], u, ACT.Identity, scale=-1.0).then_inc(S["un_ready"], 1)
                        for i in range(2):
                            last = A.activation(diag(b["UnBD"], i), half(u, i), ACT.Identity, scale=-1.0)
                        last.then_inc(S["unbd_ready"], 1)
                        done = ([(q - 1, c - 1)] if q == 1 and c - 1 < 5 else []) + ([(q, c)] if q == 1 and c < 5 else [])
                        for yq, yc in done:
                            n_own = min(C, NPR - CHUNKS[yc])
                            act.wait_ge(S["y_done"], yc + 1)
                            A.copy(yT[:, :, CHUNKS[yc]:CHUNKS[yc] + n_own],
                                   shaped(bk(yq, 3)[:, 0:NPAIR * C], NPAIR, C)[:, :, 0:n_own])\
                                .then_inc(S["y_read"], 1)

                @block.tensor
                def _(pe):
                    M = nc.tensor
                    for q, c in enumerate(pair):
                        b, ts = bufs[q], CHUNKS[c]
                        for j in range(NPAIR):
                            mm = M.transpose(bk(q, 0)[0:C, j * P:j * P + P], ldT[:, j, ts:ts + C], ident)
                        mm.then_inc(S["ld_turned"], 1)
                    for q, c in enumerate(pair):
                        b = bufs[q]
                        pe.wait_ge(S["ldtok_ready"], c + 1)
                        for j in range(NPAIR):
                            mm = M.matmul(bk(q, 1)[:, j * C:j * C + C], b["LDtok"][0:C, j, :],
                                          incl[0:C, int(c == 5), :], start=True, stop=True)
                        mm.then_inc(S["cum_done"], 1)
                        pe.wait_ge(S["vbd_ready"], c + 1)
                        for j in range(NPAIR):
                            mm = M.transpose(bk(q, 0)[:, j * P:j * P + P], b["VBD"][:, j, :], ident)
                        mm.then_inc(S["v_turned"], 1)
                    for q, c in enumerate(pair):
                        b = bufs[q]
                        pe.wait_ge(S["ktbd_ready"], c + 1)
                        for j in range(NPAIR):
                            mm = M.transpose(bk(q, 2)[:, j * P:j * P + P], b["KtBD"][:, j, :], ident)
                        mm.then_inc(S["k_turned"], 1)
                        pe.wait_ge(S["btbd_ready"], c + 1)
                        for j in range(NPAIR):
                            mm = M.transpose(bk(q, 3)[:, j * P:j * P + P], b["BtBD"][:, j, :], ident)
                        mm.then_inc(S["b_turned"], 1)
                    for q, c in enumerate(pair):
                        b = bufs[q]
                        pe.wait_ge(S["kqr_ready"], c + 1)
                        pe.wait_ge(S["lc_ready"], c + 1)
                        for j in range(NPAIR):
                            mm = M.matmul(bk(q, 1)[:, j * P:j * P + P], b["KtBD"][:, j, :],
                                          b["KqR"][:, j, :, :], start=True, stop=True)
                        mm.then_inc(S["sk_done"], 1)
                        pe.wait_ge(S["ktok_ready"], c + 1)
                        for j in range(NPAIR):
                            mm = M.matmul(bk(q, 2)[:, j * P:j * P + P], b["BtBD"][:, j, :],
                                          b["KqR"][:, j, :, :], start=True, stop=True)
                        mm.then_inc(S["sb_done"], 1)
                    for q, c in enumerate(pair):
                        b = bufs[q]
                        pe.wait_ge(S["n0_ready"], c + 1)
                        pe.wait_ge(S["btok_ready"], c + 1)
                        for j in range(NPAIR):
                            mm = M.transpose(bk(q, 3)[0:C, j * P:j * P + P], b["tmp"][:, j, :], ident)
                        mm.then_inc(S["n0_turned"], 1)

                    for l in range(1, 6):
                        qs = [q for q in range(2) if l < LEVELS[pair[q]]]
                        for q in qs:
                            b, m = bufs[q], number[(g, l, q)]
                            pe.wait_ge(S["nl_ready"], m + 1)
                            if l == 1:
                                pe.wait_ge(S["at0_ready"], pair[q] + 1)
                                pe.wait_ge(S["vtok_ready"], pair[q] + 1)
                            else:
                                pe.wait_ge(S["at_ready"], inner[(g, l - 1, q)] + 1)
                            for j in range(NPAIR):
                                mm = M.matmul(bk(q, 0)[0:C, j * P:j * P + P], b["n"][l % 2][:, j, :],
                                              b["AT"][:, j, :], start=True, stop=True)
                            mm.then_inc(S["an_done"], 1)
                        for q in qs:
                            b, m = bufs[q], number[(g, l, q)]
                            pe.wait_ge(S["e_ready"], m + 1)
                            if l == 1:
                                pe.wait_ge(S["a0_ready"], pair[q] + 1)
                                pe.wait_ge(S["sb_read"], pair[q] + 1)
                                pe.wait_ge(S["sk_read"], pair[q] + 1)
                            else:
                                pe.wait_ge(S["a_ready"], inner[(g, l - 1, q)] + 1)
                            if (g, l, q) in inner:
                                for j in range(NPAIR):
                                    mm = M.matmul(bk(q, 2)[0:C, j * P:j * P + P], b["A"][:, j, :],
                                                  b["E"][:, j, :], start=True, stop=True)
                                mm.then_inc(S["atn_done"], 1)
                            for j in range(NPAIR):
                                mm = M.matmul(bk(q, 1)[:, j * C:j * C + C], b["E"][:, j, :], b["A"][:, j, :],
                                              start=True, stop=True)
                            mm.then_inc(S["an2_done"], 1)

                    def y_part(q, lhs, rhs, start, stop):
                        for j in range(NPAIR):
                            mm = M.matmul(bk(q, 3)[:, j * C:j * C + C], lhs[:, j, :], rhs[:, j, :],
                                          start=(start and j == 0), stop=(stop and j == NPAIR - 1))
                        return mm

                    def finish_y(q, c):
                        pe.wait_ge(S["unbd_ready"], c + 1)
                        y_part(q, bufs[q]["UnBD"], bufs[q]["M2T"], start=False, stop=True).then_inc(S["y_done"], 1)

                    prompt = [(q, c) for q, c in enumerate(pair) if c < 5]
                    for q, c in prompt:
                        b = bufs[q]
                        pe.wait_ge(S["vc_ready"], c + 1)
                        if (g, LEVELS[c] - 2, q) in inner:
                            pe.wait_ge(S["at_ready"], inner[(g, LEVELS[c] - 2, q)] + 1)
                        for j in range(NPAIR):
                            M.matmul(bk(q, 0)[:, j * C:j * C + C], b["AkT"][:, j, :], b["Vc"][:, j, :],
                                     start=(j == 0), stop=False)
                        for j in range(NPAIR):
                            M.matmul(bk(q, 2)[:, j * C:j * C + C], b["Ktok"][:, j, :], b["Vc"][:, j, :],
                                     start=(j == 0), stop=False)
                    for q, c in prompt:
                        b = bufs[q]
                        pe.wait_ge(S["kqbd_ready"], c + 1)
                        if c == 0:
                            pe.wait_ge(S["zeroed"], 1)
                        else:
                            pe.wait_ge(S["z_ready"], c)
                        for j in range(NPAIR):
                            mm = M.matmul(bk(q, 0)[:, j * C:j * C + C], b["KqBD"][:, j, :], Zc[:, j, :],
                                          start=False, stop=(j == NPAIR - 1))
                        mm.then_inc(S["w_done"], 1)
                        if q == 1:
                            finish_y(0, c - 1)
                        y_part(q, b["Vtok"], b["M1T"], start=True, stop=False)
                        pe.wait_ge(S["x_ready"], whole[c])
                        pe.wait_ge(S["wc_ready"], c + 1)
                        for j in range(NPAIR):
                            mm = M.matmul(bk(q, 1)[:, j * C:j * C + C], b["X"][:, j, :], b["Wc"][:, j, :],
                                          start=True, stop=True)
                        mm.then_inc(S["u_done"], 1)
                        if c > 0:
                            pe.wait_ge(S["zbd_ready"], c)
                        y_part(q, ZBD, b["KqR"][:, :, 1, :], start=False, stop=False).then_inc(S["zbd_used"], 1)
                        pe.wait_ge(S["un_ready"], c + 1)
                        for j in range(NPAIR):
                            mm = M.matmul(bk(q, 2)[:, j * C:j * C + C], b["Btok"][:, j, :], b["Un"][:, j, :],
                                          start=False, stop=(j == NPAIR - 1))
                        mm.then_inc(S["z_done"], 1)
                    finish_y(*prompt[-1])
                    if pair[1] == 5:
                        q, c, b = 1, 5, bufs[1]
                        pe.wait_ge(S["kqbd_ready"], 6)
                        pe.wait_ge(S["vc_ready"], 6)
                        o = shaped(bk(q, 3), NPAIR * 2, C)
                        for j in range(NPAIR):
                            for s in range(NSEQ):
                                mm = M.matmul(o[:, 2 * j:2 * j + 2, SL * s:SL * s + SL],
                                              zsBD[:, NPAIR * s + j, :],
                                              b["KqR"][:, j, :, SL * s:SL * s + SL], start=True, stop=True)
                        mm.then_inc(S["sz_done"], 1)
                        pe.wait_ge(S["x_ready"], whole[c])
                        for j in range(NPAIR):
                            mm = M.matmul(bk(q, 1)[:, j * C:j * C + C], b["AkT"][:, j, :], b["Vc"][:, j, :],
                                          start=True, stop=True)
                        mm.then_inc(S["w_done"], 1)
                        pe.wait_ge(S["sz_read"], 1)
                        for j in range(NPAIR):
                            mm = M.transpose(bk(q, 0)[0:C, j * P:j * P + P], szb[:, j, 0:C], ident)
                        mm.then_inc(S["szt_turned"], 1)
                        pe.wait_ge(S["wc_ready"], c + 1)
                        for j in range(NPAIR):
                            mm = M.matmul(bk(q, 2)[:, j * C:j * C + C], b["X"][:, j, :], b["Wc"][:, j, :],
                                          start=True, stop=True)
                        mm.then_inc(S["u_done"], 1)
                        pe.wait_ge(S["unbd_ready"], c + 1)
                        for j in range(NPAIR):
                            o = bk(q, 1)[:, j * C:j * C + C]
                            M.matmul(o, b["Vtok"][:, j, :], b["M1T"][:, j, :], start=True, stop=False)
                            mm = M.matmul(o, b["UnBD"][:, j, :], b["M2T"][:, j, :], start=False, stop=True)
                        mm.then_inc(S["y_done"], 1)
                        pe.wait_ge(S["btok_ready"], c + 1)
                        for j, i in enumerate((0, 3, 2, 1)):
                            pe.wait_ge(S["vx_ready"], j + 1)
                            pe.wait_ge(S["ux_ready"], j + 1)
                            if i == 0:
                                pe.wait_ge(S["szt_ready"], 1)
                            if i == 1:
                                pe.wait_ge(S["sy_read"], 1)
                            M.matmul(bk(q, i), b["Ktok"][:, j, :], Vx[:, j, :], start=True, stop=False)
                            M.matmul(bk(q, i), b["Btok"][:, j, :], Ux[:, j, :], start=False, stop=True)\
                                .then_inc(S["zs_done"], 1)

                @block.vector
                def _(dve):
                    V = nc.vector
                    dve.wait_ge(S["zeroed"], 1)
                    for q, c in enumerate(pair):
                        b, ts = bufs[q], CHUNKS[c]
                        dve.wait_ge(S["lc_ready"], c + 1)
                        V.tensor_tensor(b["Lx"], b["Lc"], ldT[:, :, ts:ts + C], ALU.subtract)\
                            .then_inc(S["lx_ready"], 1)
                        dve.wait_ge(S["eml_ready"], c + 1)
                        for i in range(2):
                            last = V.tensor_tensor(diag(b["KtBD"], i), half(kT, i)[:, :, ts:ts + C],
                                                   half(b["emL"], i), ALU.mult)
                        last.then_inc(S["ktbd_ready"], 1)
                        dve.wait_ge(S["elx_ready"], c + 1)
                        V.tensor_tensor(b["KqR"][:, :, 0, :], kkT[:, :, ts:ts + C], b["eLx"], ALU.mult)\
                            .then_inc(S["q_ready"], 1)
                        V.tensor_tensor(b["KqR"][:, :, 1, :], rT[:, :, ts:ts + C], b["eL"], ALU.mult)\
                            .then_inc(S["kqr_ready"], 1)
                        dve.wait_ge(S["b_turned"], c + 1)
                        own = row16[:, 0:1] if c == 4 else row16[:, 1:2]
                        V.tensor_scalar(b["Btok"].rearrange("p j c -> p (j c)"), bk(q, 3), own, None, ALU.mult)\
                            .then_inc(S["btok_ready"], 1)
                    for q, c in enumerate(pair):
                        b, w = bufs[q], int(c == 5)
                        dve.wait_ge(S["sk_done"], c + 1)
                        dve.wait_ge(S["v_turned"], c + 1)
                        src = shaped(bk(q, 1), NPAIR, P)
                        for i in range(2):
                            V.tensor_tensor(diag(b["AkT"], i), half(src[:, :, 0:C], i),
                                            b2(half(strict[:, w, :], i), NPAIR), ALU.mult)
                        V.tensor_tensor(b["M1T"], src[:, :, C:P], b2(incl[:, w, :], NPAIR), ALU.mult)\
                            .then_inc(S["sk_read"], 1)
                        dve.wait_ge(S["sb_done"], c + 1)
                        dve.wait_ge(S["btbd_ready"], c + 1)
                        src = shaped(bk(q, 2), NPAIR, P)
                        V.tensor_tensor(b["tmp"], src[:, :, 0:C], b2(level[:, 0, :], NPAIR), ALU.mult)\
                            .then_inc(S["n0_ready"], 1)
                        V.tensor_copy(b["nraw"], src[:, :, 0:C]).then_inc(S["nraw_ready"], 1)
                        V.tensor_tensor(b["M2T"], src[:, :, C:P], b2(incl[:, w, :], NPAIR), ALU.mult)\
                            .then_inc(S["sb_read"], 1)
                        dve.wait_ge(S["n0_ready"], c + 1)
                        V.tensor_tensor(b["A"], b2(identc, NPAIR), b["tmp"], ALU.subtract)\
                            .then_inc(S["a0_ready"], 1)

                    def identity_minus(dst, src):
                        src = shaped(src[0:C, :], NPAIR, P)
                        for i in range(2):
                            last = V.tensor_tensor(diag(dst, i), b2(ident[0:C, 0:C], NPAIR),
                                                   src[:, :, 64 * i:64 * i + 64], ALU.subtract)
                        return last

                    for q, c in enumerate(pair):
                        dve.wait_ge(S["n0_turned"], c + 1)
                        identity_minus(bufs[q]["AT"], bk(q, 3)).then_inc(S["at0_ready"], 1)
                    for l, q in plan[g]:
                        m = number[(g, l, q)]
                        dve.wait_ge(S["an_done"], m + 1)
                        identity_minus(bufs[q]["E"], bk(q, 0)).then_inc(S["e_ready"], 1)
                    for q, c in enumerate(pair):
                        b, ts = bufs[q], CHUNKS[c]
                        dve.wait_ge(S["w_done"], c + 1)
                        if c < 5:
                            V.tensor_copy(b["Wc"], shaped(bk(q, 0)[:, 0:NPAIR * C], NPAIR, C))\
                                .then_inc(S["wc_ready"], 1)
                            dve.wait_ge(S["z_done"], c + 1)
                            V.tensor_tensor(b["tmp"], Zc, shaped(bk(q, 2)[:, 0:NPAIR * C], NPAIR, C), ALU.add)\
                                .then_inc(S["state_sum"], 1)
                            end = min(C, NPR - ts) - 1
                            g_end = b["eL"][:, :, end:end + 1].broadcast_to([P, NPAIR, C])
                            dve.wait_ge(S["state_sum"], c + 1)
                            V.tensor_tensor(Zc, b["tmp"], g_end, ALU.mult).then_inc(S["z_ready"], 1)
                            dve.wait_ge(S["zbd_used"], c + 1)
                            for i in range(2):
                                last = V.tensor_tensor(diag(ZBD, i), half(b["tmp"], i), half(g_end, i), ALU.mult)
                            last.then_inc(S["zbd_ready"], 1)
                        else:
                            dve.wait_ge(S["szt_ready"], 1)
                            V.tensor_tensor(b["Wc"], shaped(bk(q, 1)[:, 0:NPAIR * C], NPAIR, C), b["tmp"],
                                            ALU.add).then_inc(S["wc_ready"], 1)
                            dve.wait_ge(S["un_ready"], 6)
                            for j in range(NPAIR):
                                V.tensor_tensor(shaped(Ux[:, j, :], NSEQ, HD), b2(b["Un"][:, j, :], NSEQ),
                                                b3(seqrow, HD), ALU.mult).then_inc(S["ux_ready"], 1)
                            dve.wait_ge(S["y_done"], 6)
                            V.tensor_tensor(yT[:, :, NPR:NT], shaped(bk(q, 1)[:, 0:NPAIR * C], NPAIR, C),
                                            szb[:, :, C:P], ALU.add).then_inc(S["sy_read"], 1)
                            zs = zsBD.rearrange("p (s j) v -> p s j v", j=NPAIR)
                            for j, bi in enumerate((0, 3, 2, 1)):
                                dve.wait_ge(S["zs_done"], j + 1)
                                zn = shaped(zso[:, j, :], NSEQ, HD)
                                for i in range(2):
                                    last = V.tensor_tensor(
                                        half(zn, i), half(shaped(bk(q, bi), NSEQ, HD), i),
                                        zs[64 * i:64 * i + 64, :, j, 64 * i:64 * i + 64], ALU.add)
                                last.then_inc(S["state_sum"], 1)
                                dve.wait_ge(S["state_sum"], 6 + j)
                                V.tensor_tensor(zn, zn, b3(b["eL"][:, j, SL - 1:C:SL], HD), ALU.mult)\
                                    .then_inc(S["zso_ready"], 1)

        for g in range(3):
            scan_block(g)

        next_stage()
        cursor[0] = mixer_end
        acc = take(3, DM)
        hp = take(3, DM)
        gfin = take(DM)
        brows_at = cursor[0]
        xg = take(512)
        xT = take(4, 2, C)
        t1 = take(512)
        u1 = take(512)
        sg = take(512)
        sw = take(512)
        aT = take(4, 2, C)
        ys = take(512)
        brows = arena[:, brows_at:brows_at + 3 * DM].rearrange("p (w d) -> p w d", w=3)
        bmid = take(3, DM, dt=BF16)
        Pm = take(3, C)
        Pg = take(3, 2, C)
        PgT = take(3, P)
        rk = take(3)
        esel = take(C, dt=BF16)
        gjunk = arena[:, cursor[0]:cursor[0] + DM]
        cursor[0] += DM
        assert cursor[0] <= arena_words
        flat = arena[:, mixer_start:mixer_start + 8 * 4 * NT]
        sout = shaped(zsBD.rearrange("p a b -> p (a b)"), NSEQ * NPAIR, P)
        zpT = shaped(flat[:, 7488:8000], NPAIR, P)
        zsq = shaped(flat[:, 0:4 * NT], 4, NT)
        zvar = shaped(flat[:, 4 * NT:5 * NT], NT)
        ysq = shaped(flat[:, 6144:6144 + 4 * NT], 4, NT)
        h2T = shaped(flat[:, 0:KC * NT], KC, NT)
        at = [KC * NT]

        def bit(*shape, dt=F32):
            n = 1
            for d in shape:
                n *= d
            words = (n + 1) // 2 if dt == BF16 else n
            v = flat[:, at[0]:at[0] + words]
            at[0] += words
            assert at[0] <= 4096
            if dt != F32:
                v = v.bitcast(dt)
            return shaped(v, *shape)

        wr = bit(KC, NE)
        brow = bit(NE)
        logits = bit(3, NE)
        top = bit(3, 8)
        topi = bit(3, 8, dt=U32)
        topf = bit(3, 8)
        ntop = bit(3)
        eg = bit(3, TOPK)
        esum = bit(3)
        erec = bit(3)
        hot = bit(3, NE)
        mask = bit(3, NE)
        maskbf = bit(3, NE, dt=BF16)
        cnt, extra, incA, incB, exc, sel, selt = [bit(NE) for _ in range(7)]
        ovf = bit(4)
        dg = bit(2, NOVER)
        step_n = [0]

        F = {n: lsem("f_" + n) for n in [
            "acc_in", "brows_in", "wr_in", "gffn_in", "gfin_in",
            "zmean_done", "ymean_done", "z_centered", "y_centered", "zvar_done", "yvar_done", "zvar_ready",
            "zroot_ready", "yvar_ready", "yroot_ready", "z_affine", "z_sig", "zT_ready", "yT_ready", "dstep",
            "st_turned", "st_copied", "wout_done", "acc_ready", "ms_ready", "rms_ready", "hp_ready", "h2_turned",
            "h2T_ready", "logits_done", "ntop_ready", "eg_ready", "mask_ready", "rank_done", "diag_ready",
            "tab_done", "tab_ready", "bias_ready",
            "p_ready", "pg_ready", "esel_ready", "xg_done", "xg_ready", "x_turned", "x_ready", "g_done", "u_done",
            "t1_ready", "sg_ready", "act_ready", "a_turned", "aT_ready", "y_done", "ys_ready", "pgt_done",
            "pgt_ready", "cmb_done", "cmb_read", "mstep", "pstep", "fin_ms", "fin_root", "fin_ready", "rank_copied"]}

        def gate_src(w, e, u):
            return w[0][bass.ds(e, 1)].rearrange("o (p c) n -> p (o c) n", c=KC)[:, 2 * u:2 * u + 2, :]

        def down_src(w, e, u):
            return w[0][bass.ds(e, 1)].rearrange("o (c p) n -> p (o c) n", p=P)[:, 2 * u:2 * u + 2, :]

        UNITS = [(w, h, u) for h in range(2) for w in ("w_gate", "w_up", "w_down") for u in range(4)]

        def load_expert_unit(sp, it, n, experts):
            w, h, u = UNITS[n]
            src = (down_src if w == "w_down" else gate_src)(a[w], experts[h], u)
            sp.wait_ge(unit_used, it * UPAIR + (UPRE + n - RING + 1))
            sp.dma_start(slot(UPRE + n, DM), src).then_inc(unit_landed[(UPRE + n) % RING], 16)

        def wait_expert_unit(pe, it, n):
            t = UPRE + n
            pe.wait_ge(unit_landed[t % RING], it * (16 * UPAIR // RING) + 16 * (t // RING + 1))

        CMB_BANKS = [6, 7, 0, 1, 6, 7]

        def over_pairs(eng, body, first=PAIRS):
            n_over = eng.value_load(blocktab[0:1, NBLK:NBLK + 1], min_val=0, max_val=NOVER)
            with eng.Fori(first, PAIRS + OPAIRS) as it:
                with eng.If(n_over > (it - PAIRS) * 2):
                    body(it)

        with nc.Block() as block:
            @block.sync
            def _(sp):
                sp.dma_start(acc[0:META, 0, :], a["meta_tokens"]).then_inc(F["acc_in"], 16)
                sp.dma_start(acc[META:P, 0, :], a["x_prompt"][0, 0:P - META, :]).then_inc(F["acc_in"], 16)
                sp.dma_start(acc[:, 1, :], a["x_prompt"][0, P - META:2 * P - META, :]).then_inc(F["acc_in"], 16)
                sp.dma_start(acc[0:META, 2, :], a["x_prompt"][0, 2 * P - META:SEQ, :]).then_inc(F["acc_in"], 16)
                sp.dma_start(acc[META:META + NSA, 2, :],
                             a["x_sample"].rearrange("s t d -> (s t) d")).then_inc(F["acc_in"], 16)
                sp.dma_start(wr, a["w_router"][0].rearrange("(p c) e -> p c e", c=KC)).then_inc(F["wr_in"], 16)
                sp.dma_start(brow[0:1, :], a["b_router"]).then_inc(F["wr_in"], 16)
                sp.dma_start(gffn, a["norm_ffn"][0].rearrange("(p c) -> p c", c=KC)).then_inc(F["gffn_in"], 16)
                for i, nm in enumerate(("b_gate", "b_up", "b_down")):
                    sp.dma_start(brows[0:NE, i, :], a[nm][0]).then_inc(F["brows_in"], 16)
                sp.dma_start(gfin, a["norm_final"].rearrange("(o d) -> o d", o=1).broadcast_to([P, DM]))\
                    .then_inc(F["gfin_in"], 16)
                for n in range(UPAIR):
                    load_expert_unit(sp, 0, n, (0, 1))
                with sp.Fori(1, PAIRS) as it:
                    for n in range(UPAIR):
                        load_expert_unit(sp, it, n, (it * 2, it * 2 + 1))

                def body(it):
                    es = [sp.value_load(blocktab[0:1, bass.ds(it * 2 + h, 1)], min_val=0, max_val=NE - 1)
                          for h in range(2)]
                    for n in range(UPAIR):
                        load_expert_unit(sp, it, n, es)
                sp.wait_ge(F["tab_ready"], 1)
                over_pairs(sp, body)
                for i in range(3):
                    sp.wait_ge(F["fin_ready"], i + 1)
                    if i == 0:
                        sp.dma_start(a["y_prompt"][0, 0:P - META, :], acc[META:P, 0, :]).then_inc(out_stored, 16)
                    elif i == 1:
                        sp.dma_start(a["y_prompt"][0, P - META:2 * P - META, :], acc[:, 1, :])\
                            .then_inc(out_stored, 16)
                    else:
                        sp.dma_start(a["y_prompt"][0, 2 * P - META:SEQ, :], acc[0:META, 2, :])\
                            .then_inc(out_stored, 16)
                        sp.dma_start(a["y_sample"].rearrange("s t d -> (s t) d"), acc[META:META + NSA, 2, :])\
                            .then_inc(out_stored, 16)
                sp.wait_ge(out_stored, 16 * (stores[0] + 9 + 4))

            @block.gpsimd
            def _(pool):
                T = nc.gpsimd
                T.memset(rankm, -1.0)
                T.memset(gates, 0.0).then_inc(F["rank_copied"], 1)
                pool.wait_ge(F["z_centered"], 4)
                T.tensor_tensor(zsq, zT, zT, ALU.mult).then_inc(F["z_centered"], 1)
                pool.wait_ge(F["y_centered"], 4)
                T.tensor_tensor(ysq, yT, yT, ALU.mult).then_inc(F["y_centered"], 1)
                pool.wait_ge(F["brows_in"], 48)
                pstep = chain(pool, F["pstep"])
                pstep(T.tensor_copy(bias3[0:NE], brows[0:NE]))
                pstep(T.tensor_tensor(brows[0:NE], brows[0:NE], bias3[0:NE], ALU.subtract))
                pstep(T.tensor_copy(bmid[0:NE], brows[0:NE]))
                pstep(T.tensor_tensor(brows[0:NE], brows[0:NE], bmid[0:NE], ALU.subtract))
                pstep(T.tensor_copy(bias3[NE:2 * NE], bmid[0:NE]))
                pstep(T.tensor_copy(bias3[2 * NE:3 * NE], brows[0:NE]))
                nc.gpsimd.sem_inc(F["bias_ready"], 1)

            @block.scalar
            def _(act):
                A = nc.scalar
                for n in range(9):
                    act.wait_ge(F["st_turned"], n + 1)
                    dst = sout[0:C, 4 * n:4 * n + 4, :] if n < 8 else zpT[0:C, :, :]
                    A.copy(dst, shaped(bank[0:C, 6 + n % 2, :], 4, P)).then_inc(F["st_copied"], 1)
                act.wait_ge(F["st_copied"], 9)
                for j in range(NPAIR):
                    for h in range(2):
                        act.dma_start(a["wkv_sample"][0][:, 2 * j + h].rearrange("s v k -> v s k"),
                                      sout[0:C, NSEQ * j:NSEQ * j + NSEQ, C * h:C * h + C]).then_inc(out_stored, 16)
                act.dma_start(a["wkv_prompt"][0, 0].rearrange("h v k -> v h k"),
                              zpT[0:C, :, :].rearrange("v j (h k) -> v (j h) k", h=2)).then_inc(out_stored, 16)
                act.wait_ge(F["zvar_ready"], 1)
                A.activation(zvar, zvar, ACT.Sqrt).then_inc(F["zroot_ready"], 1)
                act.wait_ge(F["yvar_ready"], 4)
                A.activation(ysq, ysq, ACT.Sqrt).then_inc(F["yroot_ready"], 1)
                act.wait_ge(F["z_affine"], 4)
                A.activation(zsq, zT, ACT.Sigmoid).then_inc(F["z_sig"], 1)
                for i, (t0, n) in enumerate(TILES):
                    act.wait_ge(F["ms_ready"], i + 1)
                    A.activation(small[0:n, 20 + i:21 + i], small[0:n, 16 + i:17 + i], ACT.Sqrt)\
                        .then_inc(F["rms_ready"], 1)
                for i, (t0, n) in enumerate(TILES):
                    act.wait_ge(F["ntop_ready"], i + 1)
                    A.activation(eg[0:n, i, :], top[0:n, i, 0:TOPK], ACT.Exp, bias=ntop[0:n, i:i + 1],
                                 accum_out=esum[0:n, i:i + 1]).then_inc(F["eg_ready"], 1)
                def block_of(n):
                    act.wait_ge(F["t1_ready"], n + 1)
                    A.activation(sg, t1, ACT.Sigmoid, scale=ALPHA).then_inc(F["sg_ready"], 1)
                    act.wait_ge(F["xg_done"], n + 2)
                    A.copy(xg, bank[:, 3, :]).then_inc(F["xg_ready"], 1)
                    act.wait_ge(F["a_turned"], n + 1)
                    A.copy(aT.rearrange("p m h s -> p (m h s)"), bank[:, 4, :]).then_inc(F["aT_ready"], 1)
                    act.wait_ge(F["y_done"], n + 1)
                    A.copy(ys, bank[:, 2, :]).then_inc(F["ys_ready"], 1)
                    act.wait_ge(F["pgt_done"], n + 1)
                    A.copy(PgT.rearrange("p i t -> p (i t)")[:, 0:NT], bank[:, 4, 0:NT]).then_inc(F["pgt_ready"], 1)

                def body(it):
                    for h in range(2):
                        block_of(it * 2 + h)

                act.wait_ge(F["xg_done"], 1)
                A.copy(xg, bank[:, 3, :]).then_inc(F["xg_ready"], 1)
                with act.Fori(0, PAIRS) as it:
                    body(it)
                act.wait_ge(F["tab_ready"], 1)
                over_pairs(act, body)
                for i, (t0, n) in enumerate(TILES):
                    act.wait_ge(F["fin_ms"], i + 1)
                    A.activation(small[0:n, 36 + i:37 + i], small[0:n, 32 + i:33 + i], ACT.Sqrt)\
                        .then_inc(F["fin_root"], 1)

            @block.tensor
            def _(pe):
                M = nc.tensor
                for j in range(4):
                    mm = M.matmul(bank[:, 4, 0:NT], ones, zT[:, j, :], start=(j == 0), stop=(j == 3))
                mm.then_inc(F["zmean_done"], 1)
                for j in range(4):
                    M.matmul(bank[:, j, 0:NT], headones, yT[:, j, :], start=True, stop=True)\
                        .then_inc(F["ymean_done"], 1)
                for n in range(9):
                    if n >= 2:
                        pe.wait_ge(F["st_copied"], n - 1)
                    for q in range(4):
                        src = zso[:, n // 2, C * (4 * (n % 2) + q):C * (4 * (n % 2) + q) + C] if n < 8 \
                            else Zc[:, q, :]
                        mm = M.transpose(bank[0:C, 6 + n % 2, q * P:q * P + P], src, ident)
                    mm.then_inc(F["st_turned"], 1)
                pe.wait_ge(F["z_centered"], 5)
                for j in range(4):
                    mm = M.matmul(bank[:, 5, 0:NT], ones, zsq[:, j, :], start=(j == 0), stop=(j == 3))
                mm.then_inc(F["zvar_done"], 1)
                pe.wait_ge(F["y_centered"], 5)
                for j in range(4):
                    M.matmul(bank[:, j, 0:NT], headones, ysq[:, j, :], start=True, stop=True)\
                        .then_inc(F["yvar_done"], 1)
                pe.wait_ge(F["zT_ready"], 1)
                for u in range(UNITS_OUT):
                    t = UNITS_IN + u
                    wait_unit(pe, t)
                    w = slot(t, DM)
                    if u == 2:
                        pe.wait_ge(F["yT_ready"], 1)
                    if u == 0:
                        pe.wait_ge(F["yvar_ready"], 4)
                    for c in range(2):
                        cc = 2 * OUT_ORDER[u] + c
                        src = zT[:, cc - 4, :] if cc >= 4 else yT[:, cc, :]
                        for i, (t0, n) in enumerate(TILES):
                            for hb in range(2):
                                mm = M.matmul(bank[0:n, 2 * i + hb, :], src[:, t0:t0 + n],
                                              w[:, c, 512 * hb:512 * hb + 512],
                                              start=(u == 0 and c == 0), stop=(u == 3 and c == 1))
                    mm.then_inc(unit_used, 1)
                for i, (t0, n) in enumerate(TILES):
                    pe.wait_ge(F["hp_ready"], i + 1)
                    if i == 0:
                        pe.wait_ge(F["acc_ready"], 6)
                    for hb in range(2):
                        if i >= 1:
                            pe.wait_ge(F["h2T_ready"], 2 * i - 1 + hb)
                        for c in range(4):
                            mm = M.transpose(bank[:, hb, c * P:c * P + n],
                                             hp[0:n, i, (4 * hb + c) * P:(4 * hb + c + 1) * P], ident[0:n, 0:n])
                        mm.then_inc(F["h2_turned"], 1)
                pe.wait_ge(F["wr_in"], 32)
                for i, (t0, n) in enumerate(TILES):
                    pe.wait_ge(F["h2T_ready"], 2 * i + 2)
                    for c in range(KC):
                        M.matmul(bank[0:n, 2, NE * i:NE * i + NE], h2T[:, c, t0:t0 + n], wr[:, c, :],
                                 start=(c == 0), stop=False)
                    mm = M.matmul(bank[0:n, 2, NE * i:NE * i + NE], ones[0:1, 0:n], brow[0:1, :],
                                  start=False, stop=True)
                mm.then_inc(F["logits_done"], 1)
                pe.wait_ge(F["mask_ready"], 1)
                for i, (t0, n) in enumerate(TILES):
                    o = bank[0:n, 3, NE * i:NE * i + NE]
                    for k in range(i):
                        M.matmul(o, onesbf[0:P, 0:n], maskbf[0:P, k, :], start=(k == 0), stop=False)
                    M.matmul(o, tribf[0:n, 0:n], maskbf[0:n, i, :], start=(i == 0), stop=True)
                for i, (t0, n) in enumerate(TILES):
                    mm = M.matmul(bank[:, 3, NE * 3:NE * 4], onesbf[0:n, :], maskbf[0:n, i, :],
                                  start=(i == 0), stop=(i == 2))
                mm.then_inc(F["rank_done"], 1)
                pe.wait_ge(F["diag_ready"], 1)
                M.matmul(bank[:, 2, 0:2 * NOVER], ones[0:NOVER, :], dg[0:NOVER, :, :].rearrange("p a b -> p (a b)"),
                         start=True, stop=True).then_inc(F["tab_done"], 1)

                def gather(n):
                    pe.wait_ge(F["p_ready"], n + 1)
                    for i, (t0, m) in enumerate(TILES):
                        for hb in range(2):
                            mm = M.matmul(bank[64 * hb:64 * hb + 64, 3, :], Pm[0:m, i, :],
                                          hp[0:m, i, 512 * hb:512 * hb + 512], start=(i == 0), stop=(i == 2))
                    mm.then_inc(F["xg_done"], 1)

                def turn_x(n):
                    pe.wait_ge(F["xg_ready"], n + 1)
                    for m in range(4):
                        mm = M.transpose(bank[:, 5, m * P:m * P + P], xg[:, m * P:m * P + P], ident)
                    mm.then_inc(F["x_turned"], 1)

                def product(it, first, b, tokens, w3):
                    for u in range(4):
                        wait_expert_unit(pe, it, first + u)
                        w = slot(UPRE + first + u, DM)
                        for c in range(2):
                            cc = 2 * u + c
                            for hb in range(2):
                                mm = M.matmul(bank[64 * hb:64 * hb + 64, b, :], tokens[:, cc % 4, cc // 4, :],
                                              w[:, c, 512 * hb:512 * hb + 512], start=(cc == 0), stop=False)
                        mm.then_inc(unit_used, 1)
                    for hb in range(2):
                        mm = M.matmul(bank[64 * hb:64 * hb + 64, b, :], esel[0:3 * NE, :],
                                      bias3[0:3 * NE, w3, 512 * hb:512 * hb + 512], start=False, stop=True)
                    return mm

                def block_of(it, h):
                    n = it * 2 + h
                    pe.wait_ge(F["x_ready"], n + 1)
                    pe.wait_ge(F["esel_ready"], n + 1)
                    pe.wait_ge(F["cmb_read"], n * 6 + 2)
                    product(it, 12 * h, 0, xT, 0).then_inc(F["g_done"], 1)
                    product(it, 12 * h + 4, 1, xT, 1).then_inc(F["u_done"], 1)
                    gather(n + 1)
                    pe.wait_ge(F["act_ready"], n + 1)
                    for m in range(4):
                        mm = M.transpose(bank[:, 4, m * P:m * P + P], sw[:, m * P:m * P + P], ident)
                    mm.then_inc(F["a_turned"], 1)
                    turn_x(n + 1)
                    pe.wait_ge(F["aT_ready"], n + 1)
                    product(it, 12 * h + 8, 2, aT, 2).then_inc(F["y_done"], 1)
                    pe.wait_ge(F["pg_ready"], n + 1)
                    for i, (t0, m) in enumerate(TILES):
                        mm = M.transpose(bank[:, 4, i * P:i * P + m], Pg[0:m, i, :, :], ident[0:m, 0:m])
                    mm.then_inc(F["pgt_done"], 1)
                    pe.wait_ge(F["ys_ready"], n + 1)
                    pe.wait_ge(F["pgt_ready"], n + 1)
                    for i, (t0, m) in enumerate(TILES):
                        if i == 0:
                            pe.wait_ge(F["cmb_read"], n * 6 + 4)
                        if i == 2:
                            pe.wait_ge(F["cmb_read"], n * 6 + 6)
                        for hb in range(2):
                            M.matmul(bank[0:m, CMB_BANKS[2 * i + hb], :], PgT[64 * hb:64 * hb + 64, i, 0:m],
                                     ys[64 * hb:64 * hb + 64, :], start=True, stop=True).then_inc(F["cmb_done"], 1)

                def body(it):
                    for h in range(2):
                        block_of(it, h)

                gather(0)
                turn_x(0)
                with pe.Fori(0, PAIRS) as it:
                    body(it)
                pe.wait_ge(F["tab_ready"], 1)
                over_pairs(pe, body)

            @block.vector
            def _(dve):
                V = nc.vector
                link = chain(dve, F["dstep"])
                dve.wait_ge(F["zmean_done"], 1)
                for j in range(4):
                    V.scalar_tensor_tensor(zT[:, j, :], bank[:, 4, 0:NT], -1.0 / CB, zT[:, j, :],
                                           ALU.mult, ALU.add).then_inc(F["z_centered"], 1)
                for j in range(4):
                    dve.wait_ge(F["ymean_done"], j + 1)
                    V.scalar_tensor_tensor(yT[:, j, :], bank[:, j, 0:NT], -1.0 / HD, yT[:, j, :],
                                           ALU.mult, ALU.add).then_inc(F["y_centered"], 1)
                dve.wait_ge(F["zvar_done"], 1)
                V.tensor_scalar(zvar, bank[:, 5, 0:NT], 1.0 / CB, LN_EPS, ALU.mult, ALU.add)\
                    .then_inc(F["zvar_ready"], 1)
                dve.wait_ge(F["yvar_done"], 4)
                for j in range(4):
                    V.tensor_scalar(ysq[:, j, :], bank[:, j, 0:NT], 1.0 / HD, GN_EPS, ALU.mult, ALU.add)\
                        .then_inc(F["yvar_ready"], 1)
                dve.wait_ge(F["zroot_ready"], 1)
                link(V.reciprocal(zvar, zvar))
                link(V.tensor_tensor(zT, zT, b2(zvar, 4), ALU.mult))
                for j in range(4):
                    V.tensor_scalar(zT[:, j, :], zT[:, j, :], vecA[:, V_CLW + j:V_CLW + j + 1],
                                    vecA[:, V_CLB + j:V_CLB + j + 1], ALU.mult, ALU.add).then_inc(F["z_affine"], 1)
                dve.wait_ge(F["yroot_ready"], 1)
                link(V.reciprocal(ysq, ysq))
                dve.wait_ge(F["z_sig"], 1)
                V.tensor_tensor(zT, zT, zsq, ALU.mult).then_inc(F["zT_ready"], 1)
                link(V.tensor_tensor(yT, yT, ysq, ALU.mult))
                for j in range(4):
                    last = V.tensor_scalar(yT[:, j, :], yT[:, j, :], vecA[:, V_LW + j:V_LW + j + 1],
                                           vecA[:, V_LB + j:V_LB + j + 1], ALU.mult, ALU.add)
                link(last)
                link(V.tensor_tensor(yT, yT, bonT, ALU.add))
                V.tensor_tensor(yT, yT, gT, ALU.mult).then_inc(F["yT_ready"], 1)
                dve.wait_ge(F["acc_in"], 16 * 5)
                dve.wait_ge(unit_used, UPRE)
                for i, (t0, n) in enumerate(TILES):
                    for hb in range(2):
                        o = acc[0:n, i, 512 * hb:512 * hb + 512]
                        V.tensor_tensor(o, o, bank[0:n, 2 * i + hb, :], ALU.add).then_inc(F["acc_ready"], 1)
                for i, (t0, n) in enumerate(TILES):
                    dve.wait_ge(F["acc_ready"], 2 * i + 2)
                    link(V.tensor_tensor_reduce(out=gjunk[0:n, :], in0=acc[0:n, i, :], in1=acc[0:n, i, :], scale=1.0,
                                                scalar=0.0, op0=ALU.mult, op1=ALU.add,
                                                accum_out=small[0:n, 24 + i:25 + i]))
                    V.tensor_scalar(small[0:n, 16 + i:17 + i], small[0:n, 24 + i:25 + i], 1.0 / DM, RMS_EPS,
                                    ALU.mult, ALU.add).then_inc(F["ms_ready"], 1)
                for i, (t0, n) in enumerate(TILES):
                    dve.wait_ge(F["rms_ready"], i + 1)
                    link(V.reciprocal(small[0:n, 28 + i:29 + i], small[0:n, 20 + i:21 + i]))
                    V.tensor_scalar(hp[0:n, i, :].rearrange("t (c p) -> t c p", c=KC),
                                    acc[0:n, i, :].rearrange("t (p c) -> t c p", c=KC),
                                    small[0:n, 28 + i:29 + i], None, ALU.mult).then_inc(F["hp_ready"], 1)
                dve.wait_ge(F["gffn_in"], 16)
                for i, (t0, n) in enumerate(TILES):
                    for hb in range(2):
                        dve.wait_ge(F["h2_turned"], 2 * i + hb + 1)
                        V.tensor_tensor(h2T[:, 4 * hb:4 * hb + 4, t0:t0 + n],
                                        shaped(bank[:, hb, :], 4, P)[:, :, 0:n],
                                        b3(gffn[:, 4 * hb:4 * hb + 4], n), ALU.mult).then_inc(F["h2T_ready"], 1)
                dve.wait_ge(F["logits_done"], 1)
                dve.wait_ge(F["rank_copied"], 1)
                for i, (t0, n) in enumerate(TILES):
                    link(V.tensor_copy(logits[0:n, i, :], bank[0:n, 2, NE * i:NE * i + NE]))
                    link(V.max(out=top[0:n, i, :], in_=logits[0:n, i, :]))
                    V.tensor_scalar(ntop[0:n, i:i + 1], top[0:n, i, 0:1], -1.0, None, ALU.mult)\
                        .then_inc(F["ntop_ready"], 1)
                    link(V.max_index(out=topi[0:n, i, :], in_max=top[0:n, i, :], in_values=logits[0:n, i, :]))
                    link(V.tensor_copy(topf[0:n, i, :], topi[0:n, i, :]))
                for i, (t0, n) in enumerate(TILES):
                    dve.wait_ge(F["eg_ready"], i + 1)
                    link(V.reciprocal(erec[0:n, i:i + 1], esum[0:n, i:i + 1]))
                    link(V.tensor_scalar(eg[0:n, i, :], eg[0:n, i, :], erec[0:n, i:i + 1], None, ALU.mult))
                    link(V.tensor_scalar(mask[0:n, i, :], exp_iota[0:n, :], topf[0:n, i, 0:1], None, ALU.is_equal))
                    link(V.tensor_scalar(gates[0:n, i, :], mask[0:n, i, :], eg[0:n, i, 0:1], None, ALU.mult))
                    for k in range(1, TOPK):
                        link(V.tensor_scalar(hot[0:n, i, :], exp_iota[0:n, :], topf[0:n, i, k:k + 1], None,
                                             ALU.is_equal))
                        V.tensor_tensor(mask[0:n, i, :], mask[0:n, i, :], hot[0:n, i, :], ALU.add)
                        link(V.scalar_tensor_tensor(gates[0:n, i, :], hot[0:n, i, :], eg[0:n, i, k:k + 1],
                                                    gates[0:n, i, :], ALU.mult, ALU.add))
                    last = V.tensor_copy(maskbf[0:n, i, :], mask[0:n, i, :])
                last.then_inc(F["mask_ready"], 1)
                dve.wait_ge(F["rank_done"], 1)
                for i, (t0, n) in enumerate(TILES):
                    link(V.scalar_tensor_tensor(rankm[0:n, i, :], bank[0:n, 3, NE * i:NE * i + NE], 1.0,
                                                mask[0:n, i, :], ALU.add, ALU.mult))
                    V.tensor_scalar(rankm[0:n, i, :], rankm[0:n, i, :], -1.0, None, ALU.add)
                link(V.tensor_copy(cnt, bank[:, 3, NE * 3:NE * 4]))
                link(V.tensor_scalar(extra, cnt, float(C), None, ALU.is_gt))
                for b in range(2, -(-NT // C)):
                    link(V.scalar_tensor_tensor(extra, cnt, float(C * b), extra, ALU.is_gt, ALU.add))
                link(V.tensor_copy(incA, extra))
                src, dst = incA, incB
                for d in (1, 2, 4, 8, 16):
                    V.tensor_copy(dst[:, 0:d], src[:, 0:d])
                    link(V.tensor_tensor(dst[:, d:NE], src[:, d:NE], src[:, 0:NE - d], ALU.add))
                    src, dst = dst, src
                link(V.tensor_tensor(exc, src, extra, ALU.subtract))
                link(V.tensor_scalar(selt, exc, rowf, None, ALU.is_le))
                link(V.scalar_tensor_tensor(sel, src, rowf, selt, ALU.is_gt, ALU.mult))
                link(V.tensor_tensor_reduce(out=selt, in0=sel, in1=exp_iota, scale=1.0, scalar=0.0, op0=ALU.mult,
                                            op1=ALU.add, accum_out=ovf[:, 0:1]))
                link(V.tensor_tensor_reduce(out=selt, in0=sel, in1=exc, scale=1.0, scalar=0.0, op0=ALU.mult,
                                            op1=ALU.add, accum_out=ovf[:, 1:2]))
                link(V.tensor_tensor_reduce(out=selt, in0=sel, in1=sel, scale=1.0, scalar=0.0, op0=ALU.mult,
                                            op1=ALU.add, accum_out=ovf[:, 2:3]))
                link(V.tensor_tensor(ovf[:, 1:2], rowf, ovf[:, 1:2], ALU.subtract))
                link(V.tensor_scalar(ovf[:, 1:2], ovf[:, 1:2], 1.0, float(C), ALU.add, ALU.mult))
                link(V.tensor_scalar(ovf[:, 3:4], ovf[:, 2:3], -8192.0, 8192.0, ALU.mult, ALU.add))
                link(V.tensor_tensor(ovf[:, 1:2], ovf[:, 1:2], ovf[:, 3:4], ALU.add))
                V.tensor_scalar(dg[0:NOVER, 0, :], ident[0:NOVER, 0:NOVER], ovf[0:NOVER, 0:1], None, ALU.mult)
                V.tensor_scalar(dg[0:NOVER, 1, :], ident[0:NOVER, 0:NOVER], ovf[0:NOVER, 1:2], None, ALU.mult)\
                    .then_inc(F["diag_ready"], 1)
                V.tensor_copy(blocktab[:, 0:NE], exp_iota)
                V.memset(blockbase[:, 0:NE], 0.0)
                V.memset(blockbase[:, NE + NOVER:NBLK], 8192.0)
                V.memset(blocktab[:, NE + NOVER:NBLK], 0)
                V.tensor_copy(blocktab[:, NBLK:NBLK + 1], src[:, NE - 1:NE])
                dve.wait_ge(F["tab_done"], 1)
                V.tensor_copy(blocktab[:, NE:NE + NOVER], bank[:, 2, 0:NOVER])
                V.tensor_copy(blockbase[:, NE:NE + NOVER], bank[:, 2, NOVER:2 * NOVER]).then_inc(F["tab_ready"], 1)
                dve.wait_ge(F["tab_ready"], 1)

                def expert_of(n):
                    return dve.value_load(blocktab[0:1, bass.ds(n, 1)], min_val=0, max_val=NE - 1)

                def make_p(n, e, stepped):
                    stepped(V.tensor_scalar(rk, rankm[:, :, bass.ds(e, 1)], blockbase[:, bass.ds(n, 1)], None,
                                            ALU.subtract))
                    for i, (t0, m) in enumerate(TILES):
                        last = V.tensor_scalar(Pm[0:m, i, :], slot_iota[0:m, :], rk[0:m, i:i + 1], None,
                                               ALU.is_equal)
                    last.then_inc(F["p_ready"], 1)

                def make_pg(e):
                    for i, (t0, m) in enumerate(TILES):
                        last = V.tensor_scalar(Pg[0:m, i], b2(slot_iota[0:m, :], 2), rk[0:m, i:i + 1],
                                               gates[0:m, i, bass.ds(e, 1)], ALU.is_equal, ALU.mult)
                    last.then_inc(F["pg_ready"], 1)
                    V.tensor_scalar(esel[0:3 * NE, :], ones[0:3 * NE, 0:C], expert_row[0:3 * NE, bass.ds(e, 1)], None,
                                    ALU.mult).then_inc(F["esel_ready"], 1)

                def take_x(n):
                    dve.wait_ge(F["x_turned"], n + 1)
                    g = gffn.rearrange("p (h m) -> p m h", h=2)
                    V.tensor_tensor(xT, bank[:, 5, :].rearrange("p (m h s) -> p m h s", m=4, h=2),
                                    g.unsqueeze(3).broadcast_to([P, 4, 2, C]), ALU.mult).then_inc(F["x_ready"], 1)

                def block_of(n, e_next, stepped):
                    dve.wait_ge(F["xg_done"], n + 1)
                    dve.wait_ge(F["esel_ready"], n + 1)
                    make_p(n + 1, e_next, stepped)
                    dve.wait_ge(F["g_done"], n + 1)
                    V.tensor_scalar(t1, bank[:, 0, :], LIMIT, None, ALU.min).then_inc(F["t1_ready"], 1)
                    dve.wait_ge(F["u_done"], n + 1)
                    stepped(V.tensor_scalar(u1, bank[:, 1, :], LIMIT, -LIMIT, ALU.min, ALU.max))
                    stepped(V.scalar_tensor_tensor(u1, u1, 1.0, t1, ALU.add, ALU.mult))
                    dve.wait_ge(F["sg_ready"], n + 1)
                    V.tensor_tensor(sw, u1, sg, ALU.mult).then_inc(F["act_ready"], 1)
                    take_x(n + 1)
                    dve.wait_ge(F["pgt_done"], n + 1)
                    make_pg(e_next)
                    for i, (t0, m) in enumerate(TILES):
                        for hb in range(2):
                            k = 2 * i + hb
                            dve.wait_ge(F["cmb_done"], n * 6 + (k + 1))
                            o = acc[0:m, i, 512 * hb:512 * hb + 512]
                            V.tensor_tensor(o, o, bank[0:m, CMB_BANKS[k], :], ALU.add).then_inc(F["cmb_read"], 1)

                STEPS = 6

                def body(it):
                    n = [0]

                    def stepped(ins):
                        n[0] += 1
                        ins.then_inc(F["mstep"], 1)
                        dve.wait_ge(F["mstep"], it * STEPS + (1 + n[0]))

                    es = [expert_of(it * 2 + 1), expert_of(it * 2 + 2)]
                    for h in range(2):
                        block_of(it * 2 + h, es[h], stepped)
                    assert n[0] == STEPS

                dve.sem_inc(F["cmb_read"], 4)

                def stepped0(ins):
                    ins.then_inc(F["mstep"], 1)
                    dve.wait_ge(F["mstep"], 1)
                dve.wait_ge(F["bias_ready"], 1)
                e0 = expert_of(0)
                make_p(0, e0, stepped0)
                make_pg(e0)
                take_x(0)
                with dve.Fori(0, PAIRS) as it:
                    body(it)
                over_pairs(dve, body)
                dve.wait_ge(F["gfin_in"], 16)
                for i, (t0, n) in enumerate(TILES):
                    link(V.tensor_tensor_reduce(out=hp[0:n, i, :], in0=acc[0:n, i, :], in1=acc[0:n, i, :], scale=1.0,
                                                scalar=0.0, op0=ALU.mult, op1=ALU.add,
                                                accum_out=small[0:n, 40 + i:41 + i]))
                    V.tensor_scalar(small[0:n, 32 + i:33 + i], small[0:n, 40 + i:41 + i], 1.0 / DM, RMS_EPS,
                                    ALU.mult, ALU.add).then_inc(F["fin_ms"], 1)
                for i, (t0, n) in enumerate(TILES):
                    dve.wait_ge(F["fin_root"], i + 1)
                    link(V.reciprocal(small[0:n, 44 + i:45 + i], small[0:n, 36 + i:37 + i]))
                    V.scalar_tensor_tensor(acc[0:n, i, :], acc[0:n, i, :], small[0:n, 44 + i:45 + i], gfin[0:n, :],
                                           ALU.mult, ALU.mult).then_inc(F["fin_ready"], 1)


_INS = ['x_prompt', 'x_sample', 'state_wkv', 'state_shift', 'state_conv', 'meta_tokens', 'norm_mix', 'w_in',
        'tshift_mu', 'decay_w0', 'decay_w2', 'iclr_a0', 'iclr_a2', 'gate_g2', 'k_k', 'k_a', 'r_k', 'lnx_w', 'lnx_b',
        'glu_b', 'dw_weight', 'dw_bias', 'conv_ln_w', 'conv_ln_b', 'w_out', 'norm_ffn', 'w_router', 'b_router',
        'w_gate', 'b_gate', 'w_up', 'b_up', 'w_down', 'b_down', 'norm_final']
_OUTS = [("y_prompt", (1, SEQ, DM)), ("y_sample", (NSEQ, SL, DM)), ("wkv_prompt", (1, 1, NH, HD, HD)),
         ("shift_prompt", (1, 1, SHC)), ("conv_prompt", (1, 1, HIST, CB)), ("wkv_sample", (1, NSEQ, NH, HD, HD)),
         ("shift_sample", (1, NSEQ, SHC)), ("conv_sample", (1, NSEQ, HIST, CB))]


def kernel(**inputs):
    import numpy as _np
    import concourse.bacc as _bacc
    from concourse.bass_utils import run_bass_kernel_spmd as _run

    nc = _bacc.Bacc("TRN2", target_bir_lowering=False, num_devices=1)
    arrays, aps = {}, {}
    for name in _INS:
        v = _np.ascontiguousarray(inputs[name])
        arrays[f"in_{name}_dram"] = v
        aps[name] = nc.dram_tensor(f"in_{name}_dram", v.shape, mybir.dt.from_np(v.dtype), kind="ExternalInput").ap()
    for name, shape in _OUTS:
        aps[name] = nc.dram_tensor(f"out_{name}_dram", shape, F32, kind="ExternalOutput").ap()
    build(nc, aps)
    r = _run(nc, [arrays], core_ids=[0])
    return tuple(r.results[0][f"out_{name}_dram"] for name, _ in _OUTS)
```

```python
from contextlib import ExitStack

import concourse.bass as bass
from concourse import mybir

ALU = mybir.AluOpType
ACT = mybir.ActivationFunctionType
AX = mybir.AxisListType
F32 = mybir.dt.float32
BF16 = mybir.dt.bfloat16
I32 = mybir.dt.int32
U32 = mybir.dt.uint32

P = 128
DM = 1024
KC = DM // P
META, SEQ = 16, 256
NPR = META + SEQ
NSEQ, SL = 8, 8
NSA = NSEQ * SL
NT = NPR + NSA
TILES = [(0, 128), (128, 128), (256, NT - 256)]
CA, CB = 512, 512
NH, HD = 8, 64
NPAIR = NH // 2
NBA = 14
SHC = NBA * P
CW = 31
HIST = CW - 1
NE, TOPK = 32, 4
LIMIT, ALPHA = 7.0, 1.702
RMS_EPS, LN_EPS, GN_EPS = 1e-5, 1e-5, 64e-5
HALF_DECAY = 0.6065306597126334

UNIT = 2048
RING = 8
UNITS_IN = 11
UNITS_OUT = 4
UPRE = UNITS_IN + UNITS_OUT
UPAIR = 24
C = 64
NOVER = 20
NBLK = NE + NOVER + 2
PAIRS, OPAIRS = NE // 2, NOVER // 2
OUT_ORDER = [2, 3, 0, 1]
IN_ORDER = [7, 9, 8, 10, 6, 2, 3, 0, 1, 4, 5]
CHUNKS = [0, 64, 128, 192, 256, NPR]
LEVELS = [6, 6, 6, 6, 4, 3]
EXTP = HIST + NPR
EXTS = HIST + SL



def build(nc, a):
    ctx = ExitStack()
    with ctx:
        stage_sems = []

        def sem(name):
            return ctx.enter_context(nc.semaphore(name))

        def lsem(name):
            stage_sems.append(nc.alloc_semaphore(name))
            return stage_sems[-1]

        def next_stage():
            nc.clear_and_free_semaphores(list(stage_sems))
            stage_sems.clear()
            nc.all_engine_barrier()

        bank = ctx.enter_context(nc.psum_tensor("bank", [P, 8, 512], F32))
        ring = ctx.enter_context(nc.sbuf_tensor("ring", [P, RING, UNIT], F32))
        arena_words = 36800
        arena = ctx.enter_context(nc.sbuf_tensor("arena", [P, arena_words], F32))
        cursor = [0]

        def shaped(v, *shape):
            if len(shape) == 2:
                return v.rearrange("p (a b) -> p a b", b=shape[1])
            if len(shape) == 3:
                return v.rearrange("p (a b c) -> p a b c", b=shape[1], c=shape[2])
            return v

        def take(*shape, dt=F32):
            n = 1
            for d in shape:
                n *= d
            words = (n + 1) // 2 if dt == BF16 else n
            v = arena[:, cursor[0]:cursor[0] + words]
            cursor[0] += words
            assert cursor[0] <= arena_words, (cursor[0], arena_words)
            if dt != F32:
                v = v.bitcast(dt)
            return shaped(v, *shape)

        def b3(ap, n):
            return ap.unsqueeze(2).broadcast_to([ap.shape[0], ap.shape[1], n])

        def b2(ap, n):
            return ap.unsqueeze(1).broadcast_to([ap.shape[0], n, ap.shape[1]])

        ident = take(P)
        ones = take(P)
        headones = take(P)
        strict = take(2, C)
        incl = take(2, C)
        identc = take(C)
        level = take(6, C)
        seqrow = take(NSEQ)
        row16 = take(2)
        rowf = take(1)
        tribf = take(P, dt=BF16)
        onesbf = take(P, dt=BF16)
        vecA = take(80)
        vecW = take(CW * 4)
        vecS = take(NSEQ * NBA)
        slot_iota = take(C)
        exp_iota = take(NE)
        bias3 = take(3, DM, dt=BF16)
        expert_row = take(NE)
        gffn = take(KC)
        small = take(64)
        rankm = take(3, NE)
        gates = take(3, NE)
        blockbase = take(NBLK)
        blocktab = take(NBLK + 2, dt=I32)
        Zc = take(NPAIR, HD)
        ZBD = take(NPAIR, P)
        mixer_start = cursor[0]
        rT, kT, vT, ldT, kkT, bT, gT, bonT, yT, zT = [take(4, NT) for _ in range(10)]
        zsBD = take(NSEQ * NPAIR, P)
        mixer_end = cursor[0]

        V_NORM, V_MU, V_W0, V_A0, V_KK, V_KA, V_RK, V_GLU, V_DWB, V_CLW, V_CLB, V_LW, V_LB, V_OMKA = \
            0, 8, 22, 26, 30, 34, 38, 42, 50, 54, 58, 62, 66, 70
        NVEC = 70

        unit_landed = [sem(f"unit_landed{i}") for i in range(RING)]
        unit_used = sem("unit_used")
        out_stored = sem("out_stored")
        stores = [0]

        def slot(t, n):
            return ring[:, t % RING, :].rearrange("p (c n) -> p c n", n=n)

        def load_unit(sp, t):
            if t >= RING:
                sp.wait_ge(unit_used, t - RING + 1)
            if t < UNITS_IN:
                n = IN_ORDER[t]
                src = a["w_in"][0].rearrange("(c p) n -> p c n", p=P)[:, :, n * 256:(n + 1) * 256]
                sp.dma_start(slot(t, 256), src).then_inc(unit_landed[t % RING], 16)
            else:
                u = OUT_ORDER[t - UNITS_IN]
                src = a["w_out"][0].rearrange("(c p) n -> p c n", p=P)[:, 2 * u:2 * u + 2, :]
                sp.dma_start(slot(t, DM), src).then_inc(unit_landed[t % RING], 16)

        def wait_unit(eng, t):
            eng.wait_ge(unit_landed[t % RING], 16 * (t // RING + 1))

        def diag(ap, i):
            return ap[64 * i:64 * i + 64, :, 64 * i:64 * i + 64]

        def half(ap, i):
            return ap[64 * i:64 * i + 64]

        def chain(eng, s):
            n = [0]

            def link(ins):
                n[0] += 1
                ins.then_inc(s, 1)
                eng.wait_ge(s, n[0])
            return link

        cursor[0] = mixer_end
        xt = take(3, DM)
        hT = take(KC, NT)
        ext = take(4, EXTP + NSEQ * EXTS)
        edge = take(2, NPR + 1 + NSEQ * (SL + 1))
        diff_at = cursor[0]
        diff = take(2, NT)
        uval = take(2, NT)
        usig = take(2, NT)
        uflat = take(4, NSA)
        tmpA = take(4, NT)
        lastc = take(NBA * (1 + NSEQ))
        loraw = take(2, CA)
        tmpB = shaped(arena[:, diff_at:diff_at + 4 * NT], 4, NT)
        s0c = shaped(xt.rearrange("p a b -> p (a b)")[:, 2 * CB:2 * CB + NSEQ * NPAIR * HD], NSEQ * NPAIR, HD)
        vrow = shaped(tmpA.rearrange("p a b -> p (a b)")[:, 0:384], 3, P)
        cbuf = shaped(zT.rearrange("p a b -> p (a b)")[:, 0:1024], 2, CB)
        junk = shaped(gT.rearrange("p a b -> p (a b)")[:, 0:DM])
        yi = yT.rearrange("p a b -> p (a b)")
        icol, irow, ixor, itmp, rowm = [yi[:, P * i:P * i + P].bitcast(I32) for i in range(5)]
        geq = shaped(yi[:, 640:640 + 7 * C], 7, C)
        lor_in = bonT[:, 0:2, :]
        lor_tanh, lor_sig = bonT[0:64, 2, :], bonT[:, 3, :]
        lastT = shaped(usig.rearrange("p a b -> p (a b)")[:, 0:P])
        cpT = shaped(xt.rearrange("p a b -> p (a b)")[:, 0:CB])
        csT = shaped(xt.rearrange("p a b -> p (a b)")[:, CB:2 * CB])

        def ext_prompt(j, lo, n):
            return ext[:, j, lo:lo + n]

        def ext_sample(j, lo, n):
            return ext[:, j, EXTP:].rearrange("p (s t) -> p s t", t=EXTS)[:, :, lo:lo + n]

        def edge_prompt(b, lo, n):
            return edge[:, b, lo:lo + n]

        def edge_sample(b, lo, n):
            return edge[:, b, NPR + 1:].rearrange("p (s t) -> p s t", t=SL + 1)[:, :, lo:lo + n]

        def by_seq(ap):
            return ap[:, NPR:NT].rearrange("p (s t) -> p s t", t=SL)

        x_in = lsem("x_in")
        rows_in = lsem("rows_in")
        hist_in = lsem("hist_in")
        s0_in = lsem("s0_in")
        lora_in = lsem("lora_in")
        iota_done = lsem("iota_done")
        consts_done = lsem("consts_done")
        dve_step = lsem("dve_step")
        rows_turned = lsem("rows_turned")
        vec_ready = lsem("vec_ready")
        hist_turned = lsem("hist_turned")
        hist_ready = lsem("hist_ready")
        ms_ready = lsem("ms_ready")
        rms_ready = lsem("rms_ready")
        xn_ready = lsem("xn_ready")
        x_turned = lsem("x_turned")
        hT_ready = lsem("hT_ready")
        proj_first = lsem("proj_first")
        proj_read = lsem("proj_read")
        uv_ready = lsem("uv_ready")
        u_ready = lsem("u_ready")
        edge_ready = lsem("edge_ready")
        diff_ready = lsem("diff_ready")
        last_taken = lsem("last_taken")
        shifted = lsem("shifted")
        lora_act = lsem("lora_act")
        lora_w = lsem("lora_w")
        lora_a = lsem("lora_a")
        lora_g = lsem("lora_g")
        decay_sig = lsem("decay_sig")
        rate_sig = lsem("rate_sig")
        gate_read = lsem("gate_read")
        kk_sq = lsem("kk_sq")
        kk_sum = lsem("kk_sum")
        kk_root = lsem("kk_root")
        rk_ready = lsem("rk_ready")
        rk_sum = lsem("rk_sum")
        last_turned = lsem("last_turned")
        last_copied = lsem("last_copied")
        cout_turned = lsem("cout_turned")
        cout_copied = lsem("cout_copied")
        s0_turned = lsem("s0_turned")
        s0_read = lsem("s0_read")
        pool_step = lsem("pool_step")
        conv_step = lsem("conv_step")

        order = [2 * n + b for n in IN_ORDER for b in range(2)]
        a_index = {cb: i for i, cb in enumerate(cb for cb in order if cb < NBA)}
        u_index = {cb: i for i, cb in enumerate(cb for cb in order if cb >= NBA + 4)}

        def wait_proj(eng, n):
            if n % 2:
                eng.wait_ge(unit_used, n // 2 + 1)
            else:
                eng.wait_ge(proj_first, n // 2 + 1)

        with nc.Block() as block:
            @block.sync
            def _(sp):
                sp.dma_start(xt[0:META, 0, :], a["meta_tokens"]).then_inc(x_in, 16)
                sp.dma_start(xt[META:P, 0, :], a["x_prompt"][0, 0:P - META, :]).then_inc(x_in, 16)
                sp.dma_start(xt[:, 1, :], a["x_prompt"][0, P - META:2 * P - META, :]).then_inc(x_in, 16)
                sp.dma_start(xt[0:META, 2, :], a["x_prompt"][0, 2 * P - META:SEQ, :]).then_inc(x_in, 16)
                sp.dma_start(xt[META:META + NSA, 2, :],
                             a["x_sample"].rearrange("s t d -> (s t) d")).then_inc(x_in, 16)
                for t in range(2):
                    load_unit(sp, t)
                sp.dma_start(cbuf[0:120, :, :],
                             a["state_conv"][0].rearrange("(g s) t c -> (s t) g c", g=2)).then_inc(hist_in, 16)
                sp.wait_ge(rows_in, 16 * 15)
                for t in range(2, RING):
                    load_unit(sp, t)
                sp.dma_start(loraw[0:64, 0, :], a["decay_w2"][0]).then_inc(lora_in, 16)
                sp.dma_start(loraw[64:128, 0, :], a["iclr_a2"][0]).then_inc(lora_in, 16)
                sp.dma_start(loraw[:, 1, :], a["gate_g2"][0]).then_inc(lora_in, 16)
                sp.wait_ge(hT_ready, 6)
                sp.dma_start(s0c[:, :, :].rearrange("p (s j) k -> p s j k", j=NPAIR),
                             a["state_wkv"][0].rearrange("s (j h) v k -> (h v) s j k", h=2)) \
                    .then_inc(s0_in, 16)
                sp.dma_start(a["conv_sample"][0][:, 0:HIST - SL, :],
                             a["state_conv"][0][:, SL:HIST, :]).then_inc(out_stored, 16)
                for t in range(RING, UPRE):
                    load_unit(sp, t)
                sp.wait_ge(last_copied, 1)
                sp.dma_start(a["shift_prompt"][0, 0].rearrange("(b p) -> b p", p=P),
                             lastT[0:NBA, :]).then_inc(out_stored, 16)
                sp.dma_start(a["shift_sample"][0].rearrange("s (b p) -> (s b) p", p=P),
                             lastT[NBA:NBA * (1 + NSEQ), :]).then_inc(out_stored, 16)
                sp.wait_ge(cout_copied, 2)
                sp.dma_start(a["conv_prompt"][0, 0], cpT[0:HIST, :]).then_inc(out_stored, 16)
                for s in range(NSEQ):
                    sp.dma_start(a["conv_sample"][0, s, HIST - SL:HIST, :],
                                 csT[SL * s:SL * s + SL, :]).then_inc(out_stored, 16)
                sp.wait_ge(out_stored, 16 * (4 + NSEQ))

            stores[0] = 4 + NSEQ

            @block.gpsimd
            def _(pool):
                nc.gpsimd.iota(icol, [[1, P]], base=0, channel_multiplier=0).then_inc(iota_done, 1)
                nc.gpsimd.iota(irow, [[0, P]], base=0, channel_multiplier=1).then_inc(iota_done, 1)
                link = chain(pool, pool_step)
                nc.gpsimd.memset(edge[:, :, 0:1], 0.0)
                nc.gpsimd.memset(ext[:, :, 0:HIST], 0.0)
                link(nc.gpsimd.memset(zsBD[:, :, :], 0.0))
                n_u = 0
                pool.wait_ge(hist_ready, 8)
                for n, cb in enumerate(order):
                    if cb >= NBA + 4:
                        j = cb - NBA - 4
                        pool.wait_ge(uv_ready, n + 1)
                        nc.gpsimd.tensor_tensor(ext_prompt(j, HIST, NPR), uval[:, j % 2, 0:NPR],
                                                usig[:, j % 2, 0:NPR], ALU.mult)
                        nc.gpsimd.tensor_tensor(ext_sample(j, HIST, SL), by_seq(uval[:, j % 2, :]),
                                                by_seq(usig[:, j % 2, :]), ALU.mult)
                        nc.gpsimd.tensor_tensor(uflat[:, j, :], uval[:, j % 2, NPR:NT],
                                                usig[:, j % 2, NPR:NT], ALU.mult).then_inc(u_ready, 1)
                        n_u += 1
                    elif cb < NBA:
                        i = a_index[cb]
                        b = i % 2
                        pool.wait_ge(edge_ready, i + 1)
                        if i >= 2:
                            pool.wait_ge(shifted, i - 1)
                        nc.gpsimd.tensor_tensor(diff[:, b, 0:NPR], edge_prompt(b, 0, NPR),
                                                edge_prompt(b, 1, NPR), ALU.subtract)
                        nc.gpsimd.tensor_tensor(by_seq(diff[:, b, :]), edge_sample(b, 0, SL),
                                                edge_sample(b, 1, SL), ALU.subtract).then_inc(diff_ready, 1)
                        nc.gpsimd.tensor_copy(lastc[:, cb:cb + 1], edge_prompt(b, NPR, 1))
                        nc.gpsimd.tensor_copy(lastc[:, NBA:].rearrange("p (s b) -> p s b", b=NBA)[:, :, cb:cb + 1],
                                              edge_sample(b, SL, 1)).then_inc(last_taken, 1)

            @block.scalar
            def _(act):
                at = 0
                for name, n in [("norm_mix", 8), ("tshift_mu", 14), ("decay_w0", 4), ("iclr_a0", 4), ("k_k", 4),
                                ("k_a", 4), ("r_k", 4), ("glu_b", 8), ("dw_bias", 4), ("conv_ln_w", 4),
                                ("conv_ln_b", 4), ("lnx_w", 4), ("lnx_b", 4)]:
                    src = a[name][0]
                    if name == "r_k":
                        src = src.rearrange("h k -> (h k)")
                    act.dma_start(vrow[at:at + n, 0, :], src.rearrange("(c p) -> c p", p=P)).then_inc(rows_in, 16)
                    at += n
                act.dma_start(vrow[0:CW * 4, 1, :],
                              a["dw_weight"][0].rearrange("t (c p) -> (t c) p", p=P)).then_inc(rows_in, 16)
                act.dma_start(vrow[0:NSEQ * NBA, 2, :],
                              a["state_shift"][0].rearrange("s (c p) -> (s c) p", p=P)).then_inc(rows_in, 16)
                for i, (t0, n) in enumerate(TILES):
                    act.wait_ge(ms_ready, i + 1)
                    nc.scalar.activation(small[0:n, 4 + i:5 + i], small[0:n, i:i + 1], ACT.Sqrt)\
                        .then_inc(rms_ready, 1)
                act.wait_ge(rows_turned, 1)
                nc.scalar.copy(vecA[:, 0:NVEC], bank[:, 7, 0:NVEC])
                nc.scalar.copy(vecW[:, :], bank[:, 7, P:P + CW * 4])
                nc.scalar.copy(vecS[:, :], bank[:, 7, 2 * P:2 * P + NSEQ * NBA]).then_inc(vec_ready, 1)
                for g in range(2):
                    act.wait_ge(hist_turned, g + 1)
                    for j in range(4):
                        nc.scalar.copy(ext_sample(j, 0, HIST)[:, 4 * g:4 * g + 4, :],
                                       bank[:, 5 + g, j * 120:j * 120 + 120]
                                       .rearrange("p (s t) -> p s t", t=HIST)).then_inc(hist_ready, 1)
                for n, cb in enumerate(order):
                    wait_proj(act, n)
                    src = bank[:, n % 4, 0:NT]
                    if cb >= NBA:
                        j = cb - NBA
                        if j < 4:
                            if j >= 2:
                                act.wait_ge(u_ready, j - 1)
                            nc.scalar.activation(uval[:, j % 2, :], src, ACT.Identity,
                                                 bias=vecA[:, V_GLU + j:V_GLU + j + 1]).then_inc(uv_ready, 1)
                        else:
                            if j >= 6:
                                act.wait_ge(u_ready, j - 5)
                            nc.scalar.activation(usig[:, j % 2, :], src, ACT.Sigmoid,
                                                 bias=vecA[:, V_GLU + j:V_GLU + j + 1]).then_inc(uv_ready, 1)
                        act.wait_ge(uv_ready, n + 1)
                    else:
                        i = a_index[cb]
                        b = i % 2
                        if i >= 2:
                            act.wait_ge(shifted, i - 1)
                            act.wait_ge(last_taken, i - 1)
                        nc.scalar.copy(edge_prompt(b, 1, NPR), src[:, 0:NPR])
                        nc.scalar.copy(edge_sample(b, 0, 1),
                                       vecS.rearrange("p (s b) -> p s b", b=NBA)[:, :, cb:cb + 1])
                        nc.scalar.copy(edge_sample(b, 1, SL), by_seq(src)).then_inc(edge_ready, 1)
                        act.wait_ge(edge_ready, i + 1)
                    nc.scalar.sem_inc(proj_read, 1)
                act.wait_ge(shifted, a_index[13] + 1)
                nc.scalar.activation(lor_tanh, lor_in[0:64, 0, :], ACT.Tanh).then_inc(lora_act, 1)
                nc.scalar.activation(lor_sig, lor_in[:, 1, :], ACT.Sigmoid).then_inc(lora_act, 1)
                for j in range(4):
                    act.wait_ge(lora_w, j + 1)
                    nc.scalar.activation(ldT[:, j, :], bank[:, j, 0:NT], ACT.Sigmoid,
                                         bias=vecA[:, V_W0 + j:V_W0 + j + 1]).then_inc(decay_sig, 1)
                for j in range(4):
                    act.wait_ge(lora_a, j + 1)
                    nc.scalar.activation(bT[:, j, :], bank[:, 4 + j, 0:NT], ACT.Sigmoid,
                                         bias=vecA[:, V_A0 + j:V_A0 + j + 1]).then_inc(rate_sig, 1)
                for j in range(4):
                    act.wait_ge(lora_g, j + 1)
                    nc.scalar.copy(gT[:, j, :], bank[:, j, 0:NT]).then_inc(gate_read, 1)
                for j in range(4):
                    act.wait_ge(kk_sum, j + 1)
                    nc.scalar.activation(tmpA[:, j, :], bank[:, 4 + j, 0:NT], ACT.Sqrt).then_inc(kk_root, 1)
                act.wait_ge(last_turned, 1)
                nc.scalar.copy(lastT[0:NBA * (1 + NSEQ), :], bank[0:NBA * (1 + NSEQ), 0, 0:P])\
                    .then_inc(last_copied, 1)
                act.wait_ge(cout_turned, 1)
                nc.scalar.copy(cpT[0:HIST, :], bank[0:HIST, 1, :]).then_inc(cout_copied, 1)
                act.wait_ge(cout_turned, 2)
                nc.scalar.copy(csT[0:NSA, :], bank[0:NSA, 2, :]).then_inc(cout_copied, 1)
                for g in range(8):
                    act.wait_ge(s0_turned, g + 1)
                    src = shaped(bank[0:64, g % 2, :], 4, P)
                    for i in range(2):
                        nc.scalar.copy(zsBD[64 * i:64 * i + 64, 4 * g:4 * g + 4, 64 * i:64 * i + 64],
                                       src[:, :, 64 * i:64 * i + 64]).then_inc(s0_read, 1)

            @block.tensor
            def _(pe):
                pe.wait_ge(consts_done, 1)
                pe.wait_ge(rows_in, 16 * 15)
                nc.tensor.transpose(bank[:, 7, 0:NVEC], vrow[0:NVEC, 0, :], ident[0:NVEC, 0:NVEC])
                nc.tensor.transpose(bank[:, 7, P:P + CW * 4], vrow[0:CW * 4, 1, :], ident[0:CW * 4, 0:CW * 4])
                nc.tensor.transpose(bank[:, 7, 2 * P:2 * P + NSEQ * NBA], vrow[0:NSEQ * NBA, 2, :],
                                    ident[0:NSEQ * NBA, 0:NSEQ * NBA]).then_inc(rows_turned, 1)
                for i, (t0, n) in enumerate(TILES):
                    pe.wait_ge(xn_ready, i + 1)
                    for hb in range(2):
                        if i >= 1:
                            pe.wait_ge(hT_ready, 2 * i - 1 + hb)
                        for c in range(4):
                            mm = nc.tensor.transpose(bank[:, 3 + hb, c * P:c * P + n],
                                                     xt[0:n, i, (4 * hb + c) * P:(4 * hb + c + 1) * P],
                                                     ident[0:n, 0:n])
                        mm.then_inc(x_turned, 1)
                pe.wait_ge(hist_in, 16)
                for g in range(2):
                    for j in range(4):
                        mm = nc.tensor.transpose(bank[:, 5 + g, j * 120:j * 120 + 120],
                                                 cbuf[0:120, g, j * P:j * P + P], ident[0:120, 0:120])
                    mm.then_inc(hist_turned, 1)
                pe.wait_ge(hT_ready, 6)
                for n, cb in enumerate(order):
                    t, b = n // 2, n % 2
                    if b == 0:
                        wait_unit(pe, t)
                    if n >= 4:
                        pe.wait_ge(proj_read, n - 3)
                    w = slot(t, 256)
                    for c in range(KC):
                        mm = nc.tensor.matmul(bank[:, n % 4, 0:NT], w[:, c, b * P:b * P + P], hT[:, c, :],
                                              start=(c == 0), stop=(c == KC - 1))
                    mm.then_inc(unit_used if b else proj_first, 1)
                pe.wait_ge(lora_in, 48)
                pe.wait_ge(lora_act, 2)
                pe.wait_ge(proj_read, 22)
                for j in range(4):
                    nc.tensor.matmul(bank[:, j, 0:NT], loraw[0:64, 0, j * P:j * P + P], lor_tanh,
                                     start=True, stop=True).then_inc(lora_w, 1)
                for j in range(4):
                    nc.tensor.matmul(bank[:, 4 + j, 0:NT], loraw[64:128, 0, j * P:j * P + P], lor_in[64:128, 0, :],
                                     start=True, stop=True).then_inc(lora_a, 1)
                for j in range(4):
                    pe.wait_ge(decay_sig, j + 1)
                    nc.tensor.matmul(bank[:, j, 0:NT], loraw[:, 1, j * P:j * P + P], lor_sig,
                                     start=True, stop=True).then_inc(lora_g, 1)
                for j in range(4):
                    pe.wait_ge(rate_sig, j + 1)
                    pe.wait_ge(kk_sq, 1)
                    nc.tensor.matmul(bank[:, 4 + j, 0:NT], headones, tmpA[:, j, :],
                                     start=True, stop=True).then_inc(kk_sum, 1)
                pe.wait_ge(gate_read, 4)
                pe.wait_ge(last_taken, NBA)
                nc.tensor.transpose(bank[0:NBA * (1 + NSEQ), 0, 0:P], lastc[:, :], ident).then_inc(last_turned, 1)
                for j in range(4):
                    mm = nc.tensor.transpose(bank[0:HIST, 1, j * P:j * P + P], ext_prompt(j, NPR, HIST), ident)
                mm.then_inc(cout_turned, 1)
                for j in range(4):
                    mm = nc.tensor.transpose(bank[0:NSA, 2, j * P:j * P + P], uflat[:, j, :], ident)
                mm.then_inc(cout_turned, 1)
                pe.wait_ge(kk_root, 4)
                pe.wait_ge(rk_ready, 1)
                for j in range(4):
                    nc.tensor.matmul(bank[:, 4 + j, 0:NT], headones, tmpB[:, j, :],
                                     start=True, stop=True).then_inc(rk_sum, 1)
                pe.wait_ge(s0_in, 16)
                pe.wait_ge(last_copied, 1)
                pe.wait_ge(cout_copied, 1)
                for g in range(8):
                    if g >= 2:
                        pe.wait_ge(s0_read, 2 * (g - 1))
                    for q in range(4):
                        mm = nc.tensor.transpose(bank[0:64, g % 2, q * P:q * P + P], s0c[:, 4 * g + q, :], ident)
                    mm.then_inc(s0_turned, 1)

            @block.vector
            def _(dve):
                link = chain(dve, dve_step)
                V = nc.vector
                dve.wait_ge(iota_done, 2)
                link(V.tensor_tensor(ixor, icol, irow, ALU.bitwise_xor))
                V.tensor_scalar(ident, ixor, 0.0, None, ALU.is_equal)
                V.tensor_scalar(headones, ixor, 64.0, None, ALU.is_lt)
                link(V.memset(ones, 1.0))
                V.memset(onesbf, 1.0).then_inc(consts_done, 1)
                V.tensor_tensor(tribf, irow, icol, ALU.is_lt)
                V.tensor_copy(rowf, irow[:, 0:1])
                V.tensor_copy(slot_iota, icol[:, 0:C])
                V.tensor_copy(exp_iota, icol[:, 0:NE])
                link(V.tensor_scalar(rowm, irow, 63, None, ALU.bitwise_and))
                link(V.tensor_scalar(itmp, ixor, 63, None, ALU.bitwise_and))
                for l in range(7):
                    last = V.tensor_scalar(geq[:, l, :], itmp[:, 0:C], float(2 ** l), None, ALU.is_ge)
                V.tensor_tensor(strict[:, 0, :], rowm[:, 0:C], icol[:, 0:C], ALU.is_lt)
                V.tensor_tensor(incl[:, 0, :], rowm[:, 0:C], icol[:, 0:C], ALU.is_le)
                V.tensor_tensor(identc, rowm[:, 0:C], icol[:, 0:C], ALU.is_equal)
                V.tensor_scalar(row16[:, 0:1], rowm[:, 0:1], 16.0, None, ALU.is_lt)
                link(V.memset(row16[:, 1:2], 1.0))
                link(V.tensor_tensor(level[:, :, :], geq[:, 0:6, :], geq[:, 1:7, :], ALU.subtract))
                link(V.tensor_tensor(level[:, :, :], level[:, :, :], b2(strict[:, 0, :], 6), ALU.mult))
                link(V.tensor_scalar(itmp, irow, NE - 1, None, ALU.bitwise_and))
                V.tensor_tensor(expert_row, itmp[:, 0:NE], icol[:, 0:NE], ALU.is_equal)
                link(V.tensor_scalar(geq[:, 3, :], geq[:, 3, :], -1.0, 1.0, ALU.mult, ALU.add))
                V.tensor_tensor(strict[:, 1, :], strict[:, 0, :], geq[:, 3, :], ALU.mult)
                V.tensor_tensor(incl[:, 1, :], incl[:, 0, :], geq[:, 3, :], ALU.mult)
                link(V.tensor_scalar(itmp, rowm, 3, None, ALU.logical_shift_right))
                link(V.tensor_tensor(seqrow, itmp[:, 0:NSEQ], icol[:, 0:NSEQ], ALU.is_equal))
                dve.wait_ge(x_in, 16 * 5)
                for i, (t0, n) in enumerate(TILES):
                    link(V.tensor_tensor_reduce(out=junk[0:n, :], in0=xt[0:n, i, :], in1=xt[0:n, i, :], scale=1.0,
                                                scalar=0.0, op0=ALU.mult, op1=ALU.add,
                                                accum_out=small[0:n, 8 + i:9 + i]))
                    V.tensor_scalar(small[0:n, i:i + 1], small[0:n, 8 + i:9 + i], 1.0 / DM, RMS_EPS,
                                    ALU.mult, ALU.add).then_inc(ms_ready, 1)
                for i, (t0, n) in enumerate(TILES):
                    dve.wait_ge(rms_ready, i + 1)
                    link(V.reciprocal(small[0:n, 12 + i:13 + i], small[0:n, 4 + i:5 + i]))
                    V.tensor_scalar(xt[0:n, i, :], xt[0:n, i, :], small[0:n, 12 + i:13 + i], None,
                                    ALU.mult).then_inc(xn_ready, 1)
                dve.wait_ge(vec_ready, 1)
                for i, (t0, n) in enumerate(TILES):
                    for hb in range(2):
                        dve.wait_ge(x_turned, 2 * i + hb + 1)
                        V.tensor_tensor(hT[:, 4 * hb:4 * hb + 4, t0:t0 + n],
                                        shaped(bank[:, 3 + hb, :], 4, P)[:, :, 0:n],
                                        b3(vecA[:, V_NORM + 4 * hb:V_NORM + 4 * hb + 4], n),
                                        ALU.mult).then_inc(hT_ready, 1)
                link(V.tensor_scalar(vecA[:, V_OMKA:V_OMKA + 4], vecA[:, V_KA:V_KA + 4], -1.0, 1.0,
                                     ALU.mult, ALU.add))

                def conv_steps():
                    for k, (j, tap) in enumerate(sorted(((j, tap) for j in range(4) for tap in range(CW)),
                                                        key=lambda x: (x[0] // 2, x[1], x[0]))):
                        w = vecW[:, 4 * tap + j:4 * tap + j + 1]
                        if tap == 0:
                            dve.wait_ge(u_ready, j + 1)
                            bias = vecA[:, V_DWB + j:V_DWB + j + 1]
                            V.tensor_scalar(zT[:, j, 0:NPR], ext_prompt(j, tap, NPR), w, bias,
                                            ALU.mult, ALU.add)
                            V.tensor_scalar(by_seq(zT[:, j, :]), ext_sample(j, tap, SL), w, bias,
                                            ALU.mult, ALU.add).then_inc(conv_step, 1)
                        else:
                            dve.wait_ge(conv_step, k - 1)
                            V.scalar_tensor_tensor(zT[:, j, 0:NPR], ext_prompt(j, tap, NPR), w,
                                                   zT[:, j, 0:NPR], ALU.mult, ALU.add)
                            V.scalar_tensor_tensor(by_seq(zT[:, j, :]), ext_sample(j, tap, SL), w,
                                                   by_seq(zT[:, j, :]), ALU.mult, ALU.add)\
                                .then_inc(conv_step, 1)
                        yield

                conv = conv_steps()
                early = 46
                for _ in range(early):
                    next(conv)
                share = -(-(CW * 4 - early) // (NBA - 2))
                a_order = sorted(a_index, key=a_index.get)
                for i, cb in enumerate(a_order):
                    b = i % 2
                    dst = [rT, kT, vT][cb // 4][:, cb % 4, :] if cb < 12 else lor_in[:, cb - 12, :]
                    mu = vecA[:, V_MU + cb:V_MU + cb + 1]
                    dve.wait_ge(diff_ready, i + 1)
                    V.scalar_tensor_tensor(dst[:, 0:NPR], diff[:, b, 0:NPR], mu, edge_prompt(b, 1, NPR),
                                           ALU.mult, ALU.add)
                    V.scalar_tensor_tensor(by_seq(dst), by_seq(diff[:, b, :]), mu, edge_sample(b, 1, SL),
                                           ALU.mult, ALU.add).then_inc(shifted, 1)
                    for _ in range(share):
                        next(conv, None)
                for _ in conv:
                    pass
                dve.wait_ge(shifted, NBA)
                for j in range(4):
                    last = V.tensor_scalar(kkT[:, j, :], kT[:, j, :], vecA[:, V_KK + j:V_KK + j + 1], None, ALU.mult)
                link(last)
                V.tensor_tensor(tmpA[:, :, :], kkT[:, :, :], kkT[:, :, :], ALU.mult).then_inc(kk_sq, 1)
                dve.wait_ge(rate_sig, 4)
                for j in range(4):
                    last = V.tensor_scalar(tmpB[:, j, :], bT[:, j, :], vecA[:, V_KA + j:V_KA + j + 1],
                                           vecA[:, V_OMKA + j:V_OMKA + j + 1], ALU.mult, ALU.add)
                link(last)
                link(V.tensor_tensor(kT[:, :, :], kT[:, :, :], tmpB[:, :, :], ALU.mult))
                for j in range(4):
                    last = V.scalar_tensor_tensor(tmpB[:, j, :], rT[:, j, :], vecA[:, V_RK + j:V_RK + j + 1],
                                                  kT[:, j, :], ALU.mult, ALU.mult)
                last.then_inc(rk_ready, 1)
                dve.wait_ge(decay_sig, 4)
                V.tensor_scalar(ldT[:, :, :], ldT[:, :, :], -HALF_DECAY, None, ALU.mult)
                dve.wait_ge(kk_root, 4)
                link(V.tensor_scalar(tmpA[:, :, :], tmpA[:, :, :], 1e-12, None, ALU.max))
                link(V.reciprocal(tmpA[:, :, :], tmpA[:, :, :]))
                link(V.tensor_tensor(kkT[:, :, :], kkT[:, :, :], tmpA[:, :, :], ALU.mult))
                V.tensor_tensor(bT[:, :, :], kkT[:, :, :], bT[:, :, :], ALU.mult)
                for j in range(4):
                    dve.wait_ge(rk_sum, j + 1)
                    V.tensor_tensor(bonT[:, j, :], bank[:, 4 + j, 0:NT], vT[:, j, :], ALU.mult)

        next_stage()
        cursor[0] = mixer_end
        bufs = []
        for q in range(2):
            b = {}
            b["X"] = take(NPAIR, P)
            b["A"] = take(NPAIR, C)
            b["n"] = [take(NPAIR, C) for _ in range(2)]
            b["tmp"] = take(NPAIR, C)
            b["nraw"] = take(NPAIR, C)
            b["eL"] = take(NPAIR, C)
            b["KqR"] = take(NPAIR, 2, C)
            b["KtBD"] = take(NPAIR, P)
            b["BtBD"] = take(NPAIR, P)
            b["KqBD"] = take(NPAIR, P)
            b["AkT"] = take(NPAIR, P)
            b["M1T"] = take(NPAIR, C)
            b["M2T"] = take(NPAIR, C)
            b["Ktok"] = take(NPAIR, P)
            b["Btok"] = take(NPAIR, P)
            b["Vtok"] = take(NPAIR, P)
            b["Vc"] = take(NPAIR, C)
            b["Un"] = take(NPAIR, C)
            b["LDtok"] = b["Btok"]
            b["Lc"], b["Lx"] = b["A"], b["n"][1]
            b["emL"], b["eLx"], b["Wc"] = b["tmp"], b["n"][0], b["n"][0]
            b["VBD"] = b["AkT"]
            b["AT"] = b["UnBD"] = b["KtBD"]
            b["E"] = b["BtBD"]
            bufs.append(b)
        flat = arena[:, mixer_start:mixer_start + 6 * 4 * NT]
        Vx = shaped(flat[:, 0:2048], NPAIR, 512)
        Ux = shaped(flat[:, 2048:4096], NPAIR, 512)
        zsq = shaped(flat[:, 4096:4096 + 4 * NT], 4, NT)
        zso_at = 4096 + 4 * NT
        zso = shaped(flat[:, zso_at:zso_at + 2048], NPAIR, 512)
        zvar = flat[:, zso_at + 2048:zso_at + 2048 + NT]
        szb = bufs[1]["BtBD"]

        names = ["zeroed", "ld_turned", "ldtok_ready", "cum_done", "lc_ready", "lx_ready", "el_ready", "eml_ready",
                 "elx_ready", "ktbd_ready", "btbd_ready", "vbd_ready", "q_ready", "kqr_ready", "kqbd_ready",
                 "k_turned", "b_turned", "v_turned", "ktok_ready", "btok_ready", "vtok_ready", "vc_ready",
                 "sk_done", "sb_done", "sk_read", "sb_read", "n0_ready", "n0_turned", "nraw_ready", "a0_ready",
                 "at0_ready", "nl_ready", "an_done", "e_ready", "atn_done", "at_ready", "an2_done", "a_ready",
                 "x_ready",
                 "w_done", "wc_ready", "u_done", "un_ready", "unbd_ready", "z_done", "z_ready", "zbd_used",
                 "zbd_ready",
                 "y_done", "y_read", "sz_done", "sz_read", "szt_turned", "szt_ready",
                 "vx_ready", "ux_ready", "zs_done", "zso_ready", "state_sum", "sy_read",
                 "zmean_done", "z_centered", "z_squared", "zvar_done", "zvar_ready", "zroot_ready", "zinv_ready",
                 "z_normed", "z_affine", "z_sig", "zT_ready"]
        S = {n: lsem("scan_" + n) for n in names}

        groups = [(0, 1), (2, 3), (4, 5)]
        plan = {g: [(l, q) for l in range(1, 6) for q in range(2) if l < LEVELS[groups[g][q]]] for g in range(3)}
        number, inner, whole = {}, {}, {}
        for g in range(3):
            for l, q in plan[g]:
                number[(g, l, q)] = len(number)
                if l < LEVELS[groups[g][q]] - 1:
                    inner[(g, l, q)] = len(inner)
                else:
                    whole[groups[g][q]] = len(whole) + 1

        def scan_block(g):
            pair = groups[g]

            def bk(q, i):
                return bank[:, 4 * q + i, :]

            with nc.Block() as block:
                @block.gpsimd
                def _(pool):
                    T = nc.gpsimd
                    if g == 0:
                        for q in range(2):
                            for nm in ("X", "KtBD", "BtBD", "KqBD", "AkT"):
                                T.memset(bufs[q][nm][:, :, :], 0.0)
                        T.memset(Zc[:, :, :], 0.0)
                        T.memset(ZBD[:, :, :], 0.0).then_inc(S["zeroed"], 1)
                        pool.wait_ge(S["zeroed"], 1)
                    for q, c in enumerate(pair):
                        b, ts = bufs[q], CHUNKS[c]
                        for i in range(2):
                            last = T.tensor_copy(diag(b["VBD"], i), half(vT, i)[:, :, ts:ts + C])
                        last.then_inc(S["vbd_ready"], 1)
                    for q, c in enumerate(pair):
                        b, ts = bufs[q], CHUNKS[c]
                        pool.wait_ge(S["eml_ready"], c + 1)
                        for i in range(2):
                            last = T.tensor_tensor(diag(b["BtBD"], i), half(bT, i)[:, :, ts:ts + C],
                                                   half(b["emL"], i), ALU.mult)
                        last.then_inc(S["btbd_ready"], 1)
                    for q, c in enumerate(pair):
                        b = bufs[q]
                        pool.wait_ge(S["q_ready"], c + 1)
                        for i in range(2):
                            last = T.tensor_copy(diag(b["KqBD"], i), half(b["KqR"][:, :, 0, :], i))
                        last.then_inc(S["kqbd_ready"], 1)
                    for q, c in enumerate(pair):
                        b = bufs[q]
                        pool.wait_ge(S["vtok_ready"], c + 1)
                        for i in range(2):
                            last = T.tensor_copy(half(b["Vc"], i), diag(b["Vtok"], i))
                        last.then_inc(S["vc_ready"], 1)
                    for l, q in plan[g]:
                        b, m = bufs[q], number[(g, l, q)]
                        if l == 1:
                            pool.wait_ge(S["nraw_ready"], pair[q] + 1)
                            pool.wait_ge(S["vc_ready"], pair[1] + 1)
                        if l >= 3:
                            pool.wait_ge(S["an_done"], number[(g, l - 2, q)] + 1)
                        T.tensor_tensor(b["n"][l % 2], b["nraw"], b2(level[:, l, :], NPAIR), ALU.mult)\
                            .then_inc(S["nl_ready"], 1)
                    if pair[1] == 5:
                        b = bufs[1]
                        for j in range(NPAIR):
                            T.tensor_tensor(shaped(Vx[:, j, :], NSEQ, HD), b2(b["Vc"][:, j, :], NSEQ),
                                            b3(seqrow, HD), ALU.mult).then_inc(S["vx_ready"], 1)

                @block.scalar
                def _(act):
                    A = nc.scalar
                    for q, c in enumerate(pair):
                        b = bufs[q]
                        act.wait_ge(S["ld_turned"], c + 1)
                        A.copy(b["LDtok"].rearrange("p j c -> p (j c)")[0:C, :], bk(q, 0)[0:C, :])\
                            .then_inc(S["ldtok_ready"], 1)
                    for q, c in enumerate(pair):
                        b = bufs[q]
                        act.wait_ge(S["cum_done"], c + 1)
                        A.copy(b["Lc"], shaped(bk(q, 1)[:, 0:NPAIR * C], NPAIR, C)).then_inc(S["lc_ready"], 1)
                        act.wait_ge(S["lc_ready"], c + 1)
                        A.activation(b["emL"], b["Lc"], ACT.Exp, scale=-1.0).then_inc(S["eml_ready"], 1)
                        A.activation(b["eL"], b["Lc"], ACT.Exp).then_inc(S["el_ready"], 1)
                        act.wait_ge(S["lx_ready"], c + 1)
                        A.activation(b["eLx"], b["Lx"], ACT.Exp).then_inc(S["elx_ready"], 1)
                    for q, c in enumerate(pair):
                        b = bufs[q]
                        act.wait_ge(S["v_turned"], c + 1)
                        A.copy(b["Vtok"].rearrange("p j c -> p (j c)"), bk(q, 0)).then_inc(S["vtok_ready"], 1)
                        act.wait_ge(S["k_turned"], c + 1)
                        own = row16[:, 0:1] if c == 4 else row16[:, 1:2]
                        A.activation(b["Ktok"].rearrange("p j c -> p (j c)"), bk(q, 2), ACT.Identity, scale=own)\
                            .then_inc(S["ktok_ready"], 1)
                    for l, q in plan[g]:
                        b, m = bufs[q], number[(g, l, q)]
                        if (g, l, q) in inner:
                            act.wait_ge(S["atn_done"], inner[(g, l, q)] + 1)
                            src = shaped(bk(q, 2)[0:C, :], NPAIR, P)
                            for i in range(2):
                                last = A.copy(diag(b["AT"], i), src[:, :, 64 * i:64 * i + 64])
                            last.then_inc(S["at_ready"], 1)
                            act.wait_ge(S["an2_done"], m + 1)
                            A.copy(b["A"], shaped(bk(q, 1)[:, 0:NPAIR * C], NPAIR, C)).then_inc(S["a_ready"], 1)
                        else:
                            act.wait_ge(S["an2_done"], m + 1)
                            for i in range(2):
                                last = A.copy(diag(b["X"], i), half(shaped(bk(q, 1)[:, 0:NPAIR * C], NPAIR, C), i))
                            last.then_inc(S["x_ready"], 1)
                    for q, c in enumerate(pair):
                        b, ts = bufs[q], CHUNKS[c]
                        if c == 4:
                            act.wait_ge(S["zvar_ready"], 1)
                            A.activation(zvar, zvar, ACT.Sqrt).then_inc(S["zroot_ready"], 1)
                        if c == 5:
                            act.wait_ge(S["z_affine"], 4)
                            A.activation(zsq, zT, ACT.Sigmoid).then_inc(S["z_sig"], 1)
                            act.wait_ge(S["sz_done"], 1)
                            A.copy(szb.rearrange("p j c -> p (j c)"), bk(q, 3)).then_inc(S["sz_read"], 1)
                            act.wait_ge(S["szt_turned"], 1)
                            src = shaped(bk(q, 0)[0:C, :], NPAIR, P)
                            for i in range(2):
                                last = A.copy(half(b["tmp"], i), src[:, :, 64 * i:64 * i + 64])
                            last.then_inc(S["szt_ready"], 1)
                        act.wait_ge(S["u_done"], c + 1)
                        u = shaped(bk(q, 2 if c == 5 else 1)[:, 0:NPAIR * C], NPAIR, C)
                        A.activation(b["Un"], u, ACT.Identity, scale=-1.0).then_inc(S["un_ready"], 1)
                        for i in range(2):
                            last = A.activation(diag(b["UnBD"], i), half(u, i), ACT.Identity, scale=-1.0)
                        last.then_inc(S["unbd_ready"], 1)
                        done = ([(q - 1, c - 1)] if q == 1 and c - 1 < 5 else []) + ([(q, c)] if q == 1 and c < 5 else [])
                        for yq, yc in done:
                            n_own = min(C, NPR - CHUNKS[yc])
                            act.wait_ge(S["y_done"], yc + 1)
                            A.copy(yT[:, :, CHUNKS[yc]:CHUNKS[yc] + n_own],
                                   shaped(bk(yq, 3)[:, 0:NPAIR * C], NPAIR, C)[:, :, 0:n_own])\
                                .then_inc(S["y_read"], 1)

                @block.tensor
                def _(pe):
                    M = nc.tensor
                    for q, c in enumerate(pair):
                        b, ts = bufs[q], CHUNKS[c]
                        for j in range(NPAIR):
                            mm = M.transpose(bk(q, 0)[0:C, j * P:j * P + P], ldT[:, j, ts:ts + C], ident)
                        mm.then_inc(S["ld_turned"], 1)
                    for q, c in enumerate(pair):
                        b = bufs[q]
                        pe.wait_ge(S["ldtok_ready"], c + 1)
                        for j in range(NPAIR):
                            mm = M.matmul(bk(q, 1)[:, j * C:j * C + C], b["LDtok"][0:C, j, :],
                                          incl[0:C, int(c == 5), :], start=True, stop=True)
                        mm.then_inc(S["cum_done"], 1)
                    for q, c in enumerate(pair):
                        b = bufs[q]
                        pe.wait_ge(S["vbd_ready"], c + 1)
                        for j in range(NPAIR):
                            mm = M.transpose(bk(q, 0)[:, j * P:j * P + P], b["VBD"][:, j, :], ident)
                        mm.then_inc(S["v_turned"], 1)
                    for q, c in enumerate(pair):
                        b = bufs[q]
                        pe.wait_ge(S["ktbd_ready"], c + 1)
                        for j in range(NPAIR):
                            mm = M.transpose(bk(q, 2)[:, j * P:j * P + P], b["KtBD"][:, j, :], ident)
                        mm.then_inc(S["k_turned"], 1)
                        pe.wait_ge(S["btbd_ready"], c + 1)
                        for j in range(NPAIR):
                            mm = M.transpose(bk(q, 3)[:, j * P:j * P + P], b["BtBD"][:, j, :], ident)
                        mm.then_inc(S["b_turned"], 1)
                    for q, c in enumerate(pair):
                        b = bufs[q]
                        pe.wait_ge(S["kqr_ready"], c + 1)
                        pe.wait_ge(S["lc_ready"], c + 1)
                        for j in range(NPAIR):
                            mm = M.matmul(bk(q, 1)[:, j * P:j * P + P], b["KtBD"][:, j, :],
                                          b["KqR"][:, j, :, :], start=True, stop=True)
                        mm.then_inc(S["sk_done"], 1)
                        pe.wait_ge(S["ktok_ready"], c + 1)
                        for j in range(NPAIR):
                            mm = M.matmul(bk(q, 2)[:, j * P:j * P + P], b["BtBD"][:, j, :],
                                          b["KqR"][:, j, :, :], start=True, stop=True)
                        mm.then_inc(S["sb_done"], 1)
                    for q, c in enumerate(pair):
                        b = bufs[q]
                        pe.wait_ge(S["n0_ready"], c + 1)
                        pe.wait_ge(S["btok_ready"], c + 1)
                        for j in range(NPAIR):
                            mm = M.transpose(bk(q, 3)[0:C, j * P:j * P + P], b["tmp"][:, j, :], ident)
                        mm.then_inc(S["n0_turned"], 1)
                    if g == 2:
                        pe.wait_ge(S["at0_ready"], 5)
                        for j in range(4):
                            mm = M.matmul(bank[:, 3, 0:NT], ones, zT[:, j, :], start=(j == 0), stop=(j == 3))
                        mm.then_inc(S["zmean_done"], 1)

                    for l in range(1, 6):
                        qs = [q for q in range(2) if l < LEVELS[pair[q]]]
                        for q in qs:
                            b, m = bufs[q], number[(g, l, q)]
                            pe.wait_ge(S["nl_ready"], m + 1)
                            if l == 1:
                                pe.wait_ge(S["at0_ready"], pair[q] + 1)
                                pe.wait_ge(S["vtok_ready"], pair[q] + 1)
                            else:
                                pe.wait_ge(S["at_ready"], inner[(g, l - 1, q)] + 1)
                            for j in range(NPAIR):
                                mm = M.matmul(bk(q, 0)[0:C, j * P:j * P + P], b["n"][l % 2][:, j, :],
                                              b["AT"][:, j, :], start=True, stop=True)
                            mm.then_inc(S["an_done"], 1)
                        for q in qs:
                            b, m = bufs[q], number[(g, l, q)]
                            pe.wait_ge(S["e_ready"], m + 1)
                            if l == 1:
                                pe.wait_ge(S["a0_ready"], pair[q] + 1)
                                pe.wait_ge(S["sb_read"], pair[q] + 1)
                                pe.wait_ge(S["sk_read"], pair[q] + 1)
                            else:
                                pe.wait_ge(S["a_ready"], inner[(g, l - 1, q)] + 1)
                            if (g, l, q) in inner:
                                for j in range(NPAIR):
                                    mm = M.matmul(bk(q, 2)[0:C, j * P:j * P + P], b["A"][:, j, :],
                                                  b["E"][:, j, :], start=True, stop=True)
                                mm.then_inc(S["atn_done"], 1)
                            for j in range(NPAIR):
                                mm = M.matmul(bk(q, 1)[:, j * C:j * C + C], b["E"][:, j, :], b["A"][:, j, :],
                                              start=True, stop=True)
                            mm.then_inc(S["an2_done"], 1)

                    if g == 2:
                        pe.wait_ge(S["z_squared"], 1)
                        for j in range(4):
                            mm = M.matmul(bank[:, 3, 0:NT], ones, zsq[:, j, :], start=(j == 0), stop=(j == 3))
                        mm.then_inc(S["zvar_done"], 1)

                    def y_part(q, lhs, rhs, start, stop):
                        for j in range(NPAIR):
                            mm = M.matmul(bk(q, 3)[:, j * C:j * C + C], lhs[:, j, :], rhs[:, j, :],
                                          start=(start and j == 0), stop=(stop and j == NPAIR - 1))
                        return mm

                    def finish_y(q, c):
                        pe.wait_ge(S["unbd_ready"], c + 1)
                        y_part(q, bufs[q]["UnBD"], bufs[q]["M2T"], start=False, stop=True).then_inc(S["y_done"], 1)

                    prompt = [(q, c) for q, c in enumerate(pair) if c < 5]
                    for q, c in prompt:
                        b = bufs[q]
                        pe.wait_ge(S["vc_ready"], c + 1)
                        if (g, LEVELS[c] - 2, q) in inner:
                            pe.wait_ge(S["at_ready"], inner[(g, LEVELS[c] - 2, q)] + 1)
                        for j in range(NPAIR):
                            M.matmul(bk(q, 0)[:, j * C:j * C + C], b["AkT"][:, j, :], b["Vc"][:, j, :],
                                     start=(j == 0), stop=False)
                        for j in range(NPAIR):
                            M.matmul(bk(q, 2)[:, j * C:j * C + C], b["Ktok"][:, j, :], b["Vc"][:, j, :],
                                     start=(j == 0), stop=False)
                    for q, c in prompt:
                        b = bufs[q]
                        pe.wait_ge(S["kqbd_ready"], c + 1)
                        if c == 0:
                            pe.wait_ge(S["zeroed"], 1)
                        else:
                            pe.wait_ge(S["z_ready"], c)
                        for j in range(NPAIR):
                            mm = M.matmul(bk(q, 0)[:, j * C:j * C + C], b["KqBD"][:, j, :], Zc[:, j, :],
                                          start=False, stop=(j == NPAIR - 1))
                        mm.then_inc(S["w_done"], 1)
                        if q == 1:
                            finish_y(0, c - 1)
                        if g == 2:
                            pe.wait_ge(S["zvar_ready"], 1)
                        y_part(q, b["Vtok"], b["M1T"], start=True, stop=False)
                        pe.wait_ge(S["x_ready"], whole[c])
                        pe.wait_ge(S["wc_ready"], c + 1)
                        for j in range(NPAIR):
                            mm = M.matmul(bk(q, 1)[:, j * C:j * C + C], b["X"][:, j, :], b["Wc"][:, j, :],
                                          start=True, stop=True)
                        mm.then_inc(S["u_done"], 1)
                        if c > 0:
                            pe.wait_ge(S["zbd_ready"], c)
                        y_part(q, ZBD, b["KqR"][:, :, 1, :], start=False, stop=False).then_inc(S["zbd_used"], 1)
                        pe.wait_ge(S["un_ready"], c + 1)
                        for j in range(NPAIR):
                            mm = M.matmul(bk(q, 2)[:, j * C:j * C + C], b["Btok"][:, j, :], b["Un"][:, j, :],
                                          start=False, stop=(j == NPAIR - 1))
                        mm.then_inc(S["z_done"], 1)
                    finish_y(*prompt[-1])
                    if pair[1] == 5:
                        q, c, b = 1, 5, bufs[1]
                        pe.wait_ge(S["kqbd_ready"], 6)
                        pe.wait_ge(S["vc_ready"], 6)
                        o = shaped(bk(q, 3), NPAIR * 2, C)
                        for j in range(NPAIR):
                            for s in range(NSEQ):
                                mm = M.matmul(o[:, 2 * j:2 * j + 2, SL * s:SL * s + SL],
                                              zsBD[:, NPAIR * s + j, :],
                                              b["KqR"][:, j, :, SL * s:SL * s + SL], start=True, stop=True)
                        mm.then_inc(S["sz_done"], 1)
                        pe.wait_ge(S["x_ready"], whole[c])
                        for j in range(NPAIR):
                            mm = M.matmul(bk(q, 1)[:, j * C:j * C + C], b["AkT"][:, j, :], b["Vc"][:, j, :],
                                          start=True, stop=True)
                        mm.then_inc(S["w_done"], 1)
                        pe.wait_ge(S["sz_read"], 1)
                        for j in range(NPAIR):
                            mm = M.transpose(bk(q, 0)[0:C, j * P:j * P + P], szb[:, j, 0:C], ident)
                        mm.then_inc(S["szt_turned"], 1)
                        pe.wait_ge(S["wc_ready"], c + 1)
                        for j in range(NPAIR):
                            mm = M.matmul(bk(q, 2)[:, j * C:j * C + C], b["X"][:, j, :], b["Wc"][:, j, :],
                                          start=True, stop=True)
                        mm.then_inc(S["u_done"], 1)
                        pe.wait_ge(S["unbd_ready"], c + 1)
                        for j in range(NPAIR):
                            o = bk(q, 1)[:, j * C:j * C + C]
                            M.matmul(o, b["Vtok"][:, j, :], b["M1T"][:, j, :], start=True, stop=False)
                            mm = M.matmul(o, b["UnBD"][:, j, :], b["M2T"][:, j, :], start=False, stop=True)
                        mm.then_inc(S["y_done"], 1)
                        pe.wait_ge(S["btok_ready"], c + 1)
                        for j, i in enumerate((0, 3, 2, 1)):
                            pe.wait_ge(S["vx_ready"], j + 1)
                            pe.wait_ge(S["ux_ready"], j + 1)
                            if i == 0:
                                pe.wait_ge(S["szt_ready"], 1)
                            if i == 1:
                                pe.wait_ge(S["sy_read"], 1)
                            M.matmul(bk(q, i), b["Ktok"][:, j, :], Vx[:, j, :], start=True, stop=False)
                            M.matmul(bk(q, i), b["Btok"][:, j, :], Ux[:, j, :], start=False, stop=True)\
                                .then_inc(S["zs_done"], 1)

                @block.vector
                def _(dve):
                    V = nc.vector
                    dve.wait_ge(S["zeroed"], 1)
                    for q, c in enumerate(pair):
                        b, ts = bufs[q], CHUNKS[c]
                        dve.wait_ge(S["lc_ready"], c + 1)
                        V.tensor_tensor(b["Lx"], b["Lc"], ldT[:, :, ts:ts + C], ALU.subtract)\
                            .then_inc(S["lx_ready"], 1)
                        dve.wait_ge(S["eml_ready"], c + 1)
                        for i in range(2):
                            last = V.tensor_tensor(diag(b["KtBD"], i), half(kT, i)[:, :, ts:ts + C],
                                                   half(b["emL"], i), ALU.mult)
                        last.then_inc(S["ktbd_ready"], 1)
                        dve.wait_ge(S["elx_ready"], c + 1)
                        V.tensor_tensor(b["KqR"][:, :, 0, :], kkT[:, :, ts:ts + C], b["eLx"], ALU.mult)\
                            .then_inc(S["q_ready"], 1)
                        V.tensor_tensor(b["KqR"][:, :, 1, :], rT[:, :, ts:ts + C], b["eL"], ALU.mult)\
                            .then_inc(S["kqr_ready"], 1)
                    for q, c in enumerate(pair):
                        b = bufs[q]
                        dve.wait_ge(S["b_turned"], c + 1)
                        own = row16[:, 0:1] if c == 4 else row16[:, 1:2]
                        V.tensor_scalar(b["Btok"].rearrange("p j c -> p (j c)"), bk(q, 3), own, None, ALU.mult)\
                            .then_inc(S["btok_ready"], 1)
                    for q, c in enumerate(pair):
                        b, w = bufs[q], int(c == 5)
                        dve.wait_ge(S["sk_done"], c + 1)
                        dve.wait_ge(S["v_turned"], c + 1)
                        src = shaped(bk(q, 1), NPAIR, P)
                        for i in range(2):
                            V.tensor_tensor(diag(b["AkT"], i), half(src[:, :, 0:C], i),
                                            b2(half(strict[:, w, :], i), NPAIR), ALU.mult)
                        V.tensor_tensor(b["M1T"], src[:, :, C:P], b2(incl[:, w, :], NPAIR), ALU.mult)\
                            .then_inc(S["sk_read"], 1)
                        dve.wait_ge(S["sb_done"], c + 1)
                        dve.wait_ge(S["btbd_ready"], c + 1)
                        src = shaped(bk(q, 2), NPAIR, P)
                        V.tensor_tensor(b["tmp"], src[:, :, 0:C], b2(level[:, 0, :], NPAIR), ALU.mult)\
                            .then_inc(S["n0_ready"], 1)
                        V.tensor_copy(b["nraw"], src[:, :, 0:C]).then_inc(S["nraw_ready"], 1)
                        V.tensor_tensor(b["M2T"], src[:, :, C:P], b2(incl[:, w, :], NPAIR), ALU.mult)\
                            .then_inc(S["sb_read"], 1)
                        dve.wait_ge(S["n0_ready"], c + 1)
                        V.tensor_tensor(b["A"], b2(identc, NPAIR), b["tmp"], ALU.subtract)\
                            .then_inc(S["a0_ready"], 1)

                    def identity_minus(dst, src):
                        src = shaped(src[0:C, :], NPAIR, P)
                        for i in range(2):
                            last = V.tensor_tensor(diag(dst, i), b2(ident[0:C, 0:C], NPAIR),
                                                   src[:, :, 64 * i:64 * i + 64], ALU.subtract)
                        return last

                    for q, c in enumerate(pair):
                        dve.wait_ge(S["n0_turned"], c + 1)
                        identity_minus(bufs[q]["AT"], bk(q, 3)).then_inc(S["at0_ready"], 1)
                    for l, q in plan[g]:
                        m = number[(g, l, q)]
                        dve.wait_ge(S["an_done"], m + 1)
                        identity_minus(bufs[q]["E"], bk(q, 0)).then_inc(S["e_ready"], 1)
                        if g == 2 and q == 1 and l == 1:
                            dve.wait_ge(S["zmean_done"], 1)
                            for j in range(4):
                                V.scalar_tensor_tensor(zT[:, j, :], bank[:, 3, 0:NT], -1.0 / CB, zT[:, j, :],
                                                       ALU.mult, ALU.add).then_inc(S["z_centered"], 1)
                        if g == 2 and q == 1 and l == 2:
                            dve.wait_ge(S["z_centered"], 4)
                            V.tensor_tensor(zsq, zT, zT, ALU.mult).then_inc(S["z_squared"], 1)
                    for q, c in enumerate(pair):
                        b, ts = bufs[q], CHUNKS[c]
                        if c == 4:
                            dve.wait_ge(S["zvar_done"], 1)
                            V.tensor_scalar(zvar, bank[:, 3, 0:NT], 1.0 / CB, LN_EPS, ALU.mult, ALU.add)\
                                .then_inc(S["zvar_ready"], 1)
                        if c == 5:
                            dve.wait_ge(S["zroot_ready"], 1)
                            V.reciprocal(zvar, zvar).then_inc(S["zinv_ready"], 1)
                            dve.wait_ge(S["zinv_ready"], 1)
                            V.tensor_tensor(zT, zT, b2(zvar, 4), ALU.mult).then_inc(S["z_normed"], 1)
                            dve.wait_ge(S["z_normed"], 1)
                            for j in range(4):
                                V.tensor_scalar(zT[:, j, :], zT[:, j, :], vecA[:, V_CLW + j:V_CLW + j + 1],
                                                vecA[:, V_CLB + j:V_CLB + j + 1], ALU.mult, ALU.add)\
                                    .then_inc(S["z_affine"], 1)
                        dve.wait_ge(S["w_done"], c + 1)
                        if c < 5:
                            V.tensor_copy(b["Wc"], shaped(bk(q, 0)[:, 0:NPAIR * C], NPAIR, C))\
                                .then_inc(S["wc_ready"], 1)
                            dve.wait_ge(S["z_done"], c + 1)
                            V.tensor_tensor(b["tmp"], Zc, shaped(bk(q, 2)[:, 0:NPAIR * C], NPAIR, C), ALU.add)\
                                .then_inc(S["state_sum"], 1)
                            end = min(C, NPR - ts) - 1
                            g_end = b["eL"][:, :, end:end + 1].broadcast_to([P, NPAIR, C])
                            dve.wait_ge(S["state_sum"], c + 1)
                            V.tensor_tensor(Zc, b["tmp"], g_end, ALU.mult).then_inc(S["z_ready"], 1)
                            dve.wait_ge(S["zbd_used"], c + 1)
                            for i in range(2):
                                last = V.tensor_tensor(diag(ZBD, i), half(b["tmp"], i), half(g_end, i), ALU.mult)
                            last.then_inc(S["zbd_ready"], 1)
                        else:
                            dve.wait_ge(S["szt_ready"], 1)
                            V.tensor_tensor(b["Wc"], shaped(bk(q, 1)[:, 0:NPAIR * C], NPAIR, C), b["tmp"],
                                            ALU.add).then_inc(S["wc_ready"], 1)
                            dve.wait_ge(S["un_ready"], 6)
                            for j in range(NPAIR):
                                V.tensor_tensor(shaped(Ux[:, j, :], NSEQ, HD), b2(b["Un"][:, j, :], NSEQ),
                                                b3(seqrow, HD), ALU.mult).then_inc(S["ux_ready"], 1)
                            dve.wait_ge(S["z_sig"], 1)
                            V.tensor_tensor(zT, zT, zsq, ALU.mult).then_inc(S["zT_ready"], 1)
                            dve.wait_ge(S["y_done"], 6)
                            V.tensor_tensor(yT[:, :, NPR:NT], shaped(bk(q, 1)[:, 0:NPAIR * C], NPAIR, C),
                                            szb[:, :, C:P], ALU.add).then_inc(S["sy_read"], 1)
                            zs = zsBD.rearrange("p (s j) v -> p s j v", j=NPAIR)
                            for j, bi in enumerate((0, 3, 2, 1)):
                                dve.wait_ge(S["zs_done"], j + 1)
                                zn = shaped(zso[:, j, :], NSEQ, HD)
                                for i in range(2):
                                    last = V.tensor_tensor(
                                        half(zn, i), half(shaped(bk(q, bi), NSEQ, HD), i),
                                        zs[64 * i:64 * i + 64, :, j, 64 * i:64 * i + 64], ALU.add)
                                last.then_inc(S["state_sum"], 1)
                                dve.wait_ge(S["state_sum"], 6 + j)
                                V.tensor_tensor(zn, zn, b3(b["eL"][:, j, SL - 1:C:SL], HD), ALU.mult)\
                                    .then_inc(S["zso_ready"], 1)

        for g in range(3):
            scan_block(g)

        next_stage()
        cursor[0] = mixer_end
        acc = take(3, DM)
        hp = take(3, DM)
        gfin = take(DM)
        brows_at = cursor[0]
        xg = take(512)
        xT = take(4, 2, C)
        t1 = take(512)
        u1 = take(512)
        sg = take(512)
        sw = take(512)
        aT = take(4, 2, C)
        ys = take(512)
        brows = arena[:, brows_at:brows_at + 3 * DM].rearrange("p (w d) -> p w d", w=3)
        bmid = take(3, DM, dt=BF16)
        Pm = take(3, C)
        Pg = take(3, 2, C)
        PgT = take(3, P)
        rk = take(3)
        esel = take(C, dt=BF16)
        gjunk = arena[:, cursor[0]:cursor[0] + DM]
        cursor[0] += DM
        assert cursor[0] <= arena_words
        flat = arena[:, mixer_start:mixer_start + 8 * 4 * NT]
        sout = shaped(zsBD.rearrange("p a b -> p (a b)"), NSEQ * NPAIR, P)
        zpT = shaped(flat[:, 7488:8000], NPAIR, P)
        ysq = shaped(flat[:, 4096:4096 + 4 * NT], 4, NT)
        h2T = shaped(flat[:, 0:KC * NT], KC, NT)
        at = [KC * NT]

        def bit(*shape, dt=F32):
            n = 1
            for d in shape:
                n *= d
            words = (n + 1) // 2 if dt == BF16 else n
            v = flat[:, at[0]:at[0] + words]
            at[0] += words
            assert at[0] <= 4096
            if dt != F32:
                v = v.bitcast(dt)
            return shaped(v, *shape)

        wr = bit(KC, NE)
        brow = bit(NE)
        gffn2 = bit(KC)
        lgT = ys[:, 0:3 * P]
        logits = bit(3, NE)
        top = bit(3, 8)
        topi = bit(3, 8, dt=U32)
        topf = bit(3, 8)
        eg = bit(3, TOPK)
        esum = bit(3)
        erec = bit(3)
        hot = shaped(flat[:, 4096:4096 + 3 * TOPK * NE], 3 * TOPK, NE)
        mask = bit(3, NE)
        maskbf = bit(3, NE, dt=BF16)
        cnt, extra, incA, incB, exc = [bit(NE) for _ in range(5)]
        over_at = mixer_start + 6 * 4 * NT
        sel3 = shaped(arena[:, over_at:over_at + 3 * NOVER * NE], 3 * NOVER, NE)
        step_n = [0]

        F = {n: lsem("f_" + n) for n in [
            "acc_in", "brows_in", "wr_in", "gffn_in", "gfin_in",
            "ymean_done", "y_centered", "y_squared", "yvar_done", "yvar_ready", "yroot_ready", "yT_ready", "dstep",
            "st_turned", "st_copied", "wout_tile", "acc_ready", "ssq_ready", "ms_ready", "rms_ready", "hp_ready",
            "h2_turned", "h2T_ready", "wrg_ready", "lt_done", "lt_ready", "logits_done", "top_ready", "eg_ready",
            "mask_ready", "rank_done", "tab_ready", "bias_ready",
            "p_ready", "pg_ready", "esel_ready", "xg_done", "xg_ready", "x_turned", "x_ready", "g_done", "u_done",
            "t1_ready", "sg_ready", "act_ready", "a_turned", "aT_ready", "y_done", "ys_ready", "pgt_done",
            "pgt_ready", "cmb_done", "cmb_read", "mstep", "pstep", "fin_ms", "fin_root", "fin_ready", "lgt_zeroed"]}

        def gate_src(w, e, u):
            return w[0][bass.ds(e, 1)].rearrange("o (p c) n -> p (o c) n", c=KC)[:, 2 * u:2 * u + 2, :]

        def down_src(w, e, u):
            return w[0][bass.ds(e, 1)].rearrange("o (c p) n -> p (o c) n", p=P)[:, 2 * u:2 * u + 2, :]

        UNITS = [(w, h, u) for h in range(2) for w in ("w_gate", "w_up", "w_down") for u in range(4)]

        def load_expert_unit(sp, it, n, experts):
            w, h, u = UNITS[n]
            src = (down_src if w == "w_down" else gate_src)(a[w], experts[h], u)
            sp.wait_ge(unit_used, it * UPAIR + (UPRE + n - RING + 1))
            sp.dma_start(slot(UPRE + n, DM), src).then_inc(unit_landed[(UPRE + n) % RING], 16)

        def wait_expert_unit(pe, it, n):
            t = UPRE + n
            pe.wait_ge(unit_landed[t % RING], it * (16 * UPAIR // RING) + 16 * (t // RING + 1))

        CMB_BANKS = [6, 7, 0, 1, 6, 7]
        H2_BANKS = [6, 0, 2]

        def over_pairs(eng, body):
            n_over = eng.value_load(blocktab[0:1, NBLK:NBLK + 1], min_val=0, max_val=NOVER)
            with eng.If(n_over > 0):
                with eng.Fori(PAIRS, PAIRS + OPAIRS) as it:
                    with eng.If(n_over > (it - PAIRS) * 2):
                        body(it)

        with nc.Block() as block:
            @block.sync
            def _(sp):
                sp.dma_start(acc[0:META, 0, :], a["meta_tokens"]).then_inc(F["acc_in"], 16)
                sp.dma_start(acc[META:P, 0, :], a["x_prompt"][0, 0:P - META, :]).then_inc(F["acc_in"], 16)
                sp.dma_start(acc[:, 1, :], a["x_prompt"][0, P - META:2 * P - META, :]).then_inc(F["acc_in"], 16)
                sp.dma_start(acc[0:META, 2, :], a["x_prompt"][0, 2 * P - META:SEQ, :]).then_inc(F["acc_in"], 16)
                sp.dma_start(acc[META:META + NSA, 2, :],
                             a["x_sample"].rearrange("s t d -> (s t) d")).then_inc(F["acc_in"], 16)
                sp.dma_start(wr, a["w_router"][0].rearrange("(c p) e -> p c e", c=KC)).then_inc(F["wr_in"], 16)
                sp.dma_start(brow, a["b_router"].broadcast_to([P, NE])).then_inc(F["wr_in"], 16)
                sp.dma_start(gffn2, a["norm_ffn"][0].rearrange("(c p) -> p c", c=KC),
                             allow_slow_non_contiguous=True).then_inc(F["wr_in"], 16)
                sp.dma_start(gffn, a["norm_ffn"][0].rearrange("(p c) -> p c", c=KC)).then_inc(F["gffn_in"], 16)
                for i, nm in enumerate(("b_gate", "b_up", "b_down")):
                    sp.dma_start(brows[0:NE, i, :], a[nm][0]).then_inc(F["brows_in"], 16)
                sp.dma_start(gfin, a["norm_final"].rearrange("(o d) -> o d", o=1).broadcast_to([P, DM]))\
                    .then_inc(F["gfin_in"], 16)
                for n in range(UPAIR):
                    load_expert_unit(sp, 0, n, (0, 1))
                with sp.Fori(1, PAIRS) as it:
                    for n in range(UPAIR):
                        load_expert_unit(sp, it, n, (it * 2, it * 2 + 1))

                def body(it):
                    es = [sp.value_load(blocktab[0:1, bass.ds(it * 2 + h, 1)], min_val=0, max_val=NE - 1)
                          for h in range(2)]
                    for n in range(UPAIR):
                        load_expert_unit(sp, it, n, es)
                sp.wait_ge(F["tab_ready"], 1)
                over_pairs(sp, body)
                for i in range(3):
                    sp.wait_ge(F["fin_ready"], i + 1)
                    if i == 0:
                        sp.dma_start(a["y_prompt"][0, 0:P - META, :], acc[META:P, 0, :]).then_inc(out_stored, 16)
                    elif i == 1:
                        sp.dma_start(a["y_prompt"][0, P - META:2 * P - META, :], acc[:, 1, :])\
                            .then_inc(out_stored, 16)
                    else:
                        sp.dma_start(a["y_prompt"][0, 2 * P - META:SEQ, :], acc[0:META, 2, :])\
                            .then_inc(out_stored, 16)
                        sp.dma_start(a["y_sample"].rearrange("s t d -> (s t) d"), acc[META:META + NSA, 2, :])\
                            .then_inc(out_stored, 16)
                sp.wait_ge(out_stored, 16 * (stores[0] + 9 + 4))

            @block.gpsimd
            def _(pool):
                T = nc.gpsimd
                T.memset(lgT[0:NE, :], 0.0).then_inc(F["lgt_zeroed"], 1)
                pool.wait_ge(F["brows_in"], 48)
                pstep = chain(pool, F["pstep"])
                pstep(T.tensor_copy(bias3[0:NE], brows[0:NE]))
                pstep(T.tensor_tensor(brows[0:NE], brows[0:NE], bias3[0:NE], ALU.subtract))
                pstep(T.tensor_copy(bmid[0:NE], brows[0:NE]))
                pstep(T.tensor_tensor(brows[0:NE], brows[0:NE], bmid[0:NE], ALU.subtract))
                pstep(T.tensor_copy(bias3[NE:2 * NE], bmid[0:NE]))
                pstep(T.tensor_copy(bias3[2 * NE:3 * NE], brows[0:NE]))
                nc.gpsimd.sem_inc(F["bias_ready"], 1)

            @block.scalar
            def _(act):
                A = nc.scalar
                for j in range(4):
                    act.wait_ge(F["yvar_ready"], j + 1)
                    A.activation(ysq[:, j, :], ysq[:, j, :], ACT.Sqrt).then_inc(F["yroot_ready"], 1)
                for i, (t0, n) in enumerate(TILES):
                    act.wait_ge(F["acc_ready"], 2 * i + 2)
                    A.activation(hp[0:n, i, :], acc[0:n, i, :], ACT.Square, accum_out=small[0:n, 24 + i:25 + i])\
                        .then_inc(F["ssq_ready"], 1)
                    act.wait_ge(F["h2_turned"], 2 * i + 2)
                    A.copy(h2T[:, 4:8, t0:t0 + n], shaped(bank[:, H2_BANKS[i] + 1, :], 4, P)[:, :, 0:n])\
                        .then_inc(F["h2T_ready"], 1)
                act.wait_ge(F["ms_ready"], 1)
                A.activation(small[:, 20:23], small[:, 16:19], ACT.Sqrt).then_inc(F["rms_ready"], 1)
                act.wait_ge(F["lgt_zeroed"], 1)
                act.wait_ge(F["lt_done"], 2)
                A.copy(lgT[0:NE, 0:NT], bank[0:NE, 6, 0:NT]).then_inc(F["lt_ready"], 1)
                act.wait_ge(F["top_ready"], 1)
                A.activation(eg, eg, ACT.Exp).then_inc(F["eg_ready"], 1)
                for n in range(9):
                    if n == 6:
                        act.wait_ge(F["xg_done"], 1)
                        A.copy(xg, bank[:, 3, :]).then_inc(F["xg_ready"], 1)
                    act.wait_ge(F["st_turned"], n + 1)
                    dst = sout[0:C, 4 * n:4 * n + 4, :] if n < 8 else zpT[0:C, :, :]
                    A.copy(dst, shaped(bank[0:C, n % 2, :], 4, P)).then_inc(F["st_copied"], 1)
                act.wait_ge(F["st_copied"], 9)
                for j in range(NPAIR):
                    for h in range(2):
                        act.dma_start(a["wkv_sample"][0][:, 2 * j + h].rearrange("s v k -> v s k"),
                                      sout[0:C, NSEQ * j:NSEQ * j + NSEQ, C * h:C * h + C]).then_inc(out_stored, 16)
                act.dma_start(a["wkv_prompt"][0, 0].rearrange("h v k -> v h k"),
                              zpT[0:C, :, :].rearrange("v j (h k) -> v (j h) k", h=2)).then_inc(out_stored, 16)
                def block_of(n):
                    act.wait_ge(F["t1_ready"], n + 1)
                    A.activation(sg, t1, ACT.Sigmoid, scale=ALPHA).then_inc(F["sg_ready"], 1)
                    act.wait_ge(F["xg_done"], n + 2)
                    A.copy(xg, bank[:, 3, :]).then_inc(F["xg_ready"], 1)
                    act.wait_ge(F["a_turned"], n + 1)
                    A.copy(aT.rearrange("p m h s -> p (m h s)"), bank[:, 4, :]).then_inc(F["aT_ready"], 1)
                    act.wait_ge(F["y_done"], n + 1)
                    A.copy(ys, bank[:, 2, :]).then_inc(F["ys_ready"], 1)
                    act.wait_ge(F["pgt_done"], n + 1)
                    A.copy(PgT.rearrange("p i t -> p (i t)")[:, 0:NT], bank[:, 4, 0:NT]).then_inc(F["pgt_ready"], 1)

                def body(it):
                    for h in range(2):
                        block_of(it * 2 + h)

                with act.Fori(0, PAIRS) as it:
                    body(it)
                act.wait_ge(F["tab_ready"], 1)
                over_pairs(act, body)
                for i, (t0, n) in enumerate(TILES):
                    act.wait_ge(F["fin_ms"], i + 1)
                    A.activation(small[0:n, 36 + i:37 + i], small[0:n, 32 + i:33 + i], ACT.Sqrt)\
                        .then_inc(F["fin_root"], 1)

            @block.tensor
            def _(pe):
                M = nc.tensor

                def stats(src, done, read):
                    for j in range(4):
                        if j >= 2:
                            pe.wait_ge(read, j - 1)
                        M.matmul(bank[:, 6 + j % 2, 0:NT], headones, src[:, j, :], start=True, stop=True)\
                            .then_inc(done, 1)

                stats(yT, F["ymean_done"], F["y_centered"])
                for u in range(UNITS_OUT):
                    t = UNITS_IN + u
                    wait_unit(pe, t)
                    w = slot(t, DM)
                    if u == 2:
                        pe.wait_ge(F["yT_ready"], 1)

                    def add_chunk(i, c):
                        t0, n = TILES[i]
                        cc = 2 * OUT_ORDER[u] + c
                        src = zT[:, cc - 4, :] if cc >= 4 else yT[:, cc, :]
                        for hb in range(2):
                            mm = M.matmul(bank[0:n, 2 * i + hb, :], src[:, t0:t0 + n],
                                          w[:, c, 512 * hb:512 * hb + 512],
                                          start=(u == 0 and c == 0), stop=(u == 3 and c == 1))
                        return mm

                    if u < UNITS_OUT - 1:
                        for c in range(2):
                            for i in range(3):
                                mm = add_chunk(i, c)
                            if u == 0 and c == 0:
                                pe.wait_ge(F["y_squared"], 1)
                                stats(ysq, F["yvar_done"], F["yvar_ready"])
                        mm.then_inc(unit_used, 1)
                    else:
                        for i in range(3):
                            add_chunk(i, 0)
                            add_chunk(i, 1).then_inc(F["wout_tile"] if i < 2 else unit_used, 1)
                pe.wait_ge(F["yvar_ready"], 4)
                for i, (t0, n) in enumerate(TILES):
                    pe.wait_ge(F["acc_ready"], 2 * i + 2)
                    for hb in range(2):
                        for c in range(4):
                            mm = M.transpose(bank[:, H2_BANKS[i] + hb, c * P:c * P + n],
                                             acc[0:n, i, (4 * hb + c) * P:(4 * hb + c + 1) * P], ident[0:n, 0:n])
                        mm.then_inc(F["h2_turned"], 1)
                    if i >= 1:
                        lo = 0 if i == 1 else TILES[2][0]
                        pe.wait_ge(F["wrg_ready"], 1)
                        pe.wait_ge(F["h2T_ready"], 2 * i + 2)
                        for c in range(KC):
                            mm = M.matmul(bank[0:NE, 6, lo:t0 + n], wr[:, c, :], h2T[:, c, lo:t0 + n],
                                          start=(c == 0), stop=(c == KC - 1))
                        mm.then_inc(F["lt_done"], 1)
                pe.wait_ge(F["lt_ready"], 1)
                for i in range(3):
                    mm = M.transpose(bank[:, 7, NE * i:NE * i + NE], lgT[0:NE, i * P:i * P + P], ident[0:NE, 0:NE])
                mm.then_inc(F["logits_done"], 1)

                def turn_states(groups):
                    for n in groups:
                        if n >= 2:
                            pe.wait_ge(F["st_copied"], n - 1)
                        for q in range(4):
                            src = zso[:, n // 2, C * (4 * (n % 2) + q):C * (4 * (n % 2) + q) + C] if n < 8 \
                                else Zc[:, q, :]
                            mm = M.transpose(bank[0:C, n % 2, q * P:q * P + P], src, ident)
                        mm.then_inc(F["st_turned"], 1)

                turn_states(range(4))
                pe.wait_ge(F["mask_ready"], 1)
                for i, (t0, n) in enumerate(TILES):
                    o = bank[:, 3, NE * i:NE * i + NE]
                    for k in range(i):
                        M.matmul(o, onesbf, maskbf[:, k, :], start=(k == 0), stop=False)
                    M.matmul(o, tribf[0:n, :], maskbf[0:n, i, :], start=(i == 0), stop=True)
                for i, (t0, n) in enumerate(TILES):
                    mm = M.matmul(bank[:, 3, NE * 3:NE * 4], onesbf[0:n, :], maskbf[0:n, i, :],
                                  start=(i == 0), stop=(i == 2))
                mm.then_inc(F["rank_done"], 1)
                turn_states(range(4, 6))

                pe.wait_ge(F["hp_ready"], 3)

                def gather(n):
                    pe.wait_ge(F["p_ready"], n + 1)
                    for i, (t0, m) in enumerate(TILES):
                        for hb in range(2):
                            mm = M.matmul(bank[64 * hb:64 * hb + 64, 3, :], Pm[0:m, i, :],
                                          hp[0:m, i, 512 * hb:512 * hb + 512], start=(i == 0), stop=(i == 2))
                    mm.then_inc(F["xg_done"], 1)

                def turn_x(n):
                    pe.wait_ge(F["xg_ready"], n + 1)
                    for m in range(4):
                        mm = M.transpose(bank[:, 5, m * P:m * P + P], xg[:, m * P:m * P + P], ident)
                    mm.then_inc(F["x_turned"], 1)

                def product(it, first, b, tokens, w3):
                    for u in range(4):
                        wait_expert_unit(pe, it, first + u)
                        w = slot(UPRE + first + u, DM)
                        for c in range(2):
                            cc = 2 * u + c
                            for hb in range(2):
                                mm = M.matmul(bank[64 * hb:64 * hb + 64, b, :], tokens[:, cc % 4, cc // 4, :],
                                              w[:, c, 512 * hb:512 * hb + 512], start=(cc == 0), stop=False)
                        mm.then_inc(unit_used, 1)
                    for hb in range(2):
                        mm = M.matmul(bank[64 * hb:64 * hb + 64, b, :], esel[0:3 * NE, :],
                                      bias3[0:3 * NE, w3, 512 * hb:512 * hb + 512], start=False, stop=True)
                    return mm

                def block_of(it, h):
                    n = it * 2 + h
                    pe.wait_ge(F["x_ready"], n + 1)
                    pe.wait_ge(F["esel_ready"], n + 1)
                    pe.wait_ge(F["cmb_read"], n * 6 + 2)
                    product(it, 12 * h, 0, xT, 0).then_inc(F["g_done"], 1)
                    product(it, 12 * h + 4, 1, xT, 1).then_inc(F["u_done"], 1)
                    gather(n + 1)
                    pe.wait_ge(F["act_ready"], n + 1)
                    for m in range(4):
                        mm = M.transpose(bank[:, 4, m * P:m * P + P], sw[:, m * P:m * P + P], ident)
                    mm.then_inc(F["a_turned"], 1)
                    turn_x(n + 1)
                    pe.wait_ge(F["aT_ready"], n + 1)
                    product(it, 12 * h + 8, 2, aT, 2).then_inc(F["y_done"], 1)
                    pe.wait_ge(F["pg_ready"], n + 1)
                    for i, (t0, m) in enumerate(TILES):
                        mm = M.transpose(bank[:, 4, i * P:i * P + m], Pg[0:m, i, :, :], ident[0:m, 0:m])
                    mm.then_inc(F["pgt_done"], 1)
                    pe.wait_ge(F["ys_ready"], n + 1)
                    pe.wait_ge(F["pgt_ready"], n + 1)
                    for i, (t0, m) in enumerate(TILES):
                        if i == 0:
                            pe.wait_ge(F["cmb_read"], n * 6 + 4)
                        if i == 2:
                            pe.wait_ge(F["cmb_read"], n * 6 + 6)
                        for hb in range(2):
                            M.matmul(bank[0:m, CMB_BANKS[2 * i + hb], :], PgT[64 * hb:64 * hb + 64, i, 0:m],
                                     ys[64 * hb:64 * hb + 64, :], start=True, stop=True).then_inc(F["cmb_done"], 1)

                def body(it):
                    for h in range(2):
                        block_of(it, h)

                gather(0)
                turn_states(range(6, 9))
                turn_x(0)
                pe.wait_ge(F["st_copied"], 9)
                with pe.Fori(0, PAIRS) as it:
                    body(it)
                pe.wait_ge(F["tab_ready"], 1)
                over_pairs(pe, body)

            @block.vector
            def _(dve):
                V = nc.vector
                link = chain(dve, F["dstep"])
                for j in range(4):
                    dve.wait_ge(F["ymean_done"], j + 1)
                    V.scalar_tensor_tensor(yT[:, j, :], bank[:, 6 + j % 2, 0:NT], -1.0 / HD, yT[:, j, :],
                                           ALU.mult, ALU.add).then_inc(F["y_centered"], 1)
                dve.wait_ge(F["y_centered"], 4)
                V.tensor_tensor(ysq, yT, yT, ALU.mult).then_inc(F["y_squared"], 1)
                for j in range(4):
                    dve.wait_ge(F["yvar_done"], j + 1)
                    V.tensor_scalar(ysq[:, j, :], bank[:, 6 + j % 2, 0:NT], 1.0 / HD, GN_EPS, ALU.mult, ALU.add)\
                        .then_inc(F["yvar_ready"], 1)
                for j in range(4):
                    dve.wait_ge(F["yroot_ready"], j + 1)
                    last = V.reciprocal(ysq[:, j, :], ysq[:, j, :])
                link(last)
                link(V.tensor_tensor(yT, yT, ysq, ALU.mult))
                for j in range(4):
                    last = V.tensor_scalar(yT[:, j, :], yT[:, j, :], vecA[:, V_LW + j:V_LW + j + 1],
                                           vecA[:, V_LB + j:V_LB + j + 1], ALU.mult, ALU.add)
                link(last)
                link(V.tensor_tensor(yT, yT, bonT, ALU.add))
                V.tensor_tensor(yT, yT, gT, ALU.mult).then_inc(F["yT_ready"], 1)
                dve.wait_ge(F["wr_in"], 48)
                V.tensor_tensor(wr, wr, b3(gffn2, NE), ALU.mult).then_inc(F["wrg_ready"], 1)
                link(V.memset(small[:, 24:27], 0.0))
                dve.wait_ge(F["acc_in"], 16 * 5)
                for i, (t0, n) in enumerate(TILES):
                    if i < 2:
                        dve.wait_ge(F["wout_tile"], i + 1)
                    else:
                        dve.wait_ge(unit_used, UPRE)
                    for hb in range(2):
                        o = acc[0:n, i, 512 * hb:512 * hb + 512]
                        V.tensor_tensor(o, o, bank[0:n, 2 * i + hb, :], ALU.add).then_inc(F["acc_ready"], 1)
                    dve.wait_ge(F["h2_turned"], 2 * i + 1)
                    V.tensor_copy(h2T[:, 0:4, t0:t0 + n], shaped(bank[:, H2_BANKS[i], :], 4, P)[:, :, 0:n])\
                        .then_inc(F["h2T_ready"], 1)
                dve.wait_ge(F["ssq_ready"], 3)
                V.tensor_scalar(small[:, 16:19], small[:, 24:27], 1.0 / DM, RMS_EPS, ALU.mult, ALU.add)\
                    .then_inc(F["ms_ready"], 1)
                dve.wait_ge(F["rms_ready"], 1)
                link(V.reciprocal(small[:, 28:31], small[:, 20:23]))
                for i, (t0, n) in enumerate(TILES):
                    V.tensor_scalar(hp[0:n, i, :].rearrange("t (c p) -> t c p", c=KC),
                                    acc[0:n, i, :].rearrange("t (p c) -> t c p", c=KC),
                                    small[0:n, 28 + i:29 + i], None, ALU.mult).then_inc(F["hp_ready"], 1)
                dve.wait_ge(F["logits_done"], 1)
                for i in range(3):
                    last = V.scalar_tensor_tensor(logits[:, i, :], bank[:, 7, NE * i:NE * i + NE],
                                                  small[:, 28 + i:29 + i], brow, ALU.mult, ALU.add)
                link(last)
                for i in range(3):
                    last = V.max(out=top[:, i, :], in_=logits[:, i, :])
                link(last)
                V.tensor_tensor(eg, top[:, :, 0:TOPK], top[:, :, 0:1].broadcast_to([P, 3, TOPK]), ALU.subtract)\
                    .then_inc(F["top_ready"], 1)
                for i in range(3):
                    last = V.max_index(out=topi[:, i, :], in_max=top[:, i, :], in_values=logits[:, i, :])
                link(last)
                link(V.tensor_copy(topf, topi))
                for i in range(3):
                    last = V.tensor_tensor(hot[:, TOPK * i:TOPK * i + TOPK, :], b2(exp_iota, TOPK),
                                           b3(topf[:, i, 0:TOPK], NE), ALU.is_equal)
                link(last)

                def over_k(dst, src):
                    v = src.rearrange("p (i k) e -> p i k e", k=TOPK)
                    link(V.tensor_tensor(dst, v[:, :, 0, :], v[:, :, 1, :], ALU.add))
                    for k in range(2, TOPK):
                        link(V.tensor_tensor(dst, dst, v[:, :, k, :], ALU.add))

                over_k(mask, hot)
                V.tensor_copy(maskbf, mask).then_inc(F["mask_ready"], 1)
                dve.wait_ge(F["rank_done"], 1)
                link(V.scalar_tensor_tensor(rankm, bank[:, 3, 0:3 * NE].rearrange("p (i e) -> p i e", e=NE), 1.0,
                                            mask, ALU.add, ALU.mult))
                link(V.tensor_scalar(rankm, rankm, -1.0, None, ALU.add))
                link(V.tensor_copy(cnt, bank[:, 3, NE * 3:NE * 4]))
                V.memset(blockbase[:, 0:NE], 0.0)
                link(V.tensor_copy(blocktab[:, 0:NE], exp_iota))
                def expert_of(n):
                    return dve.value_load(blocktab[0:1, bass.ds(n, 1)], min_val=0, max_val=NE - 1)

                def make_p(n, e, stepped):
                    stepped(V.tensor_scalar(rk, rankm[:, :, bass.ds(e, 1)], blockbase[:, bass.ds(n, 1)], None,
                                            ALU.subtract))
                    for i, (t0, m) in enumerate(TILES):
                        last = V.tensor_scalar(Pm[0:m, i, :], slot_iota[0:m, :], rk[0:m, i:i + 1], None,
                                               ALU.is_equal)
                    last.then_inc(F["p_ready"], 1)

                def make_pg(e):
                    for i, (t0, m) in enumerate(TILES):
                        last = V.tensor_scalar(Pg[0:m, i], b2(slot_iota[0:m, :], 2), rk[0:m, i:i + 1],
                                               gates[0:m, i, bass.ds(e, 1)], ALU.is_equal, ALU.mult)
                    last.then_inc(F["pg_ready"], 1)
                    V.tensor_scalar(esel[0:3 * NE, :], ones[0:3 * NE, 0:C], expert_row[0:3 * NE, bass.ds(e, 1)], None,
                                    ALU.mult).then_inc(F["esel_ready"], 1)

                def take_x(n):
                    dve.wait_ge(F["x_turned"], n + 1)
                    g = gffn.rearrange("p (h m) -> p m h", h=2)
                    V.tensor_tensor(xT, bank[:, 5, :].rearrange("p (m h s) -> p m h s", m=4, h=2),
                                    g.unsqueeze(3).broadcast_to([P, 4, 2, C]), ALU.mult).then_inc(F["x_ready"], 1)

                def stepped0(ins):
                    ins.then_inc(F["mstep"], 1)
                    dve.wait_ge(F["mstep"], 1)

                dve.wait_ge(F["bias_ready"], 1)
                e0 = expert_of(0)
                make_p(0, e0, stepped0)
                dve.wait_ge(F["eg_ready"], 1)
                link(V.tensor_tensor(esum, eg[:, :, 0], eg[:, :, 1], ALU.add))
                for k in range(2, TOPK):
                    link(V.tensor_tensor(esum, esum, eg[:, :, k], ALU.add))
                link(V.reciprocal(erec, esum))
                link(V.tensor_tensor(eg, eg, b3(erec, TOPK), ALU.mult))
                for i in range(3):
                    h = hot[:, TOPK * i:TOPK * i + TOPK, :]
                    last = V.tensor_tensor(h, h, b3(eg[:, i, :], NE), ALU.mult)
                link(last)
                over_k(gates, hot)
                make_pg(e0)
                dve.wait_ge(F["gffn_in"], 16)
                take_x(0)
                link(V.tensor_scalar(extra, cnt, float(C), None, ALU.is_gt))
                for b in range(2, -(-NT // C)):
                    link(V.scalar_tensor_tensor(extra, cnt, float(C * b), extra, ALU.is_gt, ALU.add))
                link(V.tensor_copy(incA, extra))
                src, dst = incA, incB
                for d in (1, 2, 4, 8, 16):
                    V.tensor_copy(dst[:, 0:d], src[:, 0:d])
                    link(V.tensor_tensor(dst[:, d:NE], src[:, d:NE], src[:, 0:NE - d], ALU.add))
                    src, dst = dst, src
                link(V.tensor_tensor(exc, src, extra, ALU.subtract))
                pth = b3(exp_iota[:, 0:NOVER], NE)
                found = sel3[:, 2 * NOVER:3 * NOVER, :]
                link(V.tensor_tensor(found, b2(exc, NOVER), pth, ALU.is_le))
                link(V.tensor_tensor(sel3[:, 0:NOVER, :], b2(src, NOVER), pth, ALU.is_gt))
                link(V.tensor_tensor(found, found, sel3[:, 0:NOVER, :], ALU.mult))
                V.tensor_tensor(sel3[:, 0:NOVER, :], found, b2(exp_iota, NOVER), ALU.mult)
                link(V.tensor_tensor(sel3[:, NOVER:2 * NOVER, :], found, b2(exc, NOVER), ALU.mult))
                for d in (16, 8, 4, 2, 1):
                    link(V.tensor_tensor(sel3[:, :, 0:d], sel3[:, :, 0:d], sel3[:, :, d:2 * d], ALU.add))
                base = blockbase[:, NE:NE + NOVER]
                link(V.tensor_tensor(base, exp_iota[:, 0:NOVER], sel3[:, NOVER:2 * NOVER, 0], ALU.subtract))
                link(V.tensor_scalar(base, base, 1.0, float(C), ALU.add, ALU.mult))
                V.tensor_scalar(found[:, :, 0], found[:, :, 0], -8192.0, 8192.0, ALU.mult, ALU.add)
                V.tensor_copy(blocktab[:, NE:NE + NOVER], sel3[:, 0:NOVER, 0])
                V.memset(blockbase[:, NE + NOVER:NBLK], 8192.0)
                V.memset(blocktab[:, NE + NOVER:NBLK], 0)
                link(V.tensor_copy(blocktab[:, NBLK:NBLK + 1], src[:, NE - 1:NE]))
                V.tensor_tensor(base, base, found[:, :, 0], ALU.add).then_inc(F["tab_ready"], 1)
                dve.wait_ge(F["tab_ready"], 1)

                def block_of(n, e_next, stepped):
                    dve.wait_ge(F["xg_done"], n + 1)
                    dve.wait_ge(F["esel_ready"], n + 1)
                    make_p(n + 1, e_next, stepped)
                    dve.wait_ge(F["g_done"], n + 1)
                    V.tensor_scalar(t1, bank[:, 0, :], LIMIT, None, ALU.min).then_inc(F["t1_ready"], 1)
                    dve.wait_ge(F["u_done"], n + 1)
                    stepped(V.tensor_scalar(u1, bank[:, 1, :], LIMIT, -LIMIT, ALU.min, ALU.max))
                    stepped(V.scalar_tensor_tensor(u1, u1, 1.0, t1, ALU.add, ALU.mult))
                    dve.wait_ge(F["sg_ready"], n + 1)
                    V.tensor_tensor(sw, u1, sg, ALU.mult).then_inc(F["act_ready"], 1)
                    take_x(n + 1)
                    dve.wait_ge(F["pgt_done"], n + 1)
                    make_pg(e_next)
                    for i, (t0, m) in enumerate(TILES):
                        for hb in range(2):
                            k = 2 * i + hb
                            dve.wait_ge(F["cmb_done"], n * 6 + (k + 1))
                            o = acc[0:m, i, 512 * hb:512 * hb + 512]
                            V.tensor_tensor(o, o, bank[0:m, CMB_BANKS[k], :], ALU.add).then_inc(F["cmb_read"], 1)

                STEPS = 6

                def body(it):
                    n = [0]

                    def stepped(ins):
                        n[0] += 1
                        ins.then_inc(F["mstep"], 1)
                        dve.wait_ge(F["mstep"], it * STEPS + (1 + n[0]))

                    es = [expert_of(it * 2 + 1), expert_of(it * 2 + 2)]
                    for h in range(2):
                        block_of(it * 2 + h, es[h], stepped)
                    assert n[0] == STEPS

                dve.sem_inc(F["cmb_read"], 4)
                with dve.Fori(0, PAIRS) as it:
                    body(it)
                over_pairs(dve, body)
                dve.wait_ge(F["gfin_in"], 16)
                for i, (t0, n) in enumerate(TILES):
                    link(V.tensor_tensor_reduce(out=hp[0:n, i, :], in0=acc[0:n, i, :], in1=acc[0:n, i, :], scale=1.0,
                                                scalar=0.0, op0=ALU.mult, op1=ALU.add,
                                                accum_out=small[0:n, 40 + i:41 + i]))
                    V.tensor_scalar(small[0:n, 32 + i:33 + i], small[0:n, 40 + i:41 + i], 1.0 / DM, RMS_EPS,
                                    ALU.mult, ALU.add).then_inc(F["fin_ms"], 1)
                for i, (t0, n) in enumerate(TILES):
                    dve.wait_ge(F["fin_root"], i + 1)
                    link(V.reciprocal(small[0:n, 44 + i:45 + i], small[0:n, 36 + i:37 + i]))
                    V.scalar_tensor_tensor(acc[0:n, i, :], acc[0:n, i, :], small[0:n, 44 + i:45 + i], gfin[0:n, :],
                                           ALU.mult, ALU.mult).then_inc(F["fin_ready"], 1)


_INS = ['x_prompt', 'x_sample', 'state_wkv', 'state_shift', 'state_conv', 'meta_tokens', 'norm_mix', 'w_in',
        'tshift_mu', 'decay_w0', 'decay_w2', 'iclr_a0', 'iclr_a2', 'gate_g2', 'k_k', 'k_a', 'r_k', 'lnx_w', 'lnx_b',
        'glu_b', 'dw_weight', 'dw_bias', 'conv_ln_w', 'conv_ln_b', 'w_out', 'norm_ffn', 'w_router', 'b_router',
        'w_gate', 'b_gate', 'w_up', 'b_up', 'w_down', 'b_down', 'norm_final']
_OUTS = [("y_prompt", (1, SEQ, DM)), ("y_sample", (NSEQ, SL, DM)), ("wkv_prompt", (1, 1, NH, HD, HD)),
         ("shift_prompt", (1, 1, SHC)), ("conv_prompt", (1, 1, HIST, CB)), ("wkv_sample", (1, NSEQ, NH, HD, HD)),
         ("shift_sample", (1, NSEQ, SHC)), ("conv_sample", (1, NSEQ, HIST, CB))]


def kernel(**inputs):
    import numpy as _np
    import concourse.bacc as _bacc
    from concourse.bass_utils import run_bass_kernel_spmd as _run

    nc = _bacc.Bacc("TRN2", target_bir_lowering=False, num_devices=1)
    arrays, aps = {}, {}
    for name in _INS:
        v = _np.ascontiguousarray(inputs[name])
        arrays[f"in_{name}_dram"] = v
        aps[name] = nc.dram_tensor(f"in_{name}_dram", v.shape, mybir.dt.from_np(v.dtype), kind="ExternalInput").ap()
    for name, shape in _OUTS:
        aps[name] = nc.dram_tensor(f"out_{name}_dram", shape, F32, kind="ExternalOutput").ap()
    build(nc, aps)
    r = _run(nc, [arrays], core_ids=[0])
    return tuple(r.results[0][f"out_{name}_dram"] for name, _ in _OUTS)
```
